# Optimizing a Trainium2 kernel written in Bass

```python
import math
import jax, jax.numpy as jnp
from jax import lax
import numpy as np

D_MODEL = 1024
BATCH = 1
SEQ = 512
DEPTH = 2

N_MEM = 256
D_HYENA = 256
RW_HEADS = 6
RW_HEAD_DIM = 64
D_RWKV = RW_HEADS * RW_HEAD_DIM
GDN_HEADS = 6
GDN_HEAD_DIM = 64
D_GDN = GDN_HEADS * GDN_HEAD_DIM
D_MIX = D_HYENA + D_RWKV + D_GDN
HY_SHORT = 3
HY_BANDS = 16
HY_EMB = 1 + 2 * HY_BANDS
HY_FFN = 64
HY_FAST_DECAY = 0.3
HY_SLOW_DECAY = 1.5
HY_TARGET = 1e-2
RW_LORA_W = 64
RW_LORA_A = 64
RW_LORA_G = 128
RW_DECAY_SCALE = 0.606531
RW_GN_EPS = 64e-5
GDN_SHORT = 3
GDN_CHUNK = 64
XA_HEADS = 4
XA_HEAD_DIM = D_MODEL // XA_HEADS
D_FF = 2816
NORM_EPS = 1e-6
HY_COLS = 3 * D_HYENA
RW_COLS = 3 * D_RWKV + 2 * RW_LORA_W + 2 * RW_LORA_A + RW_LORA_G
GDN_COLS = 4 * D_GDN + 4 * GDN_HEADS
IN_COLS = HY_COLS + RW_COLS + GDN_COLS

kernel_name = "hybrid_hyena_rwkv7_gdn_encoder"

def _split(t, sizes):
    return jnp.split(t, np.cumsum(sizes)[:-1].tolist(), axis=-1)

def rmsnorm(x, g, eps=NORM_EPS):
    xf = x.astype(jnp.float32)
    y = xf * lax.rsqrt(jnp.mean(xf * xf, axis=-1, keepdims=True) + eps)
    return (y * g.astype(jnp.float32)).astype(x.dtype)

def l2norm_heads(t, heads, eps=1e-6):
    B_, L, D = t.shape
    th = t.reshape(B_, L, heads, D // heads)
    th = th * lax.rsqrt(jnp.sum(th * th, axis=-1, keepdims=True) + eps)
    return th.reshape(B_, L, D)

def swiglu(x, w1, w3, w2):
    return (jax.nn.silu(x @ w1) * (x @ w3)) @ w2

def depthwise_conv(u, w):
    K = w.shape[0]
    return lax.conv_general_dilated(u, w[:, None, :].astype(u.dtype), window_strides=(1,),
                                    padding=[(K // 2, K // 2)],
                                    dimension_numbers=("NWC", "WIO", "NWC"),
                                    feature_group_count=u.shape[-1])

def token_shift(u, mu_prev, mu_next):
    prev = jnp.pad(u, ((0, 0), (1, 0), (0, 0)))[:, :-1]
    nxt = jnp.pad(u, ((0, 0), (0, 1), (0, 0)))[:, 1:]
    return u + mu_prev * (prev - u) + mu_next * (nxt - u)

def hyena_positional_features(L):
    t = jnp.linspace(0.0, 1.0, L, dtype=jnp.float32)[:, None]
    ang = 2.0 * math.pi * jnp.arange(L, dtype=jnp.float32)[:, None] / L
    bands = jnp.linspace(1e-4, HY_BANDS - 1, HY_BANDS, dtype=jnp.float32)[None, :]
    z = jnp.concatenate([t, jnp.cos(bands * ang), -jnp.sin(bands * ang)], axis=-1)
    return z, t

def hyena_filter(z, t, freq, w1, b1, w2, b2, w3, decay):
    f32 = jnp.float32
    freq = freq.astype(f32)
    h = jnp.sin(freq * (z @ w1.astype(f32) + b1.astype(f32)))
    h = jnp.sin(freq * (h @ w2.astype(f32) + b2.astype(f32)))
    h = (h @ w3.astype(f32)) * jnp.exp(-t * decay.astype(f32))
    h_fwd, h_bwd = h[:, :D_HYENA], h[:, D_HYENA:]
    kern = jnp.concatenate([h_fwd, jnp.zeros_like(h_fwd[:1]), h_bwd[:0:-1]], axis=0)
    return kern / jnp.sum(jnp.abs(kern), axis=0, keepdims=True)

def two_sided_long_conv(u, kern):
    L = u.shape[1]
    uf = jnp.fft.rfft(u.astype(jnp.float32), n=2 * L, axis=1)
    kf = jnp.fft.rfft(kern, n=2 * L, axis=0)
    return jnp.fft.irfft(uf * kf[None], n=2 * L, axis=1)[:, :L]

def hyena_mixer(p, kern, conv_w, conv_b, bias):
    p = depthwise_conv(p, conv_w) + conv_b
    x0, x1, v = _split(p, (D_HYENA, D_HYENA, D_HYENA))
    u = x1 * v
    y = two_sided_long_conv(u, kern).astype(u.dtype) + bias * u
    return x0 * y

def rwkv7_scan(r, w, k, v, a, b, reverse):
    B_, L, D = r.shape

    def to_heads(t):
        return t.reshape(B_, L, RW_HEADS, RW_HEAD_DIM).transpose(1, 0, 2, 3)

    def step(S, inp):
        r_t, w_t, k_t, v_t, a_t, b_t = inp
        sa = jnp.einsum("bhij,bhj->bhi", S, a_t)
        S = S * w_t[:, :, None, :] + sa[..., None] * b_t[:, :, None, :] + v_t[..., None] * k_t[:, :, None, :]
        return S, jnp.einsum("bhij,bhj->bhi", S, r_t)

    S0 = jnp.zeros((B_, RW_HEADS, RW_HEAD_DIM, RW_HEAD_DIM), jnp.float32)
    _, ys = lax.scan(step, S0, tuple(to_heads(t) for t in (r, w, k, v, a, b)), reverse=reverse)
    return ys.transpose(1, 0, 2, 3).reshape(B_, L, D)

def head_groupnorm(y, w, b, heads, eps):
    B_, L, D = y.shape
    yh = y.reshape(B_, L, heads, D // heads)
    mu = jnp.mean(yh, axis=-1, keepdims=True)
    var = jnp.mean(jnp.square(yh - mu), axis=-1, keepdims=True)
    return ((yh - mu) * lax.rsqrt(var + eps)).reshape(B_, L, D) * w + b

def rwkv7_mixer(p, mu_prev, mu_next, w_lora, w0, a_lora, a0, g_lora, k_k, k_a, r_k, gn_w, gn_b):
    f32 = jnp.float32
    p = token_shift(p, mu_prev, mu_next).astype(f32)
    r, k, v, lw_f, lw_b, la_f, la_b, lg = _split(
        p, (D_RWKV, D_RWKV, D_RWKV, RW_LORA_W, RW_LORA_W, RW_LORA_A, RW_LORA_A, RW_LORA_G))
    gate = jax.nn.sigmoid(lg) @ g_lora.astype(f32)
    kk = l2norm_heads(k * k_k, RW_HEADS)
    y = 0.0
    for d, (lw, la, rev) in enumerate(((lw_f, la_f, False), (lw_b, la_b, True))):
        log_w = -RW_DECAY_SCALE * jax.nn.sigmoid(w0[d] + jnp.tanh(lw) @ w_lora[d].astype(f32))
        a = jax.nn.sigmoid(a0[d] + la @ a_lora[d].astype(f32))
        k_d = k * (1.0 + (a - 1.0) * k_a)
        y = y + rwkv7_scan(r, jnp.exp(log_w), k_d, v, -kk, kk * a, rev)
    y = head_groupnorm(y, gn_w, gn_b, RW_HEADS, RW_GN_EPS)
    B_, L, _ = r.shape
    bonus = jnp.sum((r * k * r_k).reshape(B_, L, RW_HEADS, RW_HEAD_DIM), axis=-1, keepdims=True)
    y = y + (bonus * v.reshape(B_, L, RW_HEADS, RW_HEAD_DIM)).reshape(B_, L, D_RWKV)
    return y * gate

def chunk_gated_delta(q, k, v, g, beta):
    B_, L, H, N = q.shape
    C = GDN_CHUNK
    n = L // C

    def chunks(t):
        return t.reshape(B_, n, C, H, -1).transpose(0, 3, 1, 2, 4)

    def chunks_s(t):
        return t.reshape(B_, n, C, H).transpose(0, 3, 1, 2)

    qc, kc, vc = chunks(q), chunks(k), chunks(v)
    gc = jnp.cumsum(chunks_s(g), axis=-1)
    bc = chunks_s(beta)
    idx = jnp.arange(C)
    causal = idx[:, None] >= idx[None, :]
    decay = jnp.exp(jnp.where(causal, gc[..., :, None] - gc[..., None, :], -jnp.inf))
    kb = kc * bc[..., None]
    lower = jnp.einsum("bhncd,bhnsd->bhncs", kb, kc) * decay
    rhs = jnp.concatenate([vc * bc[..., None], kb * jnp.exp(gc)[..., None]], axis=-1)
    sol = lax.linalg.triangular_solve(lower, rhs, left_side=True, lower=True, unit_diagonal=True)
    u_c, w_c = sol[..., :N], sol[..., N:]
    attn = jnp.einsum("bhncd,bhnsd->bhncs", qc, kc) * decay
    q_dec = qc * jnp.exp(gc)[..., None]
    g_last = gc[..., -1]
    k_end = kc * jnp.exp(g_last[..., None] - gc)[..., None]

    def step(S, inp):
        u_i, w_i, attn_i, q_i, k_i, gl = inp
        v_new = u_i - jnp.einsum("bhcd,bhde->bhce", w_i, S)
        o_i = jnp.einsum("bhcd,bhde->bhce", q_i, S) + jnp.einsum("bhcs,bhse->bhce", attn_i, v_new)
        S = S * jnp.exp(gl)[..., None, None] + jnp.einsum("bhcd,bhce->bhde", k_i, v_new)
        return S, o_i

    xs = tuple(jnp.moveaxis(t, 2, 0) for t in (u_c, w_c, attn, q_dec, k_end, g_last))
    S0 = jnp.zeros((B_, H, N, N), jnp.float32)
    _, o = lax.scan(step, S0, xs)
    return o.transpose(1, 0, 3, 2, 4).reshape(B_, L, H, N)

def gdn_mixer(p, conv_w, a_log, dt_bias, norm_w):
    f32 = jnp.float32
    qkv, zg, a_f, a_b, b_f, b_b = _split(
        p, (3 * D_GDN, D_GDN, GDN_HEADS, GDN_HEADS, GDN_HEADS, GDN_HEADS))
    qkv = jax.nn.silu(depthwise_conv(qkv, conv_w)).astype(f32)
    q, k, v = _split(qkv, (D_GDN, D_GDN, D_GDN))
    B_, L, _ = q.shape
    q = l2norm_heads(q, GDN_HEADS) * (GDN_HEAD_DIM ** -0.5)
    k = l2norm_heads(k, GDN_HEADS)
    hd = lambda t: t.reshape(B_, L, GDN_HEADS, GDN_HEAD_DIM)
    q, k, v = hd(q), hd(k), hd(v)
    o = 0.0
    for d, (ag, bg, rev) in enumerate(((a_f, b_f, False), (a_b, b_b, True))):
        g = -jnp.exp(a_log[d].astype(f32)) * jax.nn.softplus(ag.astype(f32) + dt_bias[d])
        beta = jax.nn.sigmoid(bg.astype(f32))
        if rev:
            o_d = chunk_gated_delta(q[:, ::-1], k[:, ::-1], v[:, ::-1], g[:, ::-1], beta[:, ::-1])[:, ::-1]
        else:
            o_d = chunk_gated_delta(q, k, v, g, beta)
        o = o + o_d
    o = o * lax.rsqrt(jnp.mean(o * o, axis=-1, keepdims=True) + NORM_EPS) * norm_w
    o = o * jax.nn.silu(hd(zg.astype(f32)))
    return o.reshape(B_, L, D_GDN)

def memory_cross_attention(h, mem_n, wq, wk, wv, wo):
    B_, L, _ = h.shape
    M = mem_n.shape[1]
    q = (h @ wq).reshape(B_, L, XA_HEADS, XA_HEAD_DIM)
    k = (mem_n @ wk).reshape(B_, M, XA_HEADS, XA_HEAD_DIM)
    v = (mem_n @ wv).reshape(B_, M, XA_HEADS, XA_HEAD_DIM)
    s = jnp.einsum("blhd,bmhd->bhlm", q, k).astype(jnp.float32) * (XA_HEAD_DIM ** -0.5)
    pr = jax.nn.softmax(s, axis=-1).astype(v.dtype)
    o = jnp.einsum("bhlm,bmhd->blhd", pr, v).reshape(B_, L, D_MODEL)
    return o @ wo

def setup_inputs(seed: int = 0) -> dict:
    key = jax.random.key(seed)
    ks = iter(jax.random.split(key, 96))
    f32 = jnp.float32

    def nrm(shape, scale):
        return scale * jax.random.normal(next(ks), shape, f32)

    def gain(shape):
        return 1.0 + 0.05 * jax.random.normal(next(ks), shape, f32)

    def unif(shape, lo, hi):
        return jax.random.uniform(next(ks), shape, f32, minval=lo, maxval=hi)

    hy_rates = jnp.tile(jnp.linspace(-math.log(HY_TARGET) / HY_SLOW_DECAY,
                                     -math.log(HY_TARGET) / HY_FAST_DECAY, D_HYENA, dtype=f32), 2)
    dt = jnp.exp(unif((DEPTH, 2, GDN_HEADS), math.log(1e-3), math.log(1e-1)))
    return {
        "x": nrm((BATCH, SEQ, D_MODEL), 1.0),
        "mem": nrm((BATCH, N_MEM, D_MODEL), 1.0),
        "norm_ffn1": gain((DEPTH, D_MODEL)),
        "ffn1_w1": nrm((DEPTH, D_MODEL, D_FF), D_MODEL ** -0.5),
        "ffn1_w3": nrm((DEPTH, D_MODEL, D_FF), D_MODEL ** -0.5),
        "ffn1_w2": nrm((DEPTH, D_FF, D_MODEL), D_FF ** -0.5),
        "norm_mix": gain((DEPTH, D_MODEL)),
        "w_in": nrm((DEPTH, D_MODEL, IN_COLS), D_MODEL ** -0.5),
        "w_out": nrm((DEPTH, D_MIX, D_MODEL), D_MIX ** -0.5),
        "hy_conv_w": nrm((DEPTH, HY_SHORT, HY_COLS), HY_SHORT ** -0.5),
        "hy_conv_b": nrm((DEPTH, HY_COLS), 0.02),
        "hy_freq": gain((DEPTH, HY_FFN)),
        "hy_w1": nrm((DEPTH, HY_EMB, HY_FFN), HY_EMB ** -0.5),
        "hy_b1": nrm((DEPTH, HY_FFN), 0.1),
        "hy_w2": nrm((DEPTH, HY_FFN, HY_FFN), HY_FFN ** -0.5),
        "hy_b2": nrm((DEPTH, HY_FFN), 0.1),
        "hy_w3": nrm((DEPTH, HY_FFN, 2 * D_HYENA), HY_FFN ** -0.5),
        "hy_decay": hy_rates * gain((DEPTH, 2 * D_HYENA)),
        "hy_bias": nrm((DEPTH, D_HYENA), 1.0),
        "rw_mu_prev": unif((DEPTH, RW_COLS), 0.0, 0.5),
        "rw_mu_next": unif((DEPTH, RW_COLS), 0.0, 0.5),
        "rw_w_lora": nrm((DEPTH, 2, RW_LORA_W, D_RWKV), 0.5 * RW_LORA_W ** -0.5),
        "rw_w0": jnp.linspace(-5.0, -0.5, D_RWKV, dtype=f32) + nrm((DEPTH, 2, D_RWKV), 0.1),
        "rw_a_lora": nrm((DEPTH, 2, RW_LORA_A, D_RWKV), 0.5 * RW_LORA_A ** -0.5),
        "rw_a0": nrm((DEPTH, 2, D_RWKV), 0.1),
        "rw_g_lora": nrm((DEPTH, RW_LORA_G, D_RWKV), RW_LORA_G ** -0.5),
        "rw_k_k": 0.85 + nrm((DEPTH, D_RWKV), 0.05),
        "rw_k_a": gain((DEPTH, D_RWKV)),
        "rw_r_k": nrm((DEPTH, D_RWKV), 0.1),
        "rw_gn_w": gain((DEPTH, D_RWKV)),
        "rw_gn_b": nrm((DEPTH, D_RWKV), 0.02),
        "gdn_conv_w": nrm((DEPTH, GDN_SHORT, 3 * D_GDN), GDN_SHORT ** -0.5),
        "gdn_a_log": jnp.log(unif((DEPTH, 2, GDN_HEADS), 1.0, 16.0)),
        "gdn_dt_bias": dt + jnp.log(-jnp.expm1(-dt)),
        "gdn_norm_w": gain((DEPTH, GDN_HEAD_DIM)),
        "norm_xattn": gain((DEPTH, D_MODEL)),
        "xa_wq": nrm((DEPTH, D_MODEL, D_MODEL), D_MODEL ** -0.5),
        "xa_wk": nrm((DEPTH, D_MODEL, D_MODEL), D_MODEL ** -0.5),
        "xa_wv": nrm((DEPTH, D_MODEL, D_MODEL), D_MODEL ** -0.5),
        "xa_wo": nrm((DEPTH, D_MODEL, D_MODEL), D_MODEL ** -0.5),
        "mem_norm": gain((D_MODEL,)),
        "norm_ffn2": gain((DEPTH, D_MODEL)),
        "ffn2_w1": nrm((DEPTH, D_MODEL, D_FF), D_MODEL ** -0.5),
        "ffn2_w3": nrm((DEPTH, D_MODEL, D_FF), D_MODEL ** -0.5),
        "ffn2_w2": nrm((DEPTH, D_FF, D_MODEL), D_FF ** -0.5),
        "norm_final": gain((D_MODEL,)),
    }

def reference(x, mem, norm_ffn1, ffn1_w1, ffn1_w3, ffn1_w2, norm_mix, w_in, w_out,
              hy_conv_w, hy_conv_b, hy_freq, hy_w1, hy_b1, hy_w2, hy_b2, hy_w3, hy_decay, hy_bias,
              rw_mu_prev, rw_mu_next, rw_w_lora, rw_w0, rw_a_lora, rw_a0, rw_g_lora,
              rw_k_k, rw_k_a, rw_r_k, rw_gn_w, rw_gn_b,
              gdn_conv_w, gdn_a_log, gdn_dt_bias, gdn_norm_w,
              norm_xattn, xa_wq, xa_wk, xa_wv, xa_wo, mem_norm,
              norm_ffn2, ffn2_w1, ffn2_w3, ffn2_w2, norm_final):
    L = x.shape[1]
    z_pos, t_pos = hyena_positional_features(L)
    mem_n = rmsnorm(mem, mem_norm)
    for l in range(DEPTH):
        x = x + 0.5 * swiglu(rmsnorm(x, norm_ffn1[l]), ffn1_w1[l], ffn1_w3[l], ffn1_w2[l])
        h = rmsnorm(x, norm_mix[l])
        p_hy, p_rw, p_gdn = _split(h @ w_in[l], (HY_COLS, RW_COLS, GDN_COLS))
        kern = hyena_filter(z_pos, t_pos, hy_freq[l], hy_w1[l], hy_b1[l], hy_w2[l], hy_b2[l],
                            hy_w3[l], hy_decay[l])
        y_hy = hyena_mixer(p_hy, kern, hy_conv_w[l], hy_conv_b[l], hy_bias[l])
        y_rw = rwkv7_mixer(p_rw, rw_mu_prev[l], rw_mu_next[l], rw_w_lora[l], rw_w0[l], rw_a_lora[l],
                           rw_a0[l], rw_g_lora[l], rw_k_k[l], rw_k_a[l], rw_r_k[l], rw_gn_w[l], rw_gn_b[l])
        y_gdn = gdn_mixer(p_gdn, gdn_conv_w[l], gdn_a_log[l], gdn_dt_bias[l], gdn_norm_w[l])
        y = jnp.concatenate([y_hy.astype(x.dtype), y_rw.astype(x.dtype), y_gdn.astype(x.dtype)], axis=-1)
        x = x + y @ w_out[l]
        x = x + memory_cross_attention(rmsnorm(x, norm_xattn[l]), mem_n, xa_wq[l], xa_wk[l], xa_wv[l], xa_wo[l])
        x = x + 0.5 * swiglu(rmsnorm(x, norm_ffn2[l]), ffn2_w1[l], ffn2_w3[l], ffn2_w2[l])
    return rmsnorm(x, norm_final)


_drawn_inputs = setup_inputs


def setup_inputs(seed=0):
    import zlib

    import numpy as np

    out = dict(_drawn_inputs(seed))
    spreads = {}
    factors = {'hy_conv_b': 3.032,
     'hy_freq': 8.0,
     'hy_b1': 7.119,
     'hy_b2': 5.193,
     'hy_decay': 3.718,
     'rw_w_lora': 2.865,
     'rw_a0': 2.992,
     'rw_k_k': 4.092,
     'rw_gn_w': 2.691,
     'rw_gn_b': 6.316,
     'norm_xattn': 8.0,
     'mem_norm': 5.356,
     'norm_ffn2': 3.05}
    for name, (base, spread) in spreads.items():
        noise = np.random.default_rng([zlib.crc32(name.encode()), seed]).standard_normal(out[name].shape)
        drawn = base * np.exp(spread * noise) if base else spread * noise
        out[name] = __import__('jax').numpy.asarray(drawn.astype(out[name].dtype))
    for name, factor in factors.items():
        out[name] = (out[name] * factor).astype(out[name].dtype)
    return out
```

```python
from contextlib import ExitStack

import numpy as np
import concourse.bass as bass
from concourse import mybir

F32 = mybir.dt.float32
F32R = mybir.dt.float32r
ALU = mybir.AluOpType
ACT = mybir.ActivationFunctionType

P = 128
D_MODEL, SEQ, DEPTH, N_MEM, D_FF = 1024, 512, 2, 256, 2816
KT = D_MODEL // P
TT = SEQ // P
FB = D_FF // P
HY_C = 2
PAIRS = 3
HD = 64
HY_FFN, HY_EMB = 64, 33
HEADS = 6
RW_DECAY_SCALE = 0.606531
NORM_EPS, RW_GN_EPS = 1e-6, 64e-5
XA_HEADS, XA_DIM = 4, 256
LEVELS = 7
ROUND_MAGIC = 1.5 * 2.0 ** 23
TWO_PI_HI = 6.28125
TWO_PI_LO = 6.283185307179586 - TWO_PI_HI
PI_BELOW = 3.1415925

UNIT = 2048
U_FFN_UP = 0
U_FFN_DOWN = FB
N_FFN = FB + FB // 2
U_LORA = N_FFN
U_FILTER = U_LORA + 2
U_HYENA = U_FILTER + 1
U_DFT = U_HYENA + 2 * HY_C
U_RWKV = U_DFT + 4
U_GDN = U_RWKV + 2 * PAIRS
U_WOUT = U_GDN + 2 * PAIRS
U_XQ = U_WOUT + KT // 2
U_XK = U_XQ + KT // 2
U_XV = U_XK + KT // 2
U_XO = U_XV + KT // 2
U_FFN2 = U_XO + KT // 2
U_PAD = U_FFN2 + N_FFN
UNITS = U_PAD + U_PAD % 2

S_FFN1 = 0
S_WOUT = S_FFN1 + N_FFN
S_XQ = S_WOUT + KT // 2
S_XO = S_XQ + KT // 2
S_FFN2 = S_XO + KT // 2
SPLIT_UNITS = S_FFN2 + N_FFN
assert SPLIT_UNITS % 2 == 0
A_FFN1, A_WOUT, A_XQ, A_XO, A_FFN2 = range(5)
SPLIT_SOURCES = 5

_n = 0


def _cols(k):
    global _n
    _n += k
    return _n - k


C_NORM = _cols(4 * KT)
C_HY = _cols(13 * HY_C)
C_FILT = _cols(3)
C_LMU = _cols(6)
C_GNW = _cols(1)
C_DT = _cols(2 * HEADS)
C_ALOG = _cols(2 * HEADS)
C_RW = _cols(13 * PAIRS)
C_GD = _cols(9 * PAIRS)
N_COLS = _n
RWC, GDC = 13, 9
C_MEM, C_FINAL = 0, KT

_n = 0
K_ID = _cols(P)
K_ONES = _cols(P)
K_BONES = _cols(P)
K_RWTRI = _cols(2 * 2 * P)
K_GTRI = _cols(2 * P)
K_LEVEL = _cols(LEVELS * 2 * P)
K_SI = _cols(2 * 2 * P)
K_NEGT = _cols(TT)
K_SEL = _cols(PAIRS * 4 * P)
N_CONST = _n


def shape_constants():
    c = np.zeros((P, N_CONST), np.float32)
    i = np.arange(P)
    row, col = i[:, None], i[None, :]
    c[:, K_ID:K_ID + P] = row == col
    c[:, K_ONES:K_ONES + P] = 1.0
    c[:, K_BONES:K_BONES + P] = row // HD == col // HD
    half = P // 2
    for d in range(2):
        incl = (row <= col) if d == 0 else (row >= col)
        excl = (row < col) if d == 0 else (row > col)
        mid = (row < half) if d == 0 else (row >= half)
        at = K_RWTRI + d * 2 * P
        c[:, at:at + P] = incl.astype(np.float32) - mid
        c[:, at + P:at + 2 * P] = excl.astype(np.float32) - mid
        c[:, K_GTRI + d * P:K_GTRI + (d + 1) * P] = incl
        c[:, K_SI + d * 2 * P:K_SI + d * 2 * P + P] = excl
        c[:, K_SI + d * 2 * P + P:K_SI + (d + 1) * 2 * P] = incl
        for m in range(LEVELS):
            b = 2 ** m
            target, source = (row, col) if d == 0 else (col, row)
            ok = (target // (2 * b) == source // (2 * b)) & (target // b % 2 == 1) & (source // b % 2 == 0)
            at = K_LEVEL + (m * 2 + d) * P
            c[:, at:at + P] = ok
    t = np.linspace(0.0, 1.0, SEQ, dtype=np.float32)
    c[:, K_NEGT:K_NEGT + TT] = -t.reshape(TT, P).T
    for j in range(PAIRS):
        for d in range(2):
            for h in range(2):
                at = K_SEL + (j * 4 + d * 2 + h) * P
                c[d * HEADS + 2 * j + h, at:at + P] = 1.0
    return c


def dft_units():
    t, f = np.arange(SEQ)[:, None], np.arange(SEQ)[None, :]
    ang = 2 * np.pi * (((2 * f + 1) * t) % (4 * SEQ)) / (4 * SEQ)
    out = []
    for m in (np.cos(ang), np.sin(ang), np.cos(ang).T, np.sin(ang).T):
        out.append(m.astype(np.float32).reshape(TT, P, SEQ).transpose(1, 0, 2).reshape(P, UNIT))
    return out


def positional_features():
    t = np.linspace(0.0, 1.0, SEQ, dtype=np.float32)[:, None]
    ang = (np.float32(2.0 * np.pi) * np.arange(SEQ, dtype=np.float32)[:, None] / np.float32(SEQ)).astype(np.float32)
    bands = np.linspace(1e-4, 15, 16, dtype=np.float32)[None, :]
    return np.concatenate([t, np.cos(bands * ang), -np.sin(bands * ang)], axis=-1).astype(np.float32)


class Signal:

    def __init__(self, sem, per):
        self.sem, self.per = sem, per

    def at(self, it, k):
        return it * self.per + k


def trunk_program(nc, xT, memT, units, cols, gcols, consts, out, dump=None, layers=DEPTH):
    ctx = ExitStack()
    with ctx:
        place = {}

        def sb(name, shape):
            t = ctx.enter_context(nc.sbuf_tensor(name, shape, F32))
            place[name] = nc.sbuf_base - 4 * int(np.prod(shape[1:]))
            return t

        def rounded(name, shape, where, floats=0):
            t = nc.alloc_sbuf_tensor_at(name, [P] + shape, F32R, offset=place[where] + 4 * floats)
            return t[tuple(slice(None) for _ in range(len(shape) + 1))]

        def sig(name, per=1):
            return Signal(ctx.enter_context(nc.semaphore(name)), per)

        x = sb("x", [P, KT, SEQ])
        h = sb("h", [P, KT, SEQ])
        memn = sb("memn", [P, KT, N_MEM])
        y = sb("y", [P, KT, SEQ])
        ring = [sb(f"ring{i}", [P, UNIT]) for i in range(2)]
        kon = sb("kon", [P, N_CONST])
        cols_all = sb("cols_all", [P, DEPTH, N_COLS])
        gc = sb("gcols_sb", [P, 2 * KT])
        cl = sb("cl", [P, N_COLS])
        clj = sb("clj", [P, RWC])
        eps = sb("eps", [P, 2])
        lwT, laT, lgT = (sb(n, [P, SEQ]) for n in ("lwT", "laT", "lgT"))
        lora_c0 = sb("lora_c0", [P, 3])
        nega = sb("nega", [P, 2 * HEADS])
        beta = sb("beta", [P, TT, 2 * HEADS])
        gsum = sb("gsum", [P, TT, 2 * HEADS])
        gsumT = sb("gsumT", [P, SEQ])
        sc = sb("scratch", [P, 23600])
        psum = ctx.enter_context(nc.psum_tensor("psum", [P, 8, 512], F32))
        bank = [psum[:, i, :] for i in range(8)]

        ident = kon[:, K_ID:K_ID + P]
        ones = kon[:, K_ONES:K_ONES + P]
        bones = kon[:, K_BONES:K_BONES + P]
        rwtri = [[kon[:, K_RWTRI + (2 * d + e) * P:K_RWTRI + (2 * d + e + 1) * P] for e in range(2)] for d in range(2)]
        gtri = [kon[:, K_GTRI + d * P:K_GTRI + (d + 1) * P] for d in range(2)]
        strict_incl = [kon[:, K_SI + d * 2 * P:K_SI + (d + 1) * 2 * P] for d in range(2)]
        incl = [kon[:, K_SI + (2 * d + 1) * P:K_SI + (2 * d + 2) * P] for d in range(2)]

        def level_mask(m, d):
            at = K_LEVEL + (m * 2 + d) * P
            return kon[:, at:at + P]

        def over(ap, n):
            return ap.unsqueeze(1).broadcast_to([ap.shape[0], n, ap.shape[-1]])

        at = [0]

        def carve(*shape):
            n = int(np.prod(shape))
            v = sc[:, at[0]:at[0] + n]
            at[0] += n
            assert at[0] <= 23600, at[0]
            if len(shape) == 2:
                return v.rearrange("p (a b) -> p a b", a=shape[0])
            if len(shape) == 3:
                return v.rearrange("p (a b c) -> p a b c", a=shape[0], b=shape[1])
            return v

        sq = carve(KT, SEQ)
        std = carve(SEQ)
        rstd = carve(SEQ)
        at[0] = 0
        u = carve(FB, SEQ)
        w_hi, w_lo = ([rounded(f"unit_{part}{i}", [UNIT], "scratch", at[0] + (2 * e + i) * UNIT) for i in range(2)]
                      for e, part in enumerate(("hi", "lo")))
        at[0] += 4 * UNIT
        u_hi, u_lo = ([rounded(f"inner_{part}{i}", [2, SEQ], "scratch", at[0] + (2 * e + i) * 2 * SEQ) for i in range(2)]
                      for e, part in enumerate(("hi", "lo")))
        at[0] += 8 * SEQ
        assert at[0] <= 23600
        sil = [lwT[:, :], laT[:, :]]
        a_hi, a_lo = rounded("source_hi", [KT, SEQ], "h"), rounded("source_lo", [KT, SEQ], "y")
        at[0] = 0
        gx, ge, gl = (carve(TT, 2 * HEADS) for _ in range(3))
        gtok = carve(TT, 2 * HEADS)
        at[0] = 0
        filt_arg, filt_k, filt_h1, filt_h2 = (carve(SEQ) for _ in range(4))
        filt = carve(TT, 512)
        filt_e = carve(TT, 512)
        filt_sum = carve(512)
        filt_rn = carve(256)
        kplus, kminus = carve(TT, 256), carve(TT, 256)
        at[0] = 0
        _keep = carve(4 * SEQ)
        hx0 = [carve(SEQ) for _ in range(2)]
        hu = [carve(SEQ) for _ in range(2)]
        utok = carve(TT, 256)
        at[0] = 4 * SEQ + TT * 512 * 2 + 512 + 256 + 2 * TT * 256
        hx1, hv = carve(SEQ), carve(SEQ)
        spec = carve(8, 512)
        prA, prB, prT = carve(TT, 256), carve(TT, 256), carve(TT, 256)
        hyo = prT.rearrange("p a b -> p (a b)")
        hyo = [hyo[:, 0:512], hyo[:, 512:1024]]
        at[0] = 0
        AR = [carve(TT, 2, P) for _ in range(2)]
        KTt = [carve(SEQ) for _ in range(2)]
        BTt = [carve(SEQ) for _ in range(2)]
        Vtok = carve(TT, P)
        Btok = [carve(TT, P) for _ in range(2)]
        Ktok = [carve(TT, P) for _ in range(2)]
        gateT, bv, yo = carve(SEQ), carve(SEQ), carve(SEQ)
        Z = [carve(HD) for _ in range(2)]
        Tt = [carve(P) for _ in range(2)]
        Ut = [carve(P) for _ in range(2)]
        lastP, firstP, fac = (carve(2, TT) for _ in range(3))
        rwc = carve(4)
        late = at[0]
        SCB = [carve(TT, 2, P) for _ in range(4)]
        SCK = [carve(TT, 2, P) for _ in range(4)]
        X, XT, Y = ([carve(TT, P) for _ in range(4)] for _ in range(3))
        at[0] = late
        rT, kT, vT, kkr, kk, nkk, tmpA, tmpB, rk = (carve(SEQ) for _ in range(9))
        aT = [carve(SEQ) for _ in range(2)]
        sg = [carve(TT, P) for _ in range(2)]
        Pinc = [carve(TT, P) for _ in range(2)]
        Pinv = [carve(TT, P) for _ in range(2)]
        Pexc = [carve(TT, P) for _ in range(2)]
        aP, kd = ([carve(SEQ) for _ in range(2)] for _ in range(2))
        at[0] = 0
        GA = [carve(TT, P) for _ in range(2)]
        GR = [carve(TT, P) for _ in range(2)]
        GV = carve(TT, P)
        GKtok = carve(TT, P)
        Kend = [carve(TT, 2, HD) for _ in range(2)]
        EG = [carve(TT, P) for _ in range(2)]
        zg, go, gqT, gkT, gvT = (carve(SEQ) for _ in range(5))
        GZ = [carve(HD) for _ in range(2)]
        GT = [carve(P) for _ in range(2)]
        GU = [carve(P) for _ in range(2)]
        selj = carve(4, P)
        gcj, btj, nbj = (carve(TT, 4) for _ in range(3))
        KEp, KE = carve(4, TT), carve(4, TT)
        GL = [carve(TT, P) for _ in range(4)]
        GAT = [carve(TT, P) for _ in range(4)]
        GDT = [carve(TT, P) for _ in range(4)]
        assert at[0] <= late + 8 * TT * 2 * P
        at[0] = late + 8 * TT * 2 * P
        gs1, gs2, gr1, gr2 = (carve(SEQ) for _ in range(4))
        at[0] = 0
        qT = carve(KT, SEQ)
        kmT = carve(KT, N_MEM)
        vm = carve(2, D_MODEL)
        prob = carve(TT, N_MEM)
        probT = carve(2, SEQ)
        nmx, psm, rsm = carve(TT), carve(TT), carve(TT)
        assert at[0] <= FB * SEQ
        at[0] = FB * SEQ + 4 * UNIT
        oT = carve(KT, SEQ)

        full = [sig(f"unit_loaded_in_slot{i}", 16 * UNITS // 2) for i in range(2)]
        free = sig("unit_used", UNITS)
        consts_in = sig("constants_loaded")
        eps_set = sig("eps_set")
        x_in = sig("inputs_loaded")
        lay_cols = sig("layer_columns_ready")
        J = {n: sig("joined_" + n, 4 * k) for n, k in
             dict(start=1, ffn=1, norm=1, lora=1, filter=1, hyena=1, dft=1, rwkv=5, gdn=4, proj=1, attn=1,
                  layer=1).items()}
        n_sq, n_sum, n_std = (sig(n, k) for n, k in
                                      (("squares_ready", KT), ("square_sum_ready", 1), ("std_ready", 1)))
        xv_ps = sig("mem_values_ready")
        f_sil, f_u, f_dn = sig("silu_ready", 2), sig("inner_ready", 2), sig("ffn_down_ready", KT)
        ws_hi, ws_lo, ws_done = (sig(n, SPLIT_UNITS) for n in ("unit_hi_ready", "unit_lo_ready", "unit_products_done"))
        as_f, as_hi, as_lo = (sig(n, KT) for n in ("normed_ready", "source_hi_ready", "source_lo_ready"))
        lo_ps, lo_base, lo_done = sig("lora_products_ready", 4), sig("lora_base_ready", 3), sig("lora_shifted", 3)
        ga_a, ga_b, ga_c, ga_d, ga_e, ga_f = (sig(f"gate_step{i}", 1) for i in range(6))
        ga_t, ga_g = sig("gate_rows_ready", 1), sig("gate_sums_ready", 1)
        fl_ps, fl_arg, fl_h = sig("filter_layer_ready", 2), sig("filter_argument_ready", 2), sig("filter_sine_ready", 2)
        fl_out, fl_e, fl_k, fl_abs, fl_sum, fl_s = (sig(n, k) for n, k in (
            ("filter_taps_ready", TT), ("filter_window_ready", TT), ("filter_windowed", TT), ("filter_abs_ready", TT),
            ("filter_sum_ready", 1), ("filter_sum_copied", 1)))
        hy_ps, hy_base, hy_cv = sig("hyena_projected", 3 * 2), sig("hyena_base_ready", 3 * 2), sig("hyena_u_ready", 2)
        hy_tp = sig("hyena_u_turned", 2)
        sp_ps, sp_sb, sp_pr, sp_y = sig("spectra_ready", 8), sig("spectra_copied", 8), sig("product_ready", 2), sig("hyena_y_ready", 2)
        rw_ps, rw_base, rw_cols = sig("rwkv_projected", 8), sig("rwkv_base_ready", 3), sig("rwkv_columns_ready", 1)
        rw_a, rw_w0, rw_sig = sig("rwkv_rates_ready", 2), sig("rwkv_w0_added", 2), sig("rwkv_decay_ready", 2)
        rw_kk2, rw_rk = sig("rwkv_kk_squared", 1), sig("rwkv_rk_ready", 1)
        rw_g, rw_nrm, rw_std, rw_bon = sig("rwkv_sums_ready", 4), sig("rwkv_kk_norm_ready", 1), sig("rwkv_kk_std_ready", 1), sig("rwkv_bonus_ready", 1)
        rw_exp, rw_kd, rw_gstd = sig("rwkv_decays_ready", 8), sig("rwkv_kd_ready", 2), sig("rwkv_group_std_ready")
        rw_tp = sig("rwkv_turned", 5)
        rw_scp, rw_scs = sig("rwkv_scores_ready", 16), sig("rwkv_scores_masked", 16)
        rw_fin = [sig(f"rwkv_finish{i}", 1) for i in range(6)]
        iv = dict(
            half=sig("inv_start_product", 4), xt=sig("inv_xt_ready", 4 * LEVELS),
            xps=sig("inv_x_turned", 4 * (LEVELS - 1)), x=sig("inv_x_ready", 4 * (LEVELS - 1)),
            yps=sig("inv_lx_product", 4 * (LEVELS - 1)), y=sig("inv_lx_ready", 4 * (LEVELS - 1)),
            xtps=sig("inv_xy_product", 4 * (LEVELS - 1)))
        scan_sig = dict(
            z0=sig("state_cleared", 1),
            tps=[sig(f"t_product{d}", TT) for d in range(2)], t=[sig(f"t_ready{d}", TT) for d in range(2)],
            ups=[sig(f"u_product{d}", TT) for d in range(2)], u=[sig(f"u_ready{d}", TT) for d in range(2)],
            zps=[sig(f"state_product{d}", TT - 1) for d in range(2)], z=[sig(f"state_ready{d}", TT - 1) for d in range(2)])
        gd_ps, gd_base, gd_sh, gd_silu = sig("gdn_projected", 4), sig("gdn_base_ready", 3), sig("gdn_convolved", 3), sig("gdn_silu_ready", 3)
        gd_sq, gd_nrm, gd_std, gd_qk = sig("gdn_squares_ready", 2), sig("gdn_norms_ready", 2), sig("gdn_std_ready", 2), sig("gdn_qk_ready", 2)
        gd_sel, gd_row, gd_dif, gd_exp, gd_msk = sig("gdn_pair_columns_ready", 1), sig("gdn_rows_ready", 4), sig("gdn_differences_ready", 4), sig("gdn_decays_ready", 4), sig("gdn_decays_masked", 4)
        gd_eg = sig("gdn_row_decays_ready", 4)
        gd_tp, gd_tok, gd_kk = sig("gdn_turned", 2), sig("gdn_tokens_ready", 2), sig("gdn_kk_ready", 4)
        gd_fin = [sig(f"gdn_finish{i}", 1) for i in range(6)]
        pj_done = sig("projection_added", 4)
        xk_ps, xk_done = sig("mem_projection_ready", 8), sig("mem_projection_copied", 8)
        at_s, at_mx, at_e, at_n, at_tp, at_pt, at_o, at_od = (sig(n, k) for n, k in (
            ("scores_ready", XA_HEADS * TT), ("row_max_ready", XA_HEADS), ("probs_ready", XA_HEADS * TT), ("probs_normed", XA_HEADS),
            ("probs_turned", XA_HEADS * 2), ("probs_t_ready", XA_HEADS * 2), ("attn_out_ready", XA_HEADS * 2), ("attn_out_copied", XA_HEADS * 2)))
        stored = sig("output_stored")
        passed = sig("waits_settled")
        dumped = sig("dumped") if dump else None

        def tap(eng, where, what):
            if dump is not None:
                dump(eng, where, what, dumped)

        def turn_of(l, mixer, j):
            return (l * 2 + mixer) * PAIRS + j

        def settle(eng):
            eng.sem_inc(passed.sem, 1)

        def join(eng, name, it, k, idle=False):
            s = J[name]
            if idle:
                eng.sem_inc(s.sem, 1)
            else:
                eng.drain().then_inc(s.sem, 1)
            eng.wait_ge(s.sem, s.at(it, 4 * k))
            settle(eng)

        def landed(l, n, later=0):
            return l * full[n % 2].per + 16 * (n // 2 + 1) + later * 16

        block = ctx.enter_context(nc.Block())

        @block.sync
        def _(sp):
            sp.dma_start(kon[:, :], consts).then_inc(consts_in.sem, 16)
            sp.dma_start(cols_all[:, :, :], cols).then_inc(consts_in.sem, 16)
            sp.dma_start(gc[:, :], gcols).then_inc(consts_in.sem, 16)
            sp.dma_start(sc[:, 8192:8192 + KT * N_MEM].rearrange("p (a b) -> p a b", a=KT), memT).then_inc(x_in.sem, 16)
            sp.dma_start(x[:, :, :], xT).then_inc(x_in.sem, 16)
            with sp.Fori(0, layers * UNITS // 2, 1) as n2:
                n = n2 * 2
                for s in range(2):
                    sp.wait_ge(free.sem, n + (s + 1))
                    sp.dma_start(ring[s][:, :], units[bass.ds(n + s, 1), :, :].rearrange("a p n -> (a p) n")).then_inc(full[s].sem, 16)
            sp.wait_ge(J["norm"].sem, J["norm"].at(4 * layers + 2, 0))
            sp.dma_start(out, h[:, :, :]).then_inc(stored.sem, 16)
            sp.wait_ge(stored.sem, 16)

        @block.tensor
        def _(pe):
            mm = pe.matmul

            def used(n=1):
                pe.drain().then_inc(free.sem, n)

            def norm(it, src_sq, n_tok):
                for t in range(KT):
                    pe.wait_ge(n_sq.sem, n_sq.at(it, t + 1))
                    last = mm(bank[7][:, 0:n_tok], ones, src_sq[:, t, 0:n_tok], start=t == 0, stop=t == KT - 1)
                last.then_inc(n_sum.sem, 1)
                join(pe, "norm", it, 1)

            def project(dst, slot, half, src, l, unit, done, width=SEQ):
                w = ring[slot][:, half * KT * P:(half + 1) * KT * P].rearrange("p (k c) -> p k c", k=KT)
                pe.wait_ge(full[(unit) % 2].sem, landed(l, unit))
                for k in range(KT):
                    last = mm(dst, w[:, k, :], src[:, k, 0:width], start=k == 0, stop=k == KT - 1)
                last.then_inc(done.sem, 1)

            def products(dst, w_h, w_l, a_h, a_l, start=False, stop=False):
                mm(dst, w_h, a_h, start=start, stop=False)
                mm(dst, w_h, a_l, start=False, stop=False)
                return mm(dst, w_l, a_h, start=False, stop=stop)

            def two_blocks(b, dsts, a_h, a_l, source=None):
                wh, wl = (w[b].rearrange("p (m k c) -> p m k c", m=2, k=KT) for w in (w_hi, w_lo))
                for k in range(KT):
                    if source is not None:
                        pe.wait_ge(as_lo.sem, as_lo.at(source, k + 1))
                    for m in range(2):
                        last = products(dsts[m], wh[:, m, k, :], wl[:, m, k, :], a_h[:, k, :], a_l[:, k, :],
                                        start=k == 0, stop=k == KT - 1)
                return last

            def ffn(l, which, n0, source):
                with pe.Fori(0, FB // 2, 1) as j:
                    it = (l * 2 + which) * (FB // 2) + j
                    for s in range(2):
                        pe.wait_ge(ws_lo.sem, ws_lo.at(l, n0 + s + 1) + j * 2)
                        pe.wait_ge(f_u.sem, it * 2 + (s + 1))
                        two_blocks((n0 + s) % 2, [bank[2 * s + m][:, :] for m in range(2)], a_hi, a_lo,
                                   None if s else l * SPLIT_SOURCES + source).then_inc(ws_done.sem, 1)
                n0 += FB

                def down(n, banks, ks, first=False):
                    wh, wl = (w[n % 2].rearrange("p (k c) -> p k c", k=2) for w in (w_hi, w_lo))
                    for k in ks:
                        for m in banks:
                            last = products(bank[m][:, :], wh[:, k, m * P:(m + 1) * P], wl[:, k, m * P:(m + 1) * P],
                                            u_hi[n % 2][:, k, :], u_lo[n % 2][:, k, :], start=first)
                    return last

                pe.wait_ge(ws_lo.sem, ws_lo.at(l, n0 + 1))
                down(n0, range(4, 8), (0,), first=True)
                pe.wait_ge(f_u.sem, ((l * 2 + which) + 1) * FB + 2)
                down(n0, range(4), (0,), first=True)
                down(n0, range(8), (1,)).then_inc(ws_done.sem, 1)
                with pe.Fori(0, 4, 1) as j:
                    for s in range(2):
                        pe.wait_ge(ws_lo.sem, ws_lo.at(l, n0 + s + 2) + j * 2)
                        down(n0 + 1 + s, range(8), (0, 1)).then_inc(ws_done.sem, 1)
                pe.wait_ge(ws_lo.sem, ws_lo.at(l, n0 + 10))
                down(n0 + 9, range(8), (0, 1)).then_inc(ws_done.sem, 1)
                pe.wait_ge(ws_lo.sem, ws_lo.at(l, n0 + 11))
                wh, wl = (w[n0 % 2].rearrange("p (k c) -> p k c", k=2) for w in (w_hi, w_lo))
                for m in range(KT):
                    for k in range(2):
                        last = products(bank[m][:, :], wh[:, k, m * P:(m + 1) * P], wl[:, k, m * P:(m + 1) * P],
                                        u_hi[n0 % 2][:, k, :], u_lo[n0 % 2][:, k, :], stop=k == 1)
                    last.then_inc(f_dn.sem, 1)
                pe.drain().then_inc(ws_done.sem, 1)
                join(pe, "ffn", l * 2 + which, 1)

            def lora(l):
                for m, (unit, half) in enumerate(((U_LORA, 0), (U_LORA, 1), (U_LORA + 1, 0))):
                    project(bank[m][:, :], unit % 2, half, h, l, unit, lo_ps)
                w = ring[(U_LORA + 1) % 2][:, KT * P:KT * P + KT * 24].rearrange("p (k c) -> p k c", k=KT)
                for t in range(TT):
                    for k in range(KT):
                        last = mm(bank[3][:, t * 24:t * 24 + 24], h[:, k, t * P:(t + 1) * P], w[:, k, :],
                                  start=k == 0, stop=k == KT - 1)
                last.then_inc(lo_ps.sem, 1)
                used(2)
                pe.wait_ge(ga_e.sem, ga_e.at(l, 1))
                for t in range(TT):
                    for d in range(2):
                        last = mm(bank[4][:, (t * 2 + d) * HEADS:(t * 2 + d + 1) * HEADS], gtri[d],
                                  gtok[:, t, d * HEADS:(d + 1) * HEADS], start=True, stop=True)
                last.then_inc(ga_f.sem, 1)
                pe.wait_ge(ga_g.sem, ga_g.at(l, 1))
                for t in range(TT):
                    last = pe.transpose(bank[5][0:2 * HEADS, t * P:(t + 1) * P], gsum[:, t, :], ident)
                last.then_inc(ga_t.sem, 1)
                join(pe, "lora", l, 1)

            def hyena_filter(l):
                w = ring[U_FILTER % 2]
                pe.wait_ge(full[(U_FILTER) % 2].sem, landed(l, U_FILTER))
                settle(pe)
                mm(bank[0][0:HY_FFN, :], w[0:HY_EMB, 512:512 + HY_FFN], w[0:HY_EMB, 1152:1152 + SEQ],
                   start=True, stop=True).then_inc(fl_ps.sem, 1)
                pe.wait_ge(fl_h.sem, fl_h.at(l, 1))
                settle(pe)
                mm(bank[1][0:HY_FFN, :], w[0:HY_FFN, 576:576 + HY_FFN], filt_h1[0:HY_FFN, :],
                   start=True, stop=True).then_inc(fl_ps.sem, 1)
                pe.wait_ge(fl_h.sem, fl_h.at(l, 2))
                for t in range(TT):
                    mm(bank[2 + t][:, :], filt_h2[0:HY_FFN, t * P:(t + 1) * P], w[0:HY_FFN, 0:512],
                       start=True, stop=True).then_inc(fl_out.sem, 1)
                for t in range(TT):
                    pe.wait_ge(fl_abs.sem, fl_abs.at(l, t + 1))
                    last = mm(bank[6][:, :], ones, filt_e[:, t, :], start=t == 0, stop=t == TT - 1)
                last.then_inc(fl_sum.sem, 1)
                join(pe, "filter", l, 1)
                used()

            def hyena(l):
                for c in range(HY_C):
                    for m in range(3):
                        unit = U_HYENA + 2 * c + m // 2
                        project(bank[4 * c + m][:, :], unit % 2, m % 2, h, l, unit, hy_ps)
                    used(2)
                for c in range(HY_C):
                    pe.wait_ge(hy_cv.sem, hy_cv.at(l, c + 1))
                    for t in range(TT):
                        last = pe.transpose(bank[4 * c + 3][:, t * P:(t + 1) * P], hu[c][:, t * P:(t + 1) * P], ident)
                    last.then_inc(hy_tp.sem, 1)
                join(pe, "hyena", l, 1)
                for part, flt in ((0, kplus), (1, kminus)):
                    unit = U_DFT + part
                    pe.wait_ge(full[(unit) % 2].sem, landed(l, unit))
                    w = ring[unit % 2][:, :].rearrange("p (t f) -> p t f", t=TT)
                    for f in range(TT):
                        for half, src in ((0, utok), (1, flt)):
                            for t in range(TT):
                                last = mm(bank[4 * part + f][:, half * 256:half * 256 + 256], w[:, t, f * P:(f + 1) * P],
                                          src[:, t, :], start=t == 0, stop=t == TT - 1)
                        last.then_inc(sp_ps.sem, 1)
                    used()
                pe.wait_ge(sp_pr.sem, sp_pr.at(l, 2))
                pe.wait_ge(full[(U_DFT + 2) % 2].sem, landed(l, U_DFT + 2))
                pe.wait_ge(full[(U_DFT + 3) % 2].sem, landed(l, U_DFT + 3))
                for c in range(HY_C):
                    for part, src in ((0, prA), (1, prB)):
                        w = ring[(U_DFT + part) % 2][:, :].rearrange("p (f t) -> p f t", f=TT)
                        for f in range(TT):
                            last = mm(bank[c][:, :], src[:, f, c * P:(c + 1) * P], w[:, f, :],
                                      start=part == 0 and f == 0, stop=part == 1 and f == TT - 1)
                    last.then_inc(sp_y.sem, 1)
                used(2)
                join(pe, "dft", l, 1)

            def invert(turn, LT):
                s = iv
                L1 = LEVELS - 1
                for g in range(4):
                    pe.wait_ge(s["xt"].sem, s["xt"].at(turn, g + 1))
                    for t in range(TT):
                        last = pe.transpose(bank[g][:, t * P:(t + 1) * P], XT[g][:, t, :], ident)
                    last.then_inc(s["xps"].sem, 1)
                for m in range(L1):
                    for g in range(4):
                        pe.wait_ge(s["x"].sem, s["x"].at(turn, 4 * m + g + 1))
                        for t in range(TT):
                            last = mm(bank[g][:, t * P:(t + 1) * P], LT[g](t), X[g][:, t, :], start=True, stop=True)
                        last.then_inc(s["yps"].sem, 1)
                    for g in range(4):
                        pe.wait_ge(s["y"].sem, s["y"].at(turn, 4 * m + g + 1))
                        for t in range(TT):
                            last = mm(bank[4 + g][:, t * P:(t + 1) * P], Y[g][:, t, :], XT[g][:, t, :], start=True, stop=True)
                        last.then_inc(s["xtps"].sem, 1)
                    if m < L1 - 1:
                        for g in range(4):
                            pe.wait_ge(s["xt"].sem, s["xt"].at(turn, 4 * (m + 1) + g + 1))
                            for t in range(TT):
                                last = pe.transpose(bank[g][:, t * P:(t + 1) * P], XT[g][:, t, :], ident)
                            last.then_inc(s["xps"].sem, 1)

            def scan(turn, A, R, V, LK, MB, MK, Bt, Kt_, Zs, Ts, Us):
                s = scan_sig
                pe.wait_ge(s["z0"].sem, s["z0"].at(turn, 1))
                for c in range(TT):
                    for d in range(2):
                        t = c if d == 0 else TT - 1 - c
                        if c:
                            pe.wait_ge(s["z"][d].sem, s["z"][d].at(turn, c))
                        for hh in range(2):
                            r = slice(hh * HD, hh * HD + HD)
                            g = 2 * d + hh
                            last = mm(bank[2 * d + hh][:, 0:HD], A[d](t)[r, :], Zs[d][r, :], start=True, stop=LK is None)
                            if LK is not None:
                                last = mm(bank[2 * d + hh][:, 0:HD], LK[g](t), V[:, t, r], start=False, stop=True)
                        last.then_inc(s["tps"][d].sem, 1)
                        for hh in range(2):
                            r = slice(hh * HD, hh * HD + HD)
                            mm(bank[4 + d][r, t * P:(t + 1) * P], Zs[d][r, :], R[d](t)[r, :], start=True, stop=False)
                    for d in range(2):
                        t = c if d == 0 else TT - 1 - c
                        pe.wait_ge(s["t"][d].sem, s["t"][d].at(turn, c + 1))
                        for hh in range(2):
                            r = slice(hh * HD, hh * HD + HD)
                            last = mm(bank[6 + d][:, r], XT[2 * d + hh][:, t, :], Ts[d][:, r], start=True, stop=True)
                        last.then_inc(s["ups"][d].sem, 1)
                    for d in range(2):
                        t = c if d == 0 else TT - 1 - c
                        pe.wait_ge(s["u"][d].sem, s["u"][d].at(turn, c + 1))
                        if c < TT - 1:
                            for hh in range(2):
                                r = slice(hh * HD, hh * HD + HD)
                                last = mm(bank[6 + d][r, P:P + HD], Bt[d](t)[:, r], Us[d][:, r], start=True, stop=Kt_ is None)
                                if Kt_ is not None:
                                    last = mm(bank[6 + d][r, P:P + HD], Kt_[d][:, t, r], V[:, t, r], start=False, stop=True)
                            last.then_inc(s["zps"][d].sem, 1)
                        for hh in range(2):
                            r = slice(hh * HD, hh * HD + HD)
                            g = 2 * d + hh
                            o = bank[4 + d][r, t * P:(t + 1) * P]
                            mm(o, Us[d][:, r], MB[g](t), start=False, stop=MK is None)
                            if MK is not None:
                                mm(o, V[:, t, r], MK[g](t), start=False, stop=True)

            def rwkv(l, j):
                it = l * PAIRS + j
                s0 = U_RWKV % 2
                s1 = 1 - s0
                small = ring[s1][:, KT * P:2 * KT * P]
                for m in range(3):
                    w = ring[(s0, s0, s1)[m]][:, (m % 2) * KT * P:(m % 2 + 1) * KT * P].rearrange("p (k c) -> p k c", k=KT)
                    pe.wait_ge(full[(U_RWKV + m // 2) % 2].sem, landed(l, U_RWKV + m // 2, j))
                    for k in range(KT):
                        last = mm(bank[m][:, :], w[:, k, :], h[:, k, :], start=k == 0, stop=k == KT - 1)
                    last.then_inc(rw_ps.sem, 1)
                mm(bank[3][:, :], small[:, 256:384], lgT[:, :], start=True, stop=True).then_inc(rw_ps.sem, 1)
                for d in range(2):
                    r = slice(d * HD, d * HD + HD)
                    mm(bank[4 + d][:, :], small[r, 128:256], laT[r, :], start=True, stop=True).then_inc(rw_ps.sem, 1)
                for d in range(2):
                    r = slice(d * HD, d * HD + HD)
                    for t in range(TT):
                        last = mm(bank[6 + d][:, t * P:(t + 1) * P], lwT[r, t * P:(t + 1) * P], small[r, 0:128], start=True, stop=True)
                    last.then_inc(rw_ps.sem, 1)
                join(pe, "rwkv", it, 1)
                used(2)
                pe.wait_ge(rw_kk2.sem, rw_kk2.at(it, 1))
                mm(bank[4][:, :], bones, tmpA[:, :], start=True, stop=True).then_inc(rw_nrm.sem, 1)
                pe.wait_ge(rw_rk.sem, rw_rk.at(it, 1))
                mm(bank[5][:, :], bones, rk[:, :], start=True, stop=True).then_inc(rw_bon.sem, 1)
                for d in range(2):
                    pe.wait_ge(rw_sig.sem, rw_sig.at(it, d + 1))
                    for e in range(2):
                        for t in range(TT):
                            last = mm(bank[2 * d + e][:, t * P:(t + 1) * P], sg[d][:, t, :], rwtri[d][e], start=True, stop=True)
                        last.then_inc(rw_g.sem, 1)
                join(pe, "rwkv", it, 2)
                for n, src in enumerate([vT, BTt[0], BTt[1], KTt[0], KTt[1]]):
                    for t in range(TT):
                        last = pe.transpose(bank[n][:, t * P:(t + 1) * P], src[:, t * P:(t + 1) * P], ident)
                    last.then_inc(rw_tp.sem, 1)
                join(pe, "rwkv", it, 3)
                for g in range(4):
                    d, hh = g // 2, g % 2
                    r = slice(hh * HD, hh * HD + HD)
                    for n in range(4):
                        src = (BTt, KTt)[n // 2][d]
                        if g >= 2:
                            pe.wait_ge(rw_scs.sem, rw_scs.at(it, 4 * (g - 2) + n + 1))
                        for e in range(2):
                            t = 2 * (n % 2) + e
                            last = mm(bank[4 * (g % 2) + n][:, e * 256:(e + 1) * 256], src[r, t * P:(t + 1) * P],
                                      AR[d][r, t, :, :].rearrange("p a b -> p (a b)"), start=True, stop=True)
                        last.then_inc(rw_scp.sem, 1)
                join(pe, "rwkv", it, 4)
                invert(turn_of(l, 0, j), [lambda t, g=g: SCB[g][:, t, 0, :] for g in range(4)])
                scan(turn_of(l, 0, j), [lambda t, d=d: AR[d][:, t, 0, :] for d in range(2)],
                     [lambda t, d=d: AR[d][:, t, 1, :] for d in range(2)], Vtok,
                     [lambda t, g=g: SCK[g][:, t, 0, :] for g in range(4)],
                     [lambda t, g=g: SCB[g][:, t, 1, :] for g in range(4)],
                     [lambda t, g=g: SCK[g][:, t, 1, :] for g in range(4)],
                     [lambda t, d=d: Btok[d][:, t, :] for d in range(2)], Ktok, Z, Tt, Ut)
                pe.drain().then_inc(rw_fin[0].sem, 1)
                pe.wait_ge(rw_fin[1].sem, rw_fin[1].at(it, 1))
                mm(bank[0][:, :], bones, yo[:, :], start=True, stop=True).then_inc(rw_fin[2].sem, 1)
                pe.wait_ge(rw_fin[3].sem, rw_fin[3].at(it, 1))
                mm(bank[1][:, :], bones, tmpA[:, :], start=True, stop=True).then_inc(rw_fin[4].sem, 1)
                join(pe, "rwkv", it, 5)

            def gdn(l, j):
                it = l * PAIRS + j
                for m in range(4):
                    slot = (U_GDN + m // 2) % 2
                    w = ring[slot][:, (m % 2) * KT * P:(m % 2 + 1) * KT * P].rearrange("p (k c) -> p k c", k=KT)
                    pe.wait_ge(full[(U_GDN + m // 2) % 2].sem, landed(l, U_GDN + m // 2, j))
                    for k in range(KT):
                        last = mm(bank[m][:, :], w[:, k, :], h[:, k, :], start=k == 0, stop=k == KT - 1)
                    last.then_inc(gd_ps.sem, 1)
                used(2)
                for n in range(2):
                    pe.wait_ge(gd_sq.sem, gd_sq.at(it, n + 1))
                    mm(bank[4 + n][:, :], bones, (gs1, gs2)[n][:, :], start=True, stop=True).then_inc(gd_nrm.sem, 1)
                join(pe, "gdn", it, 1)
                for g in range(4):
                    mm(bank[g][:, :], selj[0:2 * HEADS, g, :], gsumT[0:2 * HEADS, :], start=True, stop=True).then_inc(gd_row.sem, 1)
                for n, src in enumerate((gvT, gkT)):
                    for t in range(TT):
                        last = pe.transpose(bank[4 + n][:, t * P:(t + 1) * P], src[:, t * P:(t + 1) * P], ident)
                    last.then_inc(gd_tp.sem, 1)
                join(pe, "gdn", it, 2)
                for n in range(4):
                    r = slice((n % 2) * HD, (n % 2) * HD + HD)
                    rhs = (gkT, gqT)[n // 2]
                    for t in range(TT):
                        last = mm(bank[n][:, t * P:(t + 1) * P], gkT[r, t * P:(t + 1) * P], rhs[r, t * P:(t + 1) * P],
                                  start=True, stop=True)
                    last.then_inc(gd_kk.sem, 1)
                join(pe, "gdn", it, 3)
                invert(turn_of(l, 1, j), [lambda t, g=g: GL[g][:, t, :] for g in range(4)])
                scan(turn_of(l, 1, j), [lambda t, d=d: GA[d][:, t, :] for d in range(2)],
                     [lambda t, d=d: GR[d][:, t, :] for d in range(2)], GV, None,
                     [lambda t, g=g: GAT[g][:, t, :] for g in range(4)], None,
                     [lambda t, d=d: Kend[d][:, t, :, :].rearrange("p a b -> p (a b)") for d in range(2)], None, GZ, GT, GU)
                pe.drain().then_inc(gd_fin[0].sem, 1)
                pe.wait_ge(gd_fin[1].sem, gd_fin[1].at(it, 1))
                mm(bank[0][:, :], bones, gs1[:, :], start=True, stop=True).then_inc(gd_fin[2].sem, 1)
                join(pe, "gdn", it, 4)

            def projections(l, which, n0, source, a_low):
                with pe.Fori(0, 2, 1) as j:
                    it = (l * 3 + which) * 2 + j
                    for s in range(2):
                        pe.wait_ge(ws_lo.sem, ws_lo.at(l, n0 + s + 1) + j * 2)
                        pe.wait_ge(pj_done.sem, it * 4 + (2 * s + 2))
                        two_blocks((n0 + s) % 2, [bank[2 * s + m][:, :] for m in range(2)], a_hi, a_low,
                                   None if s else l * SPLIT_SOURCES + source).then_inc(ws_done.sem, 1)
                join(pe, "proj", l * 3 + which, 1)

            def attention(l):
                projections(l, 1, S_XQ, A_XQ, a_lo)
                for m in range(KT):
                    if m >= 4:
                        pe.wait_ge(xk_done.sem, xk_done.at(l, m - 3))
                    project(bank[m % 4][:, 0:N_MEM], (U_XK + m // 2) % 2, m % 2, memn, l, U_XK + m // 2, xk_ps, N_MEM)
                    if m % 2:
                        used()
                for n in range(4):
                    pe.wait_ge(full[(U_XV + n) % 2].sem, landed(l, U_XV + n))
                    w = ring[(U_XV + n) % 2][:, :].rearrange("p (k c) -> p k c", k=KT)
                    for mt in range(2):
                        for k in range(KT):
                            last = mm(bank[4 + n][:, mt * 256:(mt + 1) * 256], memn[:, k, mt * P:(mt + 1) * P], w[:, k, :],
                                      start=k == 0, stop=k == KT - 1)
                    used()
                last.then_inc(xv_ps.sem, 1)
                join(pe, "attn", l * 2, 1)
                for a in range(XA_HEADS):
                    for t in range(TT):
                        for b in range(2):
                            last = mm(bank[t // 2][:, (t % 2) * 256:(t % 2 + 1) * 256], qT[:, 2 * a + b, t * P:(t + 1) * P],
                                      kmT[:, 2 * a + b, :], start=b == 0, stop=b == 1)
                        last.then_inc(at_s.sem, 1)
                    pe.wait_ge(at_n.sem, at_n.at(l, a + 1))
                    for m in range(2):
                        for t in range(TT):
                            last = pe.transpose(bank[2 + m][:, t * P:(t + 1) * P], prob[:, t, m * P:(m + 1) * P], ident)
                        last.then_inc(at_tp.sem, 1)
                    for b in range(2):
                        for m in range(2):
                            pe.wait_ge(at_pt.sem, at_pt.at(l, 2 * a + m + 1))
                            last = mm(bank[4 + b][:, :], vm[:, m, (2 * a + b) * P:(2 * a + b + 1) * P], probT[:, m, :],
                                      start=m == 0, stop=m == 1)
                        last.then_inc(at_o.sem, 1)
                    pe.wait_ge(at_od.sem, at_od.at(l, 2 * a + 2))
                    settle(pe)
                join(pe, "attn", l * 2 + 1, 1)
                projections(l, 2, S_XO, A_XO, a_lo)

            pe.sem_inc(free.sem, 2)
            pe.sem_inc(ws_done.sem, 2)
            pe.wait_ge(consts_in.sem, 48)
            join(pe, "start", 0, 1)
            norm(0, sq, N_MEM)
            with pe.Fori(0, layers, 1) as l:
                join(pe, "layer", l, 1)
                norm(l * 4 + 1, sq, SEQ)
                ffn(l, 0, S_FFN1, A_FFN1)
                norm(l * 4 + 2, sq, SEQ)
                lora(l)
                hyena_filter(l)
                hyena(l)
                with pe.Fori(0, PAIRS, 1) as j:
                    rwkv(l, j)
                with pe.Fori(0, PAIRS, 1) as j:
                    gdn(l, j)
                projections(l, 0, S_WOUT, A_WOUT, a_lo)
                norm(l * 4 + 3, sq, SEQ)
                attention(l)
                norm(l * 4 + 4, sq, SEQ)
                ffn(l, 1, S_FFN2, A_FFN2)
            norm(4 * layers + 1, sq, SEQ)

        @block.scalar
        def _(act):
            A = act.activation

            def norm(it, src, n_tok, l=None, source=None):
                for t in range(KT):
                    A(sq[:, t, 0:n_tok], src[:, t, :], ACT.Square).then_inc(n_sq.sem, 1)
                act.wait_ge(n_sum.sem, n_sum.at(it, 1))
                A(std[:, 0:n_tok], bank[7][:, 0:n_tok], ACT.Sqrt, bias=eps[:, 0:1], scale=1.0 / D_MODEL).then_inc(n_std.sem, 1)
                if source is not None:
                    source_hi(l, source, sq, {A_FFN1: 0, A_XQ: 1, A_FFN2: 2}[source])
                join(act, "norm", it, 1)

            def unit_hi(l, n, unit, later=0, inner=None):
                act.wait_ge(full[unit % 2].sem, landed(l, unit, later))
                act.wait_ge(ws_done.sem, ws_done.at(l, n + 1) + later * 2)
                if inner is not None:
                    A(u_hi[n % 2], inner, ACT.Copy)
                A(w_hi[n % 2], ring[unit % 2][:, :], ACT.Copy).then_inc(ws_hi.sem, 1)

            def source_hi(l, source, src, normed=None):
                for t in range(KT):
                    if normed is not None:
                        act.wait_ge(as_f.sem, as_f.at(l * 3 + normed, t + 1))
                    A(a_hi[:, t, :], src[:, t, :], ACT.Copy).then_inc(as_hi.sem, 1)

            def ffn(l, which, n0, unit, source):
                unit_hi(l, n0, unit)
                unit_hi(l, n0 + 1, unit + 1)

                def silu(it, s, later):
                    act.wait_ge(ws_done.sem, ws_done.at(l, n0 + s + 3) + later * 2)
                    act.wait_ge(f_u.sem, it * 2 + (s + 1))
                    A(sil[s], bank[2 * s][:, :], ACT.Silu).then_inc(f_sil.sem, 1)

                with act.Fori(0, FB // 2 - 1, 1) as j:
                    for s in range(2):
                        silu((l * 2 + which) * (FB // 2) + j, s, j)
                        unit_hi(l, n0 + s + 2, unit + s + 2, j)
                for s in range(2):
                    silu((l * 2 + which) * (FB // 2) + (FB // 2 - 1), s, FB // 2 - 1)
                    unit_hi(l, n0 + FB + s, unit + FB + s, inner=u[:, 2 * s:2 * s + 2, :])
                n0, unit = n0 + FB, unit + FB
                with act.Fori(0, 4, 1) as j:
                    for s in range(2):
                        unit_hi(l, n0 + 2 + s, unit + 2 + s, j, u[:, bass.ds(j * 4 + (2 * s + 4), 2), :])
                act.wait_ge(f_u.sem, ((l * 2 + which) + 1) * FB + 2)
                unit_hi(l, n0 + 10, unit + 10, inner=u[:, 20:22, :])
                join(act, "ffn", l * 2 + which, 1)

            def projections(l, which, n0, unit):
                for n in range(KT // 2):
                    unit_hi(l, n0 + n, unit + n)
                join(act, "proj", l * 3 + which, 1)

            def lora(l):
                for m, dst in enumerate((lwT, laT, lgT)):
                    act.wait_ge(lo_ps.sem, lo_ps.at(l, m + 1))
                    if m == 0:
                        act.wait_ge(ga_a.sem, ga_a.at(l, 1))
                    A(dst[:, :], bank[m][:, :], ACT.Copy, scale=lora_c0[:, m:m + 1]).then_inc(lo_base.sem, 1)
                act.wait_ge(lo_done.sem, lo_done.at(l, 3))
                A(lwT[:, :], lwT[:, :], ACT.Tanh)
                A(lgT[:, :], lgT[:, :], ACT.Sigmoid)
                act.wait_ge(ga_b.sem, ga_b.at(l, 1))
                A(beta[:, :, :], bank[3][:, 0:TT * 24].rearrange("p (t c) -> p t c", t=TT)[:, :, 12:24], ACT.Sigmoid)
                A(ge[:, :, :], ge[:, :, :], ACT.Exp, scale=-1.0)
                A(nega[:, :], cl[:, C_ALOG:C_ALOG + 12], ACT.Exp)
                act.drain()
                A(gl[:, :, :], ge[:, :, :], ACT.Ln, bias=1.0).then_inc(ga_c.sem, 1)
                act.wait_ge(ga_f.sem, ga_f.at(l, 1))
                A(gsum[:, :, :], bank[4][:, 0:TT * 12].rearrange("p (t c) -> p t c", t=TT), ACT.Copy).then_inc(ga_g.sem, 1)
                act.wait_ge(ga_t.sem, ga_t.at(l, 1))
                A(gsumT[0:12, :], bank[5][0:12, :], ACT.Copy)
                join(act, "lora", l, 1)

            def hyena_filter(l):
                for n, dst in enumerate((filt_h1, filt_h2)):
                    act.wait_ge(fl_arg.sem, fl_arg.at(l, n + 1))
                    A(dst[0:HY_FFN, :], filt_arg[0:HY_FFN, :], ACT.Sin).then_inc(fl_h.sem, 1)
                w = ring[U_FILTER % 2]
                act.wait_ge(fl_out.sem, fl_out.at(l, 1))
                for t in range(TT):
                    A(filt_e[:, t, :], w[:, 640:1152], ACT.Exp, scale=kon[:, K_NEGT + t:K_NEGT + t + 1]).then_inc(fl_e.sem, 1)
                for t in range(TT):
                    act.wait_ge(fl_k.sem, fl_k.at(l, t + 1))
                    A(filt_e[:, t, :], filt[:, t, :], ACT.Abs).then_inc(fl_abs.sem, 1)
                act.wait_ge(fl_sum.sem, fl_sum.at(l, 1))
                A(filt_sum[:, :], bank[6][:, :], ACT.Copy).then_inc(fl_s.sem, 1)
                join(act, "filter", l, 1)

            def hyena(l):
                for c in range(HY_C):
                    for m, dst in enumerate((hx0[c], hx1, hv)):
                        act.wait_ge(hy_ps.sem, hy_ps.at(l, 3 * c + m + 1))
                        if c and m:
                            act.wait_ge(hy_cv.sem, hy_cv.at(l, c))
                        col = C_HY + 13 * c
                        A(dst[:, :], bank[4 * c + m][:, :], ACT.Identity, bias=cl[:, col + 9 + m:col + 10 + m],
                          scale=cl[:, col + 3 * m + 1:col + 3 * m + 2]).then_inc(hy_base.sem, 1)
                for c in range(HY_C):
                    act.wait_ge(hy_tp.sem, hy_tp.at(l, c + 1))
                    A(utok[:, :, c * P:(c + 1) * P], bank[4 * c + 3][:, :].rearrange("p (t c) -> p t c", t=TT), ACT.Copy)
                join(act, "hyena", l, 1)
                for n in range(8):
                    act.wait_ge(sp_ps.sem, sp_ps.at(l, n + 1))
                    A(spec[:, n, :], bank[n][:, :], ACT.Copy).then_inc(sp_sb.sem, 1)
                join(act, "dft", l, 1)

            def invert(turn):
                s = iv
                for m in range(LEVELS - 1):
                    for g in range(4):
                        act.wait_ge(s["xps"].sem, s["xps"].at(turn, 4 * m + g + 1))
                        A(X[g].rearrange("p a b -> p (a b)"), bank[g][:, :], ACT.Copy).then_inc(s["x"].sem, 1)

            def scan_u(turn):
                s = scan_sig
                for c in range(TT):
                    for d in range(2):
                        act.wait_ge(s["ups"][d].sem, s["ups"][d].at(turn, c + 1))
                        A(Ut[d][:, :], bank[6 + d][:, 0:P], ACT.Copy).then_inc(s["u"][d].sem, 1)

            def rwkv(l, j):
                it = l * PAIRS + j
                act.wait_ge(rw_cols.sem, rw_cols.at(it, 1))
                for m, dst in enumerate((rT, kT, vT)):
                    act.wait_ge(rw_ps.sem, rw_ps.at(it, m + 1))
                    A(dst[:, :], bank[m][:, :], ACT.Copy, scale=rwc[:, m:m + 1]).then_inc(rw_base.sem, 1)
                act.wait_ge(rw_ps.sem, rw_ps.at(it, 4))
                A(gateT[:, :], bank[3][:, :], ACT.Copy)
                for d in range(2):
                    act.wait_ge(rw_ps.sem, rw_ps.at(it, 5 + d))
                    A(aT[d][:, :], bank[4 + d][:, :], ACT.Sigmoid, bias=clj[:, 6 + d:7 + d]).then_inc(rw_a.sem, 1)
                act.drain()
                for d in range(2):
                    A(kd[d][:, :], aT[d][:, :], ACT.Identity, bias=rwc[:, 3:4], scale=clj[:, 9:10])
                join(act, "rwkv", it, 1)
                for d in range(2):
                    act.wait_ge(rw_w0.sem, rw_w0.at(it, d + 1))
                    A(sg[d][:, :, :], sg[d][:, :, :], ACT.Sigmoid).then_inc(rw_sig.sem, 1)
                act.wait_ge(rw_nrm.sem, rw_nrm.at(it, 1))
                A(tmpB[:, :], bank[4][:, :], ACT.Sqrt, bias=eps[:, 0:1]).then_inc(rw_std.sem, 1)
                for d in range(2):
                    last_t, first_t = (P - 1, 0) if d == 0 else (0, P - 1)
                    act.wait_ge(rw_g.sem, rw_g.at(it, 2 * d + 2))
                    gi = bank[2 * d][:, :].rearrange("p (t c) -> p t c", t=TT)
                    gx_ = bank[2 * d + 1][:, :].rearrange("p (t c) -> p t c", t=TT)
                    A(Pinc[d][:, :, :], gi, ACT.Exp, scale=-RW_DECAY_SCALE).then_inc(rw_exp.sem, 1)
                    A(Pinv[d][:, :, :], gi, ACT.Exp, scale=RW_DECAY_SCALE).then_inc(rw_exp.sem, 1)
                    A(Pexc[d][:, :, :], gx_, ACT.Exp, scale=-RW_DECAY_SCALE).then_inc(rw_exp.sem, 1)
                    A(lastP[:, d, :], gi[:, :, last_t], ACT.Exp, scale=-RW_DECAY_SCALE)
                    A(firstP[:, d, :], gx_[:, :, first_t], ACT.Exp, scale=RW_DECAY_SCALE).then_inc(rw_exp.sem, 1)
                join(act, "rwkv", it, 2)
                for n, dst in enumerate([Vtok, Btok[0], Btok[1], Ktok[0], Ktok[1]]):
                    act.wait_ge(rw_tp.sem, rw_tp.at(it, n + 1))
                    A(dst.rearrange("p a b -> p (a b)"), bank[n][:, :], ACT.Copy)
                join(act, "rwkv", it, 3)
                join(act, "rwkv", it, 4, idle=True)
                invert(turn_of(l, 0, j))
                scan_u(turn_of(l, 0, j))
                act.wait_ge(rw_fin[0].sem, rw_fin[0].at(it, 1))
                A(tmpB[:, :], bank[5][:, :], ACT.Copy).then_inc(rw_fin[5].sem, 1)
                act.wait_ge(rw_fin[4].sem, rw_fin[4].at(it, 1))
                A(tmpB[:, :], bank[1][:, :], ACT.Sqrt, bias=eps[:, 1:2], scale=1.0 / HD).then_inc(rw_gstd.sem, 1)
                join(act, "rwkv", it, 5)

            def gdn(l, j):
                it = l * PAIRS + j
                act.wait_ge(gd_sel.sem, gd_sel.at(it, 1))
                for m, dst in enumerate((gqT, gkT, gvT)):
                    act.wait_ge(gd_ps.sem, gd_ps.at(it, m + 1))
                    A(dst[:, :], bank[m][:, :], ACT.Copy, scale=clj[:, 3 * m + 1:3 * m + 2]).then_inc(gd_base.sem, 1)
                act.wait_ge(gd_ps.sem, gd_ps.at(it, 4))
                A(zg[:, :], bank[3][:, :], ACT.Silu)
                for m, dst in enumerate((gqT, gkT, gvT)):
                    act.wait_ge(gd_sh.sem, gd_sh.at(it, m + 1))
                    A(dst[:, :], dst[:, :], ACT.Silu).then_inc(gd_silu.sem, 1)
                for n in range(2):
                    act.wait_ge(gd_nrm.sem, gd_nrm.at(it, n + 1))
                    A((gr1, gr2)[n][:, :], bank[4 + n][:, :], ACT.Sqrt, bias=eps[:, 0:1]).then_inc(gd_std.sem, 1)
                join(act, "gdn", it, 1)
                for g in range(4):
                    d, hh = g // 2, g % 2
                    r = slice(hh * HD, hh * HD + HD)
                    act.wait_ge(gd_row.sem, gd_row.at(it, g + 1))
                    A(EG[d][r, :, :].rearrange("p a b -> p (a b)"), bank[g][r, :], ACT.Exp).then_inc(gd_eg.sem, 1)
                for g in range(4):
                    act.wait_ge(gd_dif.sem, gd_dif.at(it, g + 1))
                    A(KE[:, g, :], KEp[:, g, :], ACT.Exp)
                    A(GDT[g][:, :, :], GDT[g][:, :, :], ACT.Exp).then_inc(gd_exp.sem, 1)
                for n, dst in enumerate((GV, GKtok)):
                    act.wait_ge(gd_tp.sem, gd_tp.at(it, n + 1))
                    A(dst.rearrange("p a b -> p (a b)"), bank[4 + n][:, :], ACT.Copy).then_inc(gd_tok.sem, 1)
                join(act, "gdn", it, 2)
                join(act, "gdn", it, 3, idle=True)
                invert(turn_of(l, 1, j))
                act.wait_ge(gd_fin[0].sem, gd_fin[0].at(it, 1))
                A(gs2[:, :], bank[5][:, :], ACT.Copy).then_inc(gd_fin[5].sem, 1)
                act.wait_ge(gd_fin[2].sem, gd_fin[2].at(it, 1))
                A(gr1[:, :], bank[0][:, :], ACT.Sqrt, bias=eps[:, 0:1], scale=1.0 / HD).then_inc(gd_fin[3].sem, 1)
                join(act, "gdn", it, 4)

            def attention(l):
                projections(l, 1, S_XQ, U_XQ)
                for m in range(KT):
                    act.wait_ge(xk_ps.sem, xk_ps.at(l, m + 1))
                    A(kmT[:, m, :], bank[m % 4][:, 0:N_MEM], ACT.Copy).then_inc(xk_done.sem, 1)
                act.wait_ge(xv_ps.sem, xv_ps.at(l, 1))
                for n in range(4):
                    A(vm[:, :, n * 256:(n + 1) * 256], bank[4 + n][:, :].rearrange("p (m c) -> p m c", m=2), ACT.Copy)
                join(act, "attn", l * 2, 1)
                for a in range(XA_HEADS):
                    act.wait_ge(at_mx.sem, at_mx.at(l, a + 1))
                    for t in range(TT):
                        A(prob[:, t, :], bank[t // 2][:, (t % 2) * 256:(t % 2 + 1) * 256], ACT.Exp, bias=nmx[:, t:t + 1],
                          scale=XA_DIM ** -0.5, accum_out=psm[:, t:t + 1]).then_inc(at_e.sem, 1)
                    for m in range(2):
                        act.wait_ge(at_tp.sem, at_tp.at(l, 2 * a + m + 1))
                        A(probT[:, m, :], bank[2 + m][:, :], ACT.Copy).then_inc(at_pt.sem, 1)
                    for b in range(2):
                        act.wait_ge(at_o.sem, at_o.at(l, 2 * a + b + 1))
                        A(oT[:, 2 * a + b, :], bank[4 + b][:, :], ACT.Copy).then_inc(at_od.sem, 1)
                join(act, "attn", l * 2 + 1, 1)
                source_hi(l, A_XO, oT)
                projections(l, 2, S_XO, U_XO)

            act.wait_ge(consts_in.sem, 48)
            act.wait_ge(x_in.sem, 32)
            join(act, "start", 0, 1)
            mem_in = sc[:, 8192:8192 + KT * N_MEM].rearrange("p (a b) -> p a b", a=KT)
            norm(0, mem_in, N_MEM)
            with act.Fori(0, layers, 1) as l:
                join(act, "layer", l, 1)
                norm(l * 4 + 1, x, SEQ, l, A_FFN1)
                ffn(l, 0, S_FFN1, U_FFN_UP, A_FFN1)
                tap(act, 'x_ffn1', x)
                norm(l * 4 + 2, x, SEQ)
                tap(act, 'h_mix', h)
                lora(l)
                hyena_filter(l)
                hyena(l)
                with act.Fori(0, PAIRS, 1) as j:
                    rwkv(l, j)
                with act.Fori(0, PAIRS, 1) as j:
                    gdn(l, j)
                tap(act, 'y', y)
                source_hi(l, A_WOUT, y)
                projections(l, 0, S_WOUT, U_WOUT)
                tap(act, 'x_mix', x)
                norm(l * 4 + 3, x, SEQ, l, A_XQ)
                attention(l)
                tap(act, 'x_xa', x)
                norm(l * 4 + 4, x, SEQ, l, A_FFN2)
                ffn(l, 1, S_FFN2, U_FFN2, A_FFN2)
                tap(act, 'x_ffn2', x)
            norm(4 * layers + 1, x, SEQ)

        @block.vector
        def _(dve):
            tt_, ts_, stt = dve.tensor_tensor, dve.tensor_scalar, dve.scalar_tensor_tensor

            def norm(it, src, dst, gain, n_tok, l=None, source=None):
                dve.wait_ge(n_std.sem, n_std.at(it, 1))
                dve.reciprocal(rstd[:, 0:n_tok], std[:, 0:n_tok])
                dve.drain()
                if source is None:
                    for t in range(KT):
                        stt(dst[:, t, :], src[:, t, :], gain(t), rstd[:, 0:n_tok], ALU.mult, ALU.mult)
                else:
                    for t in range(KT):
                        stt(sq[:, t, :], src[:, t, :], gain(t), rstd[:, 0:n_tok], ALU.mult, ALU.mult).then_inc(as_f.sem, 1)
                        if t:
                            low(l, source, sq, t - 1)
                    low(l, source, sq, KT - 1)
                join(dve, "norm", it, 1)

            def low(l, source, src, t):
                dve.wait_ge(as_hi.sem, as_hi.at(l * SPLIT_SOURCES + source, t + 1))
                tt_(a_lo[:, t, :], src[:, t, :], a_hi[:, t, :].bitcast(F32), ALU.subtract).then_inc(as_lo.sem, 1)

            def unit_lo(l, n, unit, later=0, inner=None):
                dve.wait_ge(ws_hi.sem, ws_hi.at(l, n + 1) + later * 2)
                if inner is not None:
                    tt_(u_lo[n % 2], inner, u_hi[n % 2].bitcast(F32), ALU.subtract)
                tt_(w_lo[n % 2], ring[unit % 2][:, :], w_hi[n % 2].bitcast(F32), ALU.subtract)
                dve.drain().then_inc(free.sem, 1)
                dve.sem_inc(ws_lo.sem, 1)

            def layer_gain(n):
                return lambda t: cl[:, C_NORM + n * KT + t:C_NORM + n * KT + t + 1]

            def ffn(l, which, n0, unit):
                unit_lo(l, n0, unit)
                unit_lo(l, n0 + 1, unit + 1)

                def gated(it, s, dst):
                    dve.wait_ge(f_sil.sem, f_sil.at(it, s + 1))
                    tt_(dst, sil[s], bank[2 * s + 1][:, :], ALU.mult).then_inc(f_u.sem, 1)

                with dve.Fori(0, FB // 2 - 1, 1) as j:
                    for s in range(2):
                        gated((l * 2 + which) * (FB // 2) + j, s, u[:, bass.ds(j * 2 + s, 1), :].rearrange("p a n -> p (a n)"))
                        unit_lo(l, n0 + s + 2, unit + s + 2, j)
                for s in range(2):
                    gated((l * 2 + which) * (FB // 2) + (FB // 2 - 1), s, u[:, FB - 2 + s, :])
                    unit_lo(l, n0 + FB + s, unit + FB + s, inner=u[:, 2 * s:2 * s + 2, :])
                n0, unit = n0 + FB, unit + FB
                with dve.Fori(0, 4, 1) as j:
                    for s in range(2):
                        unit_lo(l, n0 + 2 + s, unit + 2 + s, j, u[:, bass.ds(j * 4 + (2 * s + 4), 2), :])
                unit_lo(l, n0 + 10, unit + 10, inner=u[:, 20:22, :])
                for m in range(KT):
                    dve.wait_ge(f_dn.sem, f_dn.at(l * 2 + which, m + 1))
                    stt(x[:, m, :], bank[m][:, :], 0.5, x[:, m, :], ALU.mult, ALU.add)
                join(dve, "ffn", l * 2 + which, 1)

            def taps(dst, ps, prev, nxt):
                stt(dst[:, 1:SEQ], ps[:, 0:SEQ - 1], prev, dst[:, 1:SEQ], ALU.mult, ALU.add)
                dve.drain()
                return stt(dst[:, 0:SEQ - 1], ps[:, 1:SEQ], nxt, dst[:, 0:SEQ - 1], ALU.mult, ALU.add)

            def lora(l):
                ts_(lora_c0[:, :], cl[:, C_LMU:C_LMU + 3], -1.0, 1.0, ALU.mult, ALU.add)
                dve.drain()
                tt_(lora_c0[:, :], lora_c0[:, :], cl[:, C_LMU + 3:C_LMU + 6], ALU.subtract).then_inc(ga_a.sem, 1)
                for m, dst in enumerate((lwT, laT, lgT)):
                    dve.wait_ge(lo_base.sem, lo_base.at(l, m + 1))
                    taps(dst, bank[m], cl[:, C_LMU + m:C_LMU + m + 1], cl[:, C_LMU + 3 + m:C_LMU + 4 + m]).then_inc(lo_done.sem, 1)
                dve.wait_ge(lo_ps.sem, lo_ps.at(l, 4))
                tt_(gx[:, :, :], bank[3][:, 0:TT * 24].rearrange("p (t c) -> p t c", t=TT)[:, :, 0:12],
                    over(cl[:, C_DT:C_DT + 12], TT), ALU.add)
                dve.drain()
                stt(ge[:, :, :], gx[:, :, :], -1.0, gx[:, :, :], ALU.mult, ALU.max).then_inc(ga_b.sem, 1)
                dve.wait_ge(ga_c.sem, ga_c.at(l, 1))
                stt(gtok[:, :, :], gx[:, :, :], 0.0, gl[:, :, :], ALU.max, ALU.add)
                dve.drain()
                stt(gtok[:, :, :], gtok[:, :, :], -1.0, over(nega[:, :], TT), ALU.mult, ALU.mult).then_inc(ga_e.sem, 1)
                join(dve, "lora", l, 1)

            def hyena_filter(l):
                for n in range(2):
                    dve.wait_ge(fl_ps.sem, fl_ps.at(l, n + 1))
                    q = slice(0, HY_FFN)
                    ts_(filt_arg[q, :], bank[n][q, :], cl[q, C_FILT + 1 + n:C_FILT + 2 + n], cl[q, C_FILT:C_FILT + 1], ALU.add, ALU.mult)
                    dve.drain()
                    ts_(filt_k[q, :], filt_arg[q, :], 0.15915494309189535, ROUND_MAGIC, ALU.mult, ALU.add)
                    dve.drain()
                    ts_(filt_k[q, :], filt_k[q, :], ROUND_MAGIC, None, ALU.subtract)
                    dve.drain()
                    stt(filt_arg[q, :], filt_k[q, :], -TWO_PI_HI, filt_arg[q, :], ALU.mult, ALU.add)
                    dve.drain()
                    stt(filt_arg[q, :], filt_k[q, :], -TWO_PI_LO, filt_arg[q, :], ALU.mult, ALU.add)
                    dve.drain()
                    ts_(filt_arg[q, :], filt_arg[q, :], PI_BELOW, -PI_BELOW, ALU.min, ALU.max).then_inc(fl_arg.sem, 1)
                for t in range(TT):
                    dve.wait_ge(fl_e.sem, fl_e.at(l, t + 1))
                    dve.wait_ge(fl_out.sem, fl_out.at(l, t + 1))
                    last = tt_(filt[:, t, :], bank[2 + t][:, :], filt_e[:, t, :], ALU.mult)
                    if t == 0:
                        dve.drain()
                        last = dve.memset(filt[0:1, 0, 256:512], 0.0)
                    last.then_inc(fl_k.sem, 1)
                dve.wait_ge(fl_s.sem, fl_s.at(l, 1))
                tt_(filt_rn[:, :], filt_sum[:, 0:256], filt_sum[:, 256:512], ALU.add)
                tt_(kplus[:, :, :], filt[:, :, 0:256], filt[:, :, 256:512], ALU.add)
                tt_(kminus[:, :, :], filt[:, :, 0:256], filt[:, :, 256:512], ALU.subtract)
                dve.drain()
                dve.reciprocal(filt_rn[:, :], filt_rn[:, :])
                dve.drain()
                for k_ in (kplus, kminus):
                    stt(k_[:, :, :], k_[:, :, :], 1.0 / SEQ, over(filt_rn[:, :], TT), ALU.mult, ALU.mult)
                join(dve, "filter", l, 1)

            def hyena(l):
                for c in range(HY_C):
                    col = C_HY + 13 * c
                    for m, dst in enumerate((hx0[c], hx1, hv)):
                        dve.wait_ge(hy_base.sem, hy_base.at(l, 3 * c + m + 1))
                        taps(dst, bank[4 * c + m], cl[:, col + 3 * m:col + 3 * m + 1], cl[:, col + 3 * m + 2:col + 3 * m + 3])
                    dve.drain()
                    tt_(hu[c][:, :], hx1[:, :], hv[:, :], ALU.mult).then_inc(hy_cv.sem, 1)
                join(dve, "hyena", l, 1)
                dve.wait_ge(sp_sb.sem, sp_sb.at(l, 8))
                u_re, u_im = spec[:, 0:4, 0:256], spec[:, 4:8, 0:256]
                k_re, k_im = spec[:, 0:4, 256:512], spec[:, 4:8, 256:512]
                tt_(prA[:, :, :], u_re, k_re, ALU.mult)
                tt_(prT[:, :, :], u_im, k_im, ALU.mult)
                dve.drain()
                tt_(prA[:, :, :], prA[:, :, :], prT[:, :, :], ALU.subtract).then_inc(sp_pr.sem, 1)
                tt_(prB[:, :, :], u_re, k_im, ALU.mult)
                dve.drain()
                tt_(prT[:, :, :], u_im, k_re, ALU.mult)
                dve.drain()
                tt_(prB[:, :, :], prB[:, :, :], prT[:, :, :], ALU.add).then_inc(sp_pr.sem, 1)
                dve.drain()
                for c in range(HY_C):
                    dve.wait_ge(sp_y.sem, sp_y.at(l, c + 1))
                    stt(hyo[c], hu[c][:, :], cl[:, C_HY + 13 * c + 12:C_HY + 13 * c + 13], bank[c][:, :], ALU.mult, ALU.add)
                    dve.drain()
                    tt_(y[:, c, :], hyo[c], hx0[c][:, :], ALU.mult)
                join(dve, "dft", l, 1)

            def invert(turn):
                s = iv
                for g in range(4):
                    dve.wait_ge(s["half"].sem, s["half"].at(turn, g + 1))
                    tt_(XT[g][:, :, :], Y[g][:, :, :], over(ident, TT), ALU.add).then_inc(s["xt"].sem, 1)
                for m in range(LEVELS - 1):
                    for g in range(4):
                        dve.wait_ge(s["yps"].sem, s["yps"].at(turn, 4 * m + g + 1))
                        tt_(Y[g][:, :, :], bank[g][:, :].rearrange("p (a b) -> p a b", a=TT), over(level_mask(m + 1, g // 2), TT),
                            ALU.mult).then_inc(s["y"].sem, 1)
                    for g in range(4):
                        dve.wait_ge(s["xtps"].sem, s["xtps"].at(turn, 4 * m + g + 1))
                        tt_(XT[g][:, :, :], bank[4 + g][:, :].rearrange("p (a b) -> p a b", a=TT), XT[g][:, :, :],
                            ALU.add).then_inc(s["xt"].sem, 1)

            def rwkv(l, j):
                it = l * PAIRS + j
                dve.wait_ge(rw_cols.sem, rw_cols.at(it, 1))
                for m, dst in enumerate((rT, kT, vT)):
                    dve.wait_ge(rw_base.sem, rw_base.at(it, m + 1))
                    taps(dst, bank[m], clj[:, m:m + 1], clj[:, 3 + m:4 + m])
                small = ring[1 - U_RWKV % 2][:, KT * P:2 * KT * P]
                for d in range(2):
                    dve.wait_ge(rw_ps.sem, rw_ps.at(it, 7 + d))
                    tt_(sg[d][:, :, :], bank[6 + d][:, :].rearrange("p (a b) -> p a b", a=TT),
                        over(small[:, 384 + d * P:384 + (d + 1) * P], TT), ALU.add).then_inc(rw_w0.sem, 1)
                dve.drain()
                ts_(kkr[:, :], kT[:, :], clj[:, 8:9], None, ALU.mult)
                join(dve, "rwkv", it, 1)
                tt_(tmpA[:, :], kkr[:, :], kkr[:, :], ALU.mult).then_inc(rw_kk2.sem, 1)
                stt(rk[:, :], rT[:, :], clj[:, 10:11], kT[:, :], ALU.mult, ALU.mult).then_inc(rw_rk.sem, 1)
                dve.wait_ge(rw_std.sem, rw_std.at(it, 1))
                dve.reciprocal(tmpB[:, :], tmpB[:, :])
                dve.drain()
                tt_(kk[:, :], kkr[:, :], tmpB[:, :], ALU.mult)
                dve.drain()
                ts_(nkk[:, :], kk[:, :], -1.0, None, ALU.mult)
                dve.drain()
                dve.wait_ge(rw_bon.sem, rw_bon.at(it, 1))
                tt_(bv[:, :], bank[5][:, :], vT[:, :], ALU.mult)
                for d in range(2):
                    dve.wait_ge(rw_exp.sem, rw_exp.at(it, 4 * d + 4))
                    pi, pv, px = (v[d].rearrange("p a b -> p (a b)") for v in (Pinc, Pinv, Pexc))
                    tt_(AR[d][:, :, 0, :], nkk[:, :].rearrange("p (a b) -> p a b", a=TT), Pexc[d][:, :, :], ALU.mult)
                    tt_(AR[d][:, :, 1, :], rT[:, :].rearrange("p (a b) -> p a b", a=TT), Pinc[d][:, :, :], ALU.mult)
                    dve.wait_ge(rw_kd.sem, rw_kd.at(it, d + 1))
                    tt_(BTt[d][:, :], aP[d][:, :], kk[:, :], ALU.mult)
                    tt_(KTt[d][:, :], kd[d][:, :], pv, ALU.mult)
                tt_(fac[:, 0, 0:3], lastP[:, 0, 0:3], firstP[:, 0, 1:4], ALU.mult)
                tt_(fac[:, 1, 0:3], lastP[:, 1, 1:4], firstP[:, 1, 0:3], ALU.mult)
                join(dve, "rwkv", it, 2)
                join(dve, "rwkv", it, 3, idle=True)
                for g in range(4):
                    d = g // 2
                    for n in range(4):
                        dve.wait_ge(rw_scp.sem, rw_scp.at(it, 4 * g + n + 1))
                        dst = (SCB, SCK)[n // 2][g][:, 2 * (n % 2):2 * (n % 2) + 2, :, :].rearrange("p t a b -> p t (a b)")
                        tt_(dst, bank[4 * (g % 2) + n][:, :].rearrange("p (t c) -> p t c", t=2), over(strict_incl[d], 2),
                            ALU.mult).then_inc(rw_scs.sem, 1)
                for d in range(2):
                    dve.memset(Z[d][:, :], 0.0)
                join(dve, "rwkv", it, 4)
                invert(turn_of(l, 0, j))
                s = scan_sig
                dve.drain().then_inc(s["z0"].sem, 1)
                for c in range(TT):
                    for d in range(2):
                        dve.wait_ge(s["tps"][d].sem, s["tps"][d].at(turn_of(l, 0, j), c + 1))
                        dve.tensor_copy(Tt[d][:, :].rearrange("p (a b) -> p a b", a=2), psum[:, 2 * d:2 * d + 2, 0:HD]).then_inc(s["t"][d].sem, 1)
                    for d in range(2):
                        if c < TT - 1:
                            f = fac[:, d, c:c + 1] if d == 0 else fac[:, d, TT - 2 - c:TT - 1 - c]
                            dve.wait_ge(s["zps"][d].sem, s["zps"][d].at(turn_of(l, 0, j), c + 1))
                            tt_(Z[d][:, :], Z[d][:, :], bank[6 + d][:, P:P + HD], ALU.add)
                            dve.drain()
                            ts_(Z[d][:, :], Z[d][:, :], f, None, ALU.mult).then_inc(s["z"][d].sem, 1)
                dve.wait_ge(rw_fin[5].sem, rw_fin[5].at(it, 1))
                tt_(yo[:, :], bank[4][:, :], tmpB[:, :], ALU.add).then_inc(rw_fin[1].sem, 1)
                dve.wait_ge(rw_fin[2].sem, rw_fin[2].at(it, 1))
                stt(yo[:, :], bank[0][:, :], -1.0 / HD, yo[:, :], ALU.mult, ALU.add)
                dve.drain()
                tt_(tmpA[:, :], yo[:, :], yo[:, :], ALU.mult).then_inc(rw_fin[3].sem, 1)
                dve.wait_ge(rw_gstd.sem, rw_gstd.at(it, 1))
                dve.reciprocal(tmpB[:, :], tmpB[:, :])
                dve.drain()
                stt(yo[:, :], yo[:, :], clj[:, 11:12], tmpB[:, :], ALU.mult, ALU.mult)
                dve.drain()
                stt(yo[:, :], yo[:, :], clj[:, 12:13], bv[:, :], ALU.add, ALU.add)
                dve.drain()
                tt_(y[:, bass.ds(j + HY_C, 1), :].rearrange("p a n -> p (a n)"), yo[:, :], gateT[:, :], ALU.mult)
                join(dve, "rwkv", it, 5)

            def gdn(l, j):
                it = l * PAIRS + j
                dve.wait_ge(gd_sel.sem, gd_sel.at(it, 1))
                for m, dst in enumerate((gqT, gkT, gvT)):
                    dve.wait_ge(gd_base.sem, gd_base.at(it, m + 1))
                    taps(dst, bank[m], clj[:, 3 * m:3 * m + 1], clj[:, 3 * m + 2:3 * m + 3]).then_inc(gd_sh.sem, 1)
                for n, (dst, r_, f) in enumerate(((gqT, gr1, HD ** -0.5), (gkT, gr2, 1.0))):
                    dve.wait_ge(gd_std.sem, gd_std.at(it, n + 1))
                    dve.reciprocal(r_[:, :], r_[:, :])
                    dve.drain()
                    stt(dst[:, :], dst[:, :], f, r_[:, :], ALU.mult, ALU.mult)
                join(dve, "gdn", it, 1)
                for g in range(4):
                    last_t = P - 1 if g < 2 else 0
                    dve.wait_ge(gd_eg.sem, gd_eg.at(it, g + 1))
                    row = bank[g][:, :].rearrange("p (t c) -> p t c", t=TT)
                    for t in range(TT):
                        ts_(GDT[g][:, t, :], row[:, t, :], gcj[:, t, g:g + 1], 0.0, ALU.subtract, ALU.min)
                    tt_(KEp[:, g, :], row[:, :, last_t], gcj[:, :, g], ALU.subtract).then_inc(gd_dif.sem, 1)
                join(dve, "gdn", it, 2)
                for g in range(4):
                    hh = g % 2
                    dve.wait_ge(gd_kk.sem, gd_kk.at(it, hh + 1))
                    dve.wait_ge(gd_msk.sem, gd_msk.at(it, g + 1))
                    for t in range(TT):
                        stt(GL[g][:, t, :], bank[hh][:, t * P:(t + 1) * P], nbj[:, t, g:g + 1], GDT[g][:, t, :], ALU.mult, ALU.mult)
                    dve.wait_ge(gd_kk.sem, gd_kk.at(it, hh + 3))
                    tt_(GAT[g][:, :, :], bank[2 + hh][:, :].rearrange("p (t c) -> p t c", t=TT), GDT[g][:, :, :], ALU.mult)
                for d in range(2):
                    dve.memset(GZ[d][:, :], 0.0)
                join(dve, "gdn", it, 3)
                invert(turn_of(l, 1, j))
                s = scan_sig
                dve.drain().then_inc(s["z0"].sem, 1)
                for c in range(TT):
                    for d in range(2):
                        t = c if d == 0 else TT - 1 - c
                        dve.wait_ge(s["tps"][d].sem, s["tps"][d].at(turn_of(l, 1, j), c + 1))
                        tt_(GT[d][:, :].rearrange("p (a b) -> p a b", a=2), GV[:, t, :].rearrange("p (a b) -> p a b", a=2),
                            psum[:, 2 * d:2 * d + 2, 0:HD], ALU.subtract).then_inc(s["t"][d].sem, 1)
                    for d in range(2):
                        t = c if d == 0 else TT - 1 - c
                        dve.wait_ge(s["ups"][d].sem, s["ups"][d].at(turn_of(l, 1, j), c + 1))
                        tt_(GU[d][:, :].rearrange("p (a b) -> p a b", a=2), bank[6 + d][:, 0:P].rearrange("p (a b) -> p a b", a=2),
                            btj[:, t, 2 * d:2 * d + 2].unsqueeze(2).broadcast_to([P, 2, HD]), ALU.mult).then_inc(s["u"][d].sem, 1)
                    for d in range(2):
                        if c < TT - 1:
                            t = c if d == 0 else TT - 1 - c
                            last_t = P - 1 if d == 0 else 0
                            dve.wait_ge(s["zps"][d].sem, s["zps"][d].at(turn_of(l, 1, j), c + 1))
                            stt(GZ[d][:, :], GZ[d][:, :], EG[d][:, t, last_t:last_t + 1], bank[6 + d][:, P:P + HD],
                                ALU.mult, ALU.add).then_inc(s["z"][d].sem, 1)
                dve.wait_ge(gd_fin[5].sem, gd_fin[5].at(it, 1))
                tt_(go[:, :], bank[4][:, :], gs2[:, :], ALU.add)
                dve.drain()
                tt_(gs1[:, :], go[:, :], go[:, :], ALU.mult).then_inc(gd_fin[1].sem, 1)
                dve.wait_ge(gd_fin[3].sem, gd_fin[3].at(it, 1))
                dve.reciprocal(gr1[:, :], gr1[:, :])
                dve.drain()
                stt(go[:, :], go[:, :], cl[:, C_GNW:C_GNW + 1], gr1[:, :], ALU.mult, ALU.mult)
                dve.drain()
                tt_(y[:, bass.ds(j + HY_C + PAIRS, 1), :].rearrange("p a n -> p (a n)"), go[:, :], zg[:, :], ALU.mult)
                join(dve, "gdn", it, 4)

            def projections(l, which, n0, unit):
                def blocks(n):
                    for m in range(2 * n, 2 * n + 2):
                        if m % 2 == 0:
                            dve.wait_ge(ws_done.sem, ws_done.at(l, n0 + n + 3))
                        if which == 1:
                            ts_(qT[:, m, :], bank[m % 4][:, :], 1.0, None, ALU.mult).then_inc(pj_done.sem, 1)
                        else:
                            tt_(x[:, m, :], bank[m % 4][:, :], x[:, m, :], ALU.add).then_inc(pj_done.sem, 1)

                for n in range(KT // 2):
                    if n >= 2:
                        blocks(n - 2)
                    unit_lo(l, n0 + n, unit + n)
                blocks(KT // 2 - 2)
                blocks(KT // 2 - 1)
                join(dve, "proj", l * 3 + which, 1)

            def attention(l):
                projections(l, 1, S_XQ, U_XQ)
                join(dve, "attn", l * 2, 1)
                for a in range(XA_HEADS):
                    dve.wait_ge(at_s.sem, at_s.at(l, TT * (a + 1)))
                    for b in range(2):
                        dve.tensor_reduce(nmx[:, 2 * b:2 * b + 2], bank[b][:, :].rearrange("p (t c) -> p t c", t=2),
                                          mybir.AxisListType.X, ALU.max)
                    dve.drain()
                    ts_(nmx[:, :], nmx[:, :], -(XA_DIM ** -0.5), None, ALU.mult).then_inc(at_mx.sem, 1)
                    dve.wait_ge(at_e.sem, at_e.at(l, TT * (a + 1)))
                    dve.reciprocal(rsm[:, :], psm[:, :])
                    dve.drain()
                    for t in range(TT):
                        last = ts_(prob[:, t, :], prob[:, t, :], rsm[:, t:t + 1], None, ALU.mult)
                    last.then_inc(at_n.sem, 1)
                join(dve, "attn", l * 2 + 1, 1)
                for t in range(KT):
                    low(l, A_XO, oT, t)
                projections(l, 2, S_XO, U_XO)

            dve.sem_inc(f_u.sem, 2)
            dve.sem_inc(pj_done.sem, 4)
            dve.wait_ge(consts_in.sem, 48)
            join(dve, "start", 0, 1)
            mem_in = sc[:, 8192:8192 + KT * N_MEM].rearrange("p (a b) -> p a b", a=KT)
            norm(0, mem_in, memn, lambda t: gc[:, C_MEM + t:C_MEM + t + 1], N_MEM)
            with dve.Fori(0, layers, 1) as l:
                join(dve, "layer", l, 1)
                norm(l * 4 + 1, x, h, layer_gain(0), SEQ, l, A_FFN1)
                ffn(l, 0, S_FFN1, U_FFN_UP)
                norm(l * 4 + 2, x, h, layer_gain(1), SEQ)
                lora(l)
                hyena_filter(l)
                hyena(l)
                with dve.Fori(0, PAIRS, 1) as j:
                    rwkv(l, j)
                with dve.Fori(0, PAIRS, 1) as j:
                    gdn(l, j)
                for t in range(KT):
                    low(l, A_WOUT, y, t)
                projections(l, 0, S_WOUT, U_WOUT)
                norm(l * 4 + 3, x, h, layer_gain(2), SEQ, l, A_XQ)
                attention(l)
                norm(l * 4 + 4, x, h, layer_gain(3), SEQ, l, A_FFN2)
                ffn(l, 1, S_FFN2, U_FFN2)
                if UNITS > U_PAD:
                    dve.wait_ge(full[U_PAD % 2].sem, landed(l, U_PAD))
                    dve.sem_inc(free.sem, 1)
            norm(4 * layers + 1, x, h, lambda t: gc[:, C_FINAL + t:C_FINAL + t + 1], SEQ)

        @block.gpsimd
        def _(pool):
            tt_, ts_ = pool.tensor_tensor, pool.tensor_scalar

            def invert_start(turn, LT):
                for g in range(4):
                    tt_(Y[g][:, :, :], LT[g], over(level_mask(0, 1 - g // 2), TT), ALU.mult).then_inc(iv["half"].sem, 1)

            def rwkv(l, j):
                it = l * PAIRS + j
                pool.tensor_copy(clj[:, 0:RWC], cl[:, bass.ds(j * RWC + C_RW, RWC)])
                pool.drain()
                tt_(rwc[:, 0:3], clj[:, 0:3], clj[:, 3:6], ALU.add)
                ts_(rwc[:, 3:4], clj[:, 9:10], -1.0, 1.0, ALU.mult, ALU.add)
                pool.drain()
                ts_(rwc[:, 0:3], rwc[:, 0:3], -1.0, 1.0, ALU.mult, ALU.add).then_inc(rw_cols.sem, 1)
                join(pool, "rwkv", it, 1)
                for d in range(2):
                    tt_(kd[d][:, :], kd[d][:, :], kT[:, :], ALU.mult)
                    pool.wait_ge(rw_exp.sem, rw_exp.at(it, 4 * d + 2))
                    tt_(aP[d][:, :], aT[d][:, :], Pinv[d].rearrange("p a b -> p (a b)"), ALU.mult)
                    pool.drain().then_inc(rw_kd.sem, 1)
                join(pool, "rwkv", it, 2)
                join(pool, "rwkv", it, 3, idle=True)
                join(pool, "rwkv", it, 4, idle=True)
                invert_start(turn_of(l, 0, j), [SCB[g][:, :, 0, :] for g in range(4)])
                join(pool, "rwkv", it, 5)

            def gdn(l, j):
                it = l * PAIRS + j
                pool.tensor_copy(clj[:, 0:GDC], cl[:, bass.ds(j * GDC + C_GD, GDC)])
                pool.tensor_copy(selj[0:12, :, :].rearrange("p a b -> p (a b)"), kon[0:12, bass.ds(j * (4 * P) + K_SEL, 4 * P)])
                for dst, src in ((gcj, gsum), (btj, beta)):
                    for d in range(2):
                        pool.tensor_copy(dst[:, :, 2 * d:2 * d + 2], src[:, :, bass.ds(j * 2 + d * HEADS, 2)])
                pool.drain()
                ts_(nbj[:, :, :], btj[:, :, :], -1.0, 0.0, ALU.mult, ALU.add)
                pool.drain().then_inc(gd_sel.sem, 1)
                for n, (dst, src) in enumerate(((gs1, gqT), (gs2, gkT))):
                    pool.wait_ge(gd_silu.sem, gd_silu.at(it, n + 1))
                    tt_(dst[:, :], src[:, :], src[:, :], ALU.mult).then_inc(gd_sq.sem, 1)
                join(pool, "gdn", it, 1)
                for d in range(2):
                    pool.wait_ge(gd_eg.sem, gd_eg.at(it, 2 * d + 2))
                    tt_(GA[d].rearrange("p a b -> p (a b)"), gkT[:, :], EG[d].rearrange("p a b -> p (a b)"), ALU.mult)
                    tt_(GR[d].rearrange("p a b -> p (a b)"), gqT[:, :], EG[d].rearrange("p a b -> p (a b)"), ALU.mult)
                for g in range(4):
                    pool.wait_ge(gd_exp.sem, gd_exp.at(it, g + 1))
                    tt_(GDT[g][:, :, :], GDT[g][:, :, :], over(incl[g // 2], TT), ALU.mult).then_inc(gd_msk.sem, 1)
                pool.wait_ge(gd_tok.sem, gd_tok.at(it, 2))
                for d in range(2):
                    for hh in range(2):
                        tt_(Kend[d][:, :, hh, :], GKtok[:, :, hh * HD:hh * HD + HD],
                            KE[:, 2 * d + hh, :].unsqueeze(2).broadcast_to([P, TT, HD]), ALU.mult)
                join(pool, "gdn", it, 2)
                join(pool, "gdn", it, 3, idle=True)
                invert_start(turn_of(l, 1, j), [GL[g][:, :, :] for g in range(4)])
                join(pool, "gdn", it, 4)

            pool.memset(eps[:, 0:1], NORM_EPS)
            pool.memset(eps[:, 1:2], RW_GN_EPS)
            pool.wait_ge(consts_in.sem, 48)
            join(pool, "start", 0, 1)
            join(pool, "norm", 0, 1, idle=True)
            with pool.Fori(0, layers, 1) as l:
                pool.tensor_copy(cl[:, :], cols_all[:, bass.ds(l, 1), :].rearrange("p a n -> p (a n)"))
                join(pool, "layer", l, 1)
                join(pool, "norm", l * 4 + 1, 1, idle=True)
                for which in range(2):
                    if which:
                        join(pool, "norm", l * 4 + 2, 1)
                        join(pool, "lora", l, 1, idle=True)
                        join(pool, "filter", l, 1, idle=True)
                        join(pool, "hyena", l, 1, idle=True)
                        join(pool, "dft", l, 1, idle=True)
                        with pool.Fori(0, PAIRS, 1) as j:
                            rwkv(l, j)
                        with pool.Fori(0, PAIRS, 1) as j:
                            gdn(l, j)
                        join(pool, "proj", l * 3, 1)
                        join(pool, "norm", l * 4 + 3, 1, idle=True)
                        join(pool, "proj", l * 3 + 1, 1, idle=True)
                        join(pool, "attn", l * 2, 1, idle=True)
                        join(pool, "attn", l * 2 + 1, 1, idle=True)
                        join(pool, "proj", l * 3 + 2, 1, idle=True)
                        join(pool, "norm", l * 4 + 4, 1, idle=True)
                    join(pool, "ffn", l * 2 + which, 1, idle=True)
            join(pool, "norm", 4 * layers + 1, 1, idle=True)


def tiles_of(w):
    n = w.shape[1] // P
    return w.reshape(KT, P, n, P).transpose(2, 1, 0, 3).reshape(n, P, KT * P)


def weight_units(a, l):
    out = np.zeros((UNITS, P, UNIT), np.float32)
    half = KT * P
    for which, base in ((1, U_FFN_UP), (2, U_FFN2)):
        out[base:base + FB, :, :half] = tiles_of(a[f"ffn{which}_w1"][l])
        out[base:base + FB, :, half:] = tiles_of(a[f"ffn{which}_w3"][l])
        w2 = a[f"ffn{which}_w2"][l].reshape(FB // 2, 2, P, D_MODEL)
        out[base + FB:base + N_FFN] = w2.transpose(0, 2, 1, 3).reshape(FB // 2, P, UNIT)
    w = a["w_in"][l]
    hy, rw, gd = 0, 768, 768 + 1536
    b = [tiles_of(w[:, s:s + n * P]) for s, n in ((hy, 6), (rw, 12), (gd, 12))]
    for m in range(2):
        out[U_LORA, :, m * half:(m + 1) * half] = b[1][9 + m]
    out[U_LORA + 1, :, :half] = b[1][11]
    out[U_LORA + 1, :, half:half + KT * 24] = w[:, -24:].reshape(KT, P, 24).transpose(1, 0, 2).reshape(P, KT * 24)
    f = out[U_FILTER]
    f[:HY_FFN, :512] = a["hy_w3"][l]
    f[:HY_EMB, 512:576] = a["hy_w1"][l]
    f[:HY_FFN, 576:640] = a["hy_w2"][l]
    f[:, 640:1152] = a["hy_decay"][l][None, :]
    f[:HY_EMB, 1152:1152 + SEQ] = positional_features().T
    for c in range(HY_C):
        for m in range(3):
            out[U_HYENA + 2 * c + m // 2, :, (m % 2) * half:(m % 2 + 1) * half] = b[0][2 * m + c]
    out[U_DFT:U_DFT + 4] = dft_units()
    for j in range(PAIRS):
        for m in range(3):
            out[U_RWKV + 2 * j + m // 2, :, (m % 2) * half:(m % 2 + 1) * half] = b[1][3 * m + j]
        s, q = out[U_RWKV + 2 * j + 1, :, half:], slice(j * P, (j + 1) * P)
        s[:, 0:128] = a["rw_w_lora"][l].reshape(P, -1)[:, q]
        s[:, 128:256] = a["rw_a_lora"][l].reshape(P, -1)[:, q]
        s[:, 256:384] = a["rw_g_lora"][l][:, q]
        s[:, 384:512] = a["rw_w0"][l, 0, q][None, :]
        s[:, 512:640] = a["rw_w0"][l, 1, q][None, :]
        for m in range(4):
            out[U_GDN + 2 * j + m // 2, :, (m % 2) * half:(m % 2 + 1) * half] = b[2][3 * m + j]
    for name, base in (("w_out", U_WOUT), ("xa_wq", U_XQ), ("xa_wk", U_XK), ("xa_wo", U_XO)):
        t = tiles_of(a[name][l]).reshape(KT // 2, 2, P, half)
        out[base:base + KT // 2] = t.transpose(0, 2, 1, 3).reshape(KT // 2, P, UNIT)
    out[U_XV:U_XV + 4] = a["xa_wv"][l].reshape(KT, P, 4, 256).transpose(2, 1, 0, 3).reshape(4, P, UNIT)
    return out


def column_params(a, l):
    c = np.zeros((P, N_COLS), np.float32)

    def put(at, v):
        v = np.asarray(v).reshape(-1, P)
        c[:, at:at + v.shape[0]] = v.T

    for n, name in enumerate(("norm_ffn1", "norm_mix", "norm_xattn", "norm_ffn2")):
        put(C_NORM + n * KT, a[name][l])
    for t in range(HY_C):
        for m in range(3):
            q = slice(m * 256 + t * P, m * 256 + (t + 1) * P)
            for tap in range(3):
                put(C_HY + 13 * t + 3 * m + tap, a["hy_conv_w"][l, tap, q])
            put(C_HY + 13 * t + 9 + m, a["hy_conv_b"][l, q])
        put(C_HY + 13 * t + 12, a["hy_bias"][l, t * P:(t + 1) * P])
    for n, name in enumerate(("hy_freq", "hy_b1", "hy_b2")):
        c[:HY_FFN, C_FILT + n] = a[name][l]
    for e, name in enumerate(("rw_mu_prev", "rw_mu_next")):
        put(C_LMU + 3 * e, a[name][l, 9 * P:])
        for j in range(PAIRS):
            for m in range(3):
                put(C_RW + RWC * j + 3 * e + m, a[name][l, (3 * m + j) * P:(3 * m + j + 1) * P])
    c[:, C_GNW] = np.concatenate([a["gdn_norm_w"][l]] * 2)
    c[:, C_DT:C_DT + 12] = a["gdn_dt_bias"][l].reshape(1, 12)
    c[:, C_ALOG:C_ALOG + 12] = a["gdn_a_log"][l].reshape(1, 12)
    for j in range(PAIRS):
        q = slice(j * P, (j + 1) * P)
        at = C_RW + RWC * j
        for d in range(2):
            put(at + 6 + d, a["rw_a0"][l, d, q])
        for n, name in enumerate(("rw_k_k", "rw_k_a", "rw_r_k", "rw_gn_w", "rw_gn_b")):
            put(at + 8 + n, a[name][l, q])
        for m in range(3):
            for tap in range(3):
                put(C_GD + GDC * j + 3 * m + tap, a["gdn_conv_w"][l, tap, m * 384 + j * P:m * 384 + (j + 1) * P])
    return c


def feature_tiles(v):
    return np.ascontiguousarray(v.T.reshape(KT, P, -1).transpose(1, 0, 2))


def host_arrays(a):
    units = np.concatenate([weight_units(a, l) for l in range(DEPTH)])
    cols = np.stack([column_params(a, l) for l in range(DEPTH)], axis=1)
    gcols = np.concatenate([a["mem_norm"].reshape(KT, P).T, a["norm_final"].reshape(KT, P).T], axis=1)
    return {"xT": feature_tiles(a["x"][0]), "memT": feature_tiles(a["mem"][0]), "units": units, "cols": cols,
            "gcols": np.ascontiguousarray(gcols), "consts": shape_constants()}


def kernel(**inputs):
    import concourse.bacc as _bacc
    from concourse.bass_utils import run_bass_kernel_spmd as _run

    arrays = host_arrays({k: np.asarray(v) for k, v in inputs.items()})
    nc = _bacc.Bacc("TRN2", target_bir_lowering=False, num_devices=1)
    args = [nc.dram_tensor(n, v.shape, F32, kind="ExternalInput").ap() for n, v in arrays.items()]
    out = nc.dram_tensor("out", (P, KT, SEQ), F32, kind="ExternalOutput").ap()
    trunk_program(nc, *args, out)
    r = _run(nc, [arrays], core_ids=[0])
    o = r.results[0]["out"]
    return o.transpose(1, 0, 2).reshape(1, D_MODEL, SEQ).transpose(0, 2, 1)
```

```python
from contextlib import ExitStack

import numpy as np
import concourse.bass as bass
from concourse import mybir

F32 = mybir.dt.float32
F32R = mybir.dt.float32r
ALU = mybir.AluOpType
ACT = mybir.ActivationFunctionType

P = 128
D_MODEL, SEQ, DEPTH, N_MEM, D_FF = 1024, 512, 2, 256, 2816
KT = D_MODEL // P
TT = SEQ // P
FB = D_FF // P
HY_C = 2
PAIRS = 3
HD = 64
HY_FFN, HY_EMB = 64, 33
HEADS = 6
RW_DECAY_SCALE = 0.606531
NORM_EPS, RW_GN_EPS = 1e-6, 64e-5
XA_HEADS, XA_DIM = 4, 256
LEVELS = 7
ROUND_MAGIC = 1.5 * 2.0 ** 23
TWO_PI_HI = 6.28125
TWO_PI_LO = 6.283185307179586 - TWO_PI_HI
PI_BELOW = 3.1415925

UNIT = 2048
U_FFN_UP = 0
U_FFN_DOWN = FB
N_FFN = FB + FB // 2
U_LORA = N_FFN
U_FILTER = U_LORA + 2
U_HYENA = U_FILTER + 1
U_DFT = U_HYENA + 2 * HY_C
U_RWKV = U_DFT + 4
U_GDN = U_RWKV + 2 * PAIRS
U_WOUT = U_GDN + 2 * PAIRS
U_XQ = U_WOUT + KT // 2
U_XK = U_XQ + KT // 2
U_XV = U_XK + KT // 2
U_XO = U_XV + KT // 2
U_FFN2 = U_XO + KT // 2
U_PAD = U_FFN2 + N_FFN
UNITS = U_PAD + U_PAD % 2

S_FFN1 = 0
S_WOUT = S_FFN1 + N_FFN
S_XQ = S_WOUT + KT // 2
S_XO = S_XQ + KT // 2
S_FFN2 = S_XO + KT // 2
SPLIT_UNITS = S_FFN2 + N_FFN
assert SPLIT_UNITS % 2 == 0
A_FFN1, A_WOUT, A_XQ, A_XO, A_FFN2 = range(5)
SPLIT_SOURCES = 5

_n = 0


def _cols(k):
    global _n
    _n += k
    return _n - k


C_NORM = _cols(4 * KT)
C_HY = _cols(13 * HY_C)
C_FILT = _cols(3)
C_LMU = _cols(6)
C_GNW = _cols(1)
C_DT = _cols(2 * HEADS)
C_ALOG = _cols(2 * HEADS)
C_RW = _cols(13 * PAIRS)
C_GD = _cols(9 * PAIRS)
N_COLS = _n
RWC, GDC = 13, 9
C_MEM, C_FINAL = 0, KT

_n = 0
K_ID = _cols(P)
K_ONES = _cols(P)
K_BONES = _cols(P)
K_RWTRI = _cols(2 * 2 * P)
K_GTRI = _cols(2 * P)
K_LEVEL = _cols(LEVELS * 2 * P)
K_SI = _cols(2 * 2 * P)
K_NEGT = _cols(TT)
K_SEL = _cols(PAIRS * 4 * P)
N_CONST = _n


def shape_constants():
    c = np.zeros((P, N_CONST), np.float32)
    i = np.arange(P)
    row, col = i[:, None], i[None, :]
    c[:, K_ID:K_ID + P] = row == col
    c[:, K_ONES:K_ONES + P] = 1.0
    c[:, K_BONES:K_BONES + P] = row // HD == col // HD
    half = P // 2
    for d in range(2):
        incl = (row <= col) if d == 0 else (row >= col)
        excl = (row < col) if d == 0 else (row > col)
        mid = (row < half) if d == 0 else (row >= half)
        at = K_RWTRI + d * 2 * P
        c[:, at:at + P] = incl.astype(np.float32) - mid
        c[:, at + P:at + 2 * P] = excl.astype(np.float32) - mid
        c[:, K_GTRI + d * P:K_GTRI + (d + 1) * P] = incl
        c[:, K_SI + d * 2 * P:K_SI + d * 2 * P + P] = excl
        c[:, K_SI + d * 2 * P + P:K_SI + (d + 1) * 2 * P] = incl
        for m in range(LEVELS):
            b = 2 ** m
            target, source = (row, col) if d == 0 else (col, row)
            ok = (target // (2 * b) == source // (2 * b)) & (target // b % 2 == 1) & (source // b % 2 == 0)
            at = K_LEVEL + (m * 2 + d) * P
            c[:, at:at + P] = ok
    t = np.linspace(0.0, 1.0, SEQ, dtype=np.float32)
    c[:, K_NEGT:K_NEGT + TT] = -t.reshape(TT, P).T
    for j in range(PAIRS):
        for d in range(2):
            for h in range(2):
                at = K_SEL + (j * 4 + d * 2 + h) * P
                c[d * HEADS + 2 * j + h, at:at + P] = 1.0
    return c


def dft_units():
    t, f = np.arange(SEQ)[:, None], np.arange(SEQ)[None, :]
    ang = 2 * np.pi * (((2 * f + 1) * t) % (4 * SEQ)) / (4 * SEQ)
    out = []
    for m in (np.cos(ang), np.sin(ang), np.cos(ang).T, np.sin(ang).T):
        out.append(m.astype(np.float32).reshape(TT, P, SEQ).transpose(1, 0, 2).reshape(P, UNIT))
    return out


def positional_features():
    t = np.linspace(0.0, 1.0, SEQ, dtype=np.float32)[:, None]
    ang = (np.float32(2.0 * np.pi) * np.arange(SEQ, dtype=np.float32)[:, None] / np.float32(SEQ)).astype(np.float32)
    bands = np.linspace(1e-4, 15, 16, dtype=np.float32)[None, :]
    return np.concatenate([t, np.cos(bands * ang), -np.sin(bands * ang)], axis=-1).astype(np.float32)


class Signal:

    def __init__(self, sem, per):
        self.sem, self.per = sem, per

    def at(self, it, k):
        return it * self.per + k


def trunk_program(nc, xT, memT, units, cols, gcols, consts, out, layers=DEPTH):
    ctx = ExitStack()
    with ctx:
        place = {}

        def sb(name, shape):
            t = ctx.enter_context(nc.sbuf_tensor(name, shape, F32))
            place[name] = nc.sbuf_base - 4 * int(np.prod(shape[1:]))
            return t

        def rounded(name, shape, where, floats=0):
            t = nc.alloc_sbuf_tensor_at(name, [P] + shape, F32R, offset=place[where] + 4 * floats)
            return t[tuple(slice(None) for _ in range(len(shape) + 1))]

        def sig(name, per=1):
            return Signal(ctx.enter_context(nc.semaphore(name)), per)

        x = sb("x", [P, KT, SEQ])
        h = sb("h", [P, KT, SEQ])
        memn = sb("memn", [P, KT, N_MEM])
        y = sb("y", [P, KT, SEQ])
        ring = [sb(f"ring{i}", [P, UNIT]) for i in range(2)]
        kon = sb("kon", [P, N_CONST])
        cols_all = sb("cols_all", [P, DEPTH, N_COLS])
        gc = sb("gcols_sb", [P, 2 * KT])
        cl = sb("cl", [P, N_COLS])
        clj = sb("clj", [P, RWC])
        eps = sb("eps", [P, 2])
        lwT, laT, lgT = (sb(n, [P, SEQ]) for n in ("lwT", "laT", "lgT"))
        lora_c0 = sb("lora_c0", [P, 3])
        nega = sb("nega", [P, 2 * HEADS])
        beta = sb("beta", [P, TT, 2 * HEADS])
        gsum = sb("gsum", [P, TT, 2 * HEADS])
        gsumT = sb("gsumT", [P, SEQ])
        sc = sb("scratch", [P, 23600])
        psum = ctx.enter_context(nc.psum_tensor("psum", [P, 8, 512], F32))
        bank = [psum[:, i, :] for i in range(8)]

        ident = kon[:, K_ID:K_ID + P]
        ones = kon[:, K_ONES:K_ONES + P]
        bones = kon[:, K_BONES:K_BONES + P]
        rwtri = [[kon[:, K_RWTRI + (2 * d + e) * P:K_RWTRI + (2 * d + e + 1) * P] for e in range(2)] for d in range(2)]
        gtri = [kon[:, K_GTRI + d * P:K_GTRI + (d + 1) * P] for d in range(2)]
        strict_incl = [kon[:, K_SI + d * 2 * P:K_SI + (d + 1) * 2 * P] for d in range(2)]
        incl = [kon[:, K_SI + (2 * d + 1) * P:K_SI + (2 * d + 2) * P] for d in range(2)]

        def level_mask(m, d):
            at = K_LEVEL + (m * 2 + d) * P
            return kon[:, at:at + P]

        def over(ap, n):
            return ap.unsqueeze(1).broadcast_to([ap.shape[0], n, ap.shape[-1]])

        at = [0]

        def carve(*shape):
            n = int(np.prod(shape))
            v = sc[:, at[0]:at[0] + n]
            at[0] += n
            assert at[0] <= 23600, at[0]
            if len(shape) == 2:
                return v.rearrange("p (a b) -> p a b", a=shape[0])
            if len(shape) == 3:
                return v.rearrange("p (a b c) -> p a b c", a=shape[0], b=shape[1])
            return v

        sq = carve(KT, SEQ)
        std = carve(SEQ)
        rstd = carve(SEQ)
        at[0] = 0
        u = carve(FB, SEQ)
        w_hi, w_lo = ([rounded(f"unit_{part}{i}", [UNIT], "scratch", at[0] + (2 * e + i) * UNIT) for i in range(2)]
                      for e, part in enumerate(("hi", "lo")))
        at[0] += 4 * UNIT
        u_hi, u_lo = ([rounded(f"inner_{part}{i}", [2, SEQ], "scratch", at[0] + (2 * e + i) * 2 * SEQ) for i in range(2)]
                      for e, part in enumerate(("hi", "lo")))
        at[0] += 8 * SEQ
        assert at[0] <= 23600
        sil = [lwT[:, :], laT[:, :]]
        a_hi, a_lo = rounded("source_hi", [KT, SEQ], "h"), rounded("source_lo", [KT, SEQ], "y")
        at[0] = 0
        gx, ge, gl = (carve(TT, 2 * HEADS) for _ in range(3))
        gtok = carve(TT, 2 * HEADS)
        at[0] = 0
        filt_arg, filt_k, filt_h1, filt_h2 = (carve(SEQ) for _ in range(4))
        filt = carve(TT, 512)
        filt_e = carve(TT, 512)
        filt_sum = carve(512)
        filt_rn = carve(256)
        kplus, kminus = carve(TT, 256), carve(TT, 256)
        at[0] = 0
        _keep = carve(4 * SEQ)
        hx0 = [carve(SEQ) for _ in range(2)]
        hu = [carve(SEQ) for _ in range(2)]
        utok = carve(TT, 256)
        at[0] = 4 * SEQ + TT * 512 * 2 + 512 + 256 + 2 * TT * 256
        hx1, hv = carve(SEQ), carve(SEQ)
        spec = carve(8, 512)
        prA, prB, prT = carve(TT, 256), carve(TT, 256), carve(TT, 256)
        hyo = prT.rearrange("p a b -> p (a b)")
        hyo = [hyo[:, 0:512], hyo[:, 512:1024]]
        at[0] = 0
        AR = [carve(TT, 2, P) for _ in range(2)]
        KTt = [carve(SEQ) for _ in range(2)]
        BTt = [carve(SEQ) for _ in range(2)]
        Vtok = carve(TT, P)
        Btok = [carve(TT, P) for _ in range(2)]
        Ktok = [carve(TT, P) for _ in range(2)]
        gateT, bv, yo = carve(SEQ), carve(SEQ), carve(SEQ)
        Z = [carve(HD) for _ in range(2)]
        Tt = [carve(P) for _ in range(2)]
        Ut = [carve(P) for _ in range(2)]
        lastP, firstP, fac = (carve(2, TT) for _ in range(3))
        rwc = carve(4)
        late = at[0]
        SCB = [carve(TT, 2, P) for _ in range(4)]
        SCK = [carve(TT, 2, P) for _ in range(4)]
        X, XT, Y = ([carve(TT, P) for _ in range(4)] for _ in range(3))
        at[0] = late
        rT, kT, vT, kkr, kk, nkk, tmpA, tmpB, rk = (carve(SEQ) for _ in range(9))
        aT = [carve(SEQ) for _ in range(2)]
        sg = [carve(TT, P) for _ in range(2)]
        Pinc = [carve(TT, P) for _ in range(2)]
        Pinv = [carve(TT, P) for _ in range(2)]
        Pexc = [carve(TT, P) for _ in range(2)]
        aP, kd = ([carve(SEQ) for _ in range(2)] for _ in range(2))
        at[0] = 0
        GA = [carve(TT, P) for _ in range(2)]
        GR = [carve(TT, P) for _ in range(2)]
        GV = carve(TT, P)
        GKtok = carve(TT, P)
        Kend = [carve(TT, 2, HD) for _ in range(2)]
        EG = [carve(TT, P) for _ in range(2)]
        zg, go, gqT, gkT, gvT = (carve(SEQ) for _ in range(5))
        GZ = [carve(HD) for _ in range(2)]
        GT = [carve(P) for _ in range(2)]
        GU = [carve(P) for _ in range(2)]
        selj = carve(4, P)
        gcj, btj, nbj = (carve(TT, 4) for _ in range(3))
        KEp, KE = carve(4, TT), carve(4, TT)
        GL = [carve(TT, P) for _ in range(4)]
        GAT = [carve(TT, P) for _ in range(4)]
        GDT = [carve(TT, P) for _ in range(4)]
        assert at[0] <= late + 8 * TT * 2 * P
        at[0] = late + 8 * TT * 2 * P
        gs1, gs2, gr1, gr2 = (carve(SEQ) for _ in range(4))
        at[0] = 0
        qT = carve(KT, SEQ)
        kmT = carve(KT, N_MEM)
        vm = carve(2, D_MODEL)
        prob = [carve(TT, N_MEM) for _ in range(2)]
        probT = carve(2, SEQ)
        assert at[0] <= FB * SEQ
        at[0] = FB * SEQ + 4 * UNIT
        oT = carve(KT, SEQ)
        nmx, psm, rsm = ([carve(TT) for _ in range(2)] for _ in range(3))

        full = [sig(f"unit_loaded_in_slot{i}", 16 * UNITS // 2) for i in range(2)]
        free = sig("unit_used", UNITS)
        consts_in = sig("constants_loaded")
        x_in = sig("inputs_loaded")
        J = {n: sig("joined_" + n, 4 * k) for n, k in
             dict(start=1, ffn=1, norm=1, lora=1, filter=1, hyena=1, dft=1, rwkv=1, gdn=1, proj=1, attn=1,
                  layer=1).items()}
        n_sq, n_sum, n_std = (sig(n, k) for n, k in
                                      (("squares_ready", KT), ("square_sum_ready", 1), ("std_ready", 1)))
        xv_ps = sig("mem_values_ready")
        f_sil, f_u, f_dn = sig("silu_ready", 2), sig("inner_ready", 2), sig("ffn_down_ready", KT)
        ws_hi, ws_lo, ws_done = (sig(n, SPLIT_UNITS) for n in ("unit_hi_ready", "unit_lo_ready", "unit_products_done"))
        x_up = sig("x_updated", KT)
        as_f, as_hi, as_lo = (sig(n, KT) for n in ("normed_ready", "source_hi_ready", "source_lo_ready"))
        lo_ps, lo_base, lo_done = sig("lora_products_ready", 4), sig("lora_base_ready", 3), sig("lora_shifted", 3)
        ga_a, ga_b, ga_c, ga_e, ga_f = (sig(n, 1) for n in (
            "lora_scales_ready", "gate_negated_abs_ready", "gate_log_ready", "gate_decays_ready", "gate_sums_product"))
        ga_t, ga_g = sig("gate_rows_ready", 1), sig("gate_sums_ready", 1)
        fl_ps, fl_arg, fl_h = sig("filter_layer_ready", 2), sig("filter_argument_ready", 2), sig("filter_sine_ready", 2)
        fl_out, fl_e, fl_k, fl_abs, fl_sum, fl_s = (sig(n, k) for n, k in (
            ("filter_taps_ready", TT), ("filter_window_ready", TT), ("filter_windowed", TT), ("filter_abs_ready", TT),
            ("filter_sum_ready", 1), ("filter_sum_copied", 1)))
        hy_ps, hy_base, hy_cv = sig("hyena_projected", 3 * 2), sig("hyena_base_ready", 3 * 2), sig("hyena_u_ready", 2)
        hy_tp = sig("hyena_u_turned", 2)
        sp_ps, sp_sb, sp_pr, sp_y = sig("spectra_ready", 8), sig("spectra_copied", 8), sig("product_ready", 2), sig("hyena_y_ready", 2)
        rw_ps, rw_base, rw_cols = sig("rwkv_projected", 8), sig("rwkv_base_ready", 3), sig("rwkv_columns_ready", 1)
        rw_w0, rw_sig = sig("rwkv_w0_added", 2), sig("rwkv_decay_ready", 2)
        rw_kk2, rw_rk = sig("rwkv_kk_squared", 1), sig("rwkv_rk_ready", 1)
        rw_g, rw_nrm, rw_std, rw_bon = sig("rwkv_sums_ready", 4), sig("rwkv_kk_norm_ready", 1), sig("rwkv_kk_std_ready", 1), sig("rwkv_bonus_ready", 1)
        rw_exp, rw_kd, rw_gstd = sig("rwkv_decays_ready", 8), sig("rwkv_kd_ready", 2), sig("rwkv_group_std_ready")
        rw_tp, rw_tok = sig("rwkv_turned", 5), sig("rwkv_tokens_ready", 5)
        rw_op, rw_vt = sig("rwkv_operands_ready", 2), sig("rwkv_v_ready", 1)
        rw_scp, rw_scs = sig("rwkv_scores_ready", 16), sig("rwkv_scores_masked", 16)
        rw_fin = [sig(f"rwkv_finish{i}", 1) for i in range(6)]
        iv = dict(
            half=sig("inv_start_product", 4), xt=sig("inv_xt_ready", 4 * LEVELS),
            xps=sig("inv_x_turned", 4 * (LEVELS - 1)), x=sig("inv_x_ready", 4 * (LEVELS - 1)),
            yps=sig("inv_lx_product", 4 * (LEVELS - 1)), y=sig("inv_lx_ready", 4 * (LEVELS - 1)),
            xtps=sig("inv_xy_product", 4 * (LEVELS - 1)))
        scan_sig = dict(
            z0=sig("state_cleared", 1),
            tps=[sig(f"t_product{d}", TT) for d in range(2)], t=[sig(f"t_ready{d}", TT) for d in range(2)],
            ups=[sig(f"u_product{d}", TT) for d in range(2)], u=[sig(f"u_ready{d}", TT) for d in range(2)],
            zps=[sig(f"state_product{d}", TT - 1) for d in range(2)], z=[sig(f"state_ready{d}", TT - 1) for d in range(2)])
        gd_ps, gd_base, gd_sh, gd_silu = sig("gdn_projected", 4), sig("gdn_base_ready", 3), sig("gdn_convolved", 3), sig("gdn_silu_ready", 3)
        gd_sq, gd_nrm, gd_std, gd_qk = sig("gdn_squares_ready", 2), sig("gdn_norms_ready", 2), sig("gdn_std_ready", 2), sig("gdn_qk_ready", 2)
        gd_sel, gd_row, gd_dif, gd_exp, gd_msk = sig("gdn_pair_columns_ready", 1), sig("gdn_rows_ready", 4), sig("gdn_differences_ready", 4), sig("gdn_decays_ready", 4), sig("gdn_decays_masked", 4)
        gd_eg = sig("gdn_row_decays_ready", 4)
        gd_tp, gd_tok, gd_kk = sig("gdn_turned", 2), sig("gdn_tokens_ready", 2), sig("gdn_kk_ready", 4)
        gd_L, gd_kq, gd_scan = sig("gdn_l_ready", 4), sig("gdn_kq_copied", 2), sig("gdn_scan_operands_ready", 1)
        gd_fin = [sig(f"gdn_finish{i}", 1) for i in range(6)]
        pj_done = sig("projection_added", 4)
        xk_ps, xk_done = sig("mem_projection_ready", 8), sig("mem_projection_copied", 8)
        at_s, at_mx, at_e, at_n, at_tp, at_pt, at_o, at_od = (sig(n, k) for n, k in (
            ("scores_ready", XA_HEADS * TT), ("row_max_ready", XA_HEADS), ("probs_ready", XA_HEADS * TT), ("probs_normed", XA_HEADS),
            ("probs_turned", XA_HEADS * 2), ("probs_t_ready", XA_HEADS * 2), ("attn_out_ready", XA_HEADS * 2), ("attn_out_copied", XA_HEADS * 2)))
        stored = sig("output_stored")
        passed = sig("waits_settled")

        def turn_of(l, mixer, j):
            return (l * 2 + mixer) * PAIRS + j

        def settle(eng):
            eng.sem_inc(passed.sem, 1)

        def join(eng, name, it, k, idle=False):
            s = J[name]
            if idle:
                eng.sem_inc(s.sem, 1)
            else:
                eng.drain().then_inc(s.sem, 1)
            eng.wait_ge(s.sem, s.at(it, 4 * k))
            settle(eng)

        def arrive(eng, name):
            eng.drain().then_inc(J[name].sem, 1)

        def landed(l, n, later=0):
            return l * full[n % 2].per + 16 * (n // 2 + 1) + later * 16

        block = ctx.enter_context(nc.Block())

        @block.sync
        def _(sp):
            sp.dma_start(kon[:, :], consts).then_inc(consts_in.sem, 16)
            sp.dma_start(cols_all[:, :, :], cols).then_inc(consts_in.sem, 16)
            sp.dma_start(gc[:, :], gcols).then_inc(consts_in.sem, 16)
            sp.dma_start(sc[:, 8192:8192 + KT * N_MEM].rearrange("p (a b) -> p a b", a=KT), memT).then_inc(x_in.sem, 16)
            sp.dma_start(x[:, :, :], xT).then_inc(x_in.sem, 16)
            with sp.Fori(0, layers * UNITS // 2, 1) as n2:
                n = n2 * 2
                for s in range(2):
                    sp.wait_ge(free.sem, n + (s + 1))
                    sp.dma_start(ring[s][:, :], units[bass.ds(n + s, 1), :, :].rearrange("a p n -> (a p) n")).then_inc(full[s].sem, 16)
            sp.wait_ge(J["norm"].sem, J["norm"].at(layers + 2, 0))
            sp.dma_start(out, h[:, :, :]).then_inc(stored.sem, 16)
            sp.wait_ge(stored.sem, 16)

        @block.tensor
        def _(pe):
            mm = pe.matmul

            def used(n=1):
                pe.drain().then_inc(free.sem, n)

            def square_sum(it, t, b, n_tok=SEQ):
                pe.wait_ge(n_sq.sem, n_sq.at(it, t + 1))
                last = mm(bank[b][:, 0:n_tok], ones, sq[:, t, 0:n_tok], start=t == 0, stop=t == KT - 1)
                if t == KT - 1:
                    last.then_inc(n_sum.sem, 1)

            def project(dst, slot, half, src, l, unit, done, width=SEQ):
                w = ring[slot][:, half * KT * P:(half + 1) * KT * P].rearrange("p (k c) -> p k c", k=KT)
                pe.wait_ge(full[(unit) % 2].sem, landed(l, unit))
                for k in range(KT):
                    last = mm(dst, w[:, k, :], src[:, k, 0:width], start=k == 0, stop=k == KT - 1)
                last.then_inc(done.sem, 1)

            def products(dst, w_h, w_l, a_h, a_l, start=False, stop=False):
                mm(dst, w_h, a_h, start=start, stop=False)
                mm(dst, w_h, a_l, start=False, stop=False)
                return mm(dst, w_l, a_h, start=False, stop=stop)

            def two_blocks(b, dsts, a_h, a_l, source=None):
                wh, wl = (w[b].rearrange("p (m k c) -> p m k c", m=2, k=KT) for w in (w_hi, w_lo))
                for k in range(KT):
                    if source is not None:
                        pe.wait_ge(as_lo.sem, as_lo.at(source, k + 1))
                    for m in range(2):
                        last = products(dsts[m], wh[:, m, k, :], wl[:, m, k, :], a_h[:, k, :], a_l[:, k, :],
                                        start=k == 0, stop=k == KT - 1)
                return last

            def ffn(l, which, n0, source):
                with pe.Fori(0, FB // 2, 1) as j:
                    it = (l * 2 + which) * (FB // 2) + j
                    for s in range(2):
                        pe.wait_ge(ws_lo.sem, ws_lo.at(l, n0 + s + 1) + j * 2)
                        pe.wait_ge(f_u.sem, it * 2 + (s + 1))
                        two_blocks((n0 + s) % 2, [bank[2 * s + m][:, :] for m in range(2)], a_hi, a_lo,
                                   None if s else l * SPLIT_SOURCES + source).then_inc(ws_done.sem, 1)
                n0 += FB

                def down(n, banks, ks, first=False):
                    wh, wl = (w[n % 2].rearrange("p (k c) -> p k c", k=2) for w in (w_hi, w_lo))
                    for k in ks:
                        for m in banks:
                            last = products(bank[m][:, :], wh[:, k, m * P:(m + 1) * P], wl[:, k, m * P:(m + 1) * P],
                                            u_hi[n % 2][:, k, :], u_lo[n % 2][:, k, :], start=first)
                    return last

                pe.wait_ge(ws_lo.sem, ws_lo.at(l, n0 + 1))
                down(n0, range(4, 8), (0,), first=True)
                pe.wait_ge(f_u.sem, ((l * 2 + which) + 1) * FB + 2)
                down(n0, range(4), (0,), first=True)
                down(n0, range(8), (1,)).then_inc(ws_done.sem, 1)
                with pe.Fori(0, 4, 1) as j:
                    for s in range(2):
                        pe.wait_ge(ws_lo.sem, ws_lo.at(l, n0 + s + 2) + j * 2)
                        down(n0 + 1 + s, range(8), (0, 1)).then_inc(ws_done.sem, 1)
                pe.wait_ge(ws_lo.sem, ws_lo.at(l, n0 + 10))
                down(n0 + 9, range(8), (0, 1)).then_inc(ws_done.sem, 1)
                pe.wait_ge(ws_lo.sem, ws_lo.at(l, n0 + 11))
                wh, wl = (w[n0 % 2].rearrange("p (k c) -> p k c", k=2) for w in (w_hi, w_lo))
                for m in range(KT):
                    for k in range(2):
                        last = products(bank[m][:, :], wh[:, k, m * P:(m + 1) * P], wl[:, k, m * P:(m + 1) * P],
                                        u_hi[n0 % 2][:, k, :], u_lo[n0 % 2][:, k, :], stop=k == 1)
                    last.then_inc(f_dn.sem, 1)
                    if m >= 2:
                        square_sum(l * 4 + 2 + 3 * which, m - 2, 0)
                square_sum(l * 4 + 2 + 3 * which, KT - 2, 0)
                square_sum(l * 4 + 2 + 3 * which, KT - 1, 0)
                pe.drain().then_inc(ws_done.sem, 1)
                join(pe, "ffn", l * 2 + which, 1)

            def lora(l):
                for m, (unit, half) in enumerate(((U_LORA, 0), (U_LORA, 1), (U_LORA + 1, 0))):
                    project(bank[m][:, :], unit % 2, half, h, l, unit, lo_ps)
                w = ring[(U_LORA + 1) % 2][:, KT * P:KT * P + KT * 24].rearrange("p (k c) -> p k c", k=KT)
                for t in range(TT):
                    for k in range(KT):
                        last = mm(bank[3][:, t * 24:t * 24 + 24], h[:, k, t * P:(t + 1) * P], w[:, k, :],
                                  start=k == 0, stop=k == KT - 1)
                last.then_inc(lo_ps.sem, 1)
                used(2)
                pe.wait_ge(ga_e.sem, ga_e.at(l, 1))
                for t in range(TT):
                    for d in range(2):
                        last = mm(bank[4][:, (t * 2 + d) * HEADS:(t * 2 + d + 1) * HEADS], gtri[d],
                                  gtok[:, t, d * HEADS:(d + 1) * HEADS], start=True, stop=True)
                last.then_inc(ga_f.sem, 1)
                pe.wait_ge(ga_g.sem, ga_g.at(l, 1))
                for t in range(TT):
                    last = pe.transpose(bank[5][0:2 * HEADS, t * P:(t + 1) * P], gsum[:, t, :], ident)
                last.then_inc(ga_t.sem, 1)
                arrive(pe, "lora")

            def hyena_filter(l):
                w = ring[U_FILTER % 2]
                pe.wait_ge(full[(U_FILTER) % 2].sem, landed(l, U_FILTER))
                settle(pe)
                mm(bank[0][0:HY_FFN, :], w[0:HY_EMB, 512:512 + HY_FFN], w[0:HY_EMB, 1152:1152 + SEQ],
                   start=True, stop=True).then_inc(fl_ps.sem, 1)
                pe.wait_ge(fl_h.sem, fl_h.at(l, 1))
                settle(pe)
                mm(bank[1][0:HY_FFN, :], w[0:HY_FFN, 576:576 + HY_FFN], filt_h1[0:HY_FFN, :],
                   start=True, stop=True).then_inc(fl_ps.sem, 1)
                pe.wait_ge(fl_h.sem, fl_h.at(l, 2))
                for t in range(TT):
                    mm(bank[2 + t][:, :], filt_h2[0:HY_FFN, t * P:(t + 1) * P], w[0:HY_FFN, 0:512],
                       start=True, stop=True).then_inc(fl_out.sem, 1)
                for t in range(TT):
                    pe.wait_ge(fl_abs.sem, fl_abs.at(l, t + 1))
                    last = mm(bank[6][:, :], ones, filt_e[:, t, :], start=t == 0, stop=t == TT - 1)
                last.then_inc(fl_sum.sem, 1)
                arrive(pe, "filter")
                used()

            def hyena(l):
                for c in range(HY_C):
                    if c:
                        pe.wait_ge(J["filter"].sem, J["filter"].at(l, 4))
                        settle(pe)
                    for m in range(3):
                        unit = U_HYENA + 2 * c + m // 2
                        project(bank[4 * c + m][:, :], unit % 2, m % 2, h, l, unit, hy_ps)
                    used(2)
                for c in range(HY_C):
                    pe.wait_ge(hy_cv.sem, hy_cv.at(l, c + 1))
                    for t in range(TT):
                        last = pe.transpose(bank[4 * c + 3][:, t * P:(t + 1) * P], hu[c][:, t * P:(t + 1) * P], ident)
                    last.then_inc(hy_tp.sem, 1)
                join(pe, "hyena", l, 1)
                for part, flt in ((0, kplus), (1, kminus)):
                    unit = U_DFT + part
                    pe.wait_ge(full[(unit) % 2].sem, landed(l, unit))
                    w = ring[unit % 2][:, :].rearrange("p (t f) -> p t f", t=TT)
                    for f in range(TT):
                        for half, src in ((0, utok), (1, flt)):
                            for t in range(TT):
                                last = mm(bank[4 * part + f][:, half * 256:half * 256 + 256], w[:, t, f * P:(f + 1) * P],
                                          src[:, t, :], start=t == 0, stop=t == TT - 1)
                        last.then_inc(sp_ps.sem, 1)
                    used()
                pe.wait_ge(sp_pr.sem, sp_pr.at(l, 2))
                pe.wait_ge(full[(U_DFT + 2) % 2].sem, landed(l, U_DFT + 2))
                pe.wait_ge(full[(U_DFT + 3) % 2].sem, landed(l, U_DFT + 3))
                for c in range(HY_C):
                    for part, src in ((0, prA), (1, prB)):
                        w = ring[(U_DFT + part) % 2][:, :].rearrange("p (f t) -> p f t", f=TT)
                        for f in range(TT):
                            last = mm(bank[c][:, :], src[:, f, c * P:(c + 1) * P], w[:, f, :],
                                      start=part == 0 and f == 0, stop=part == 1 and f == TT - 1)
                    last.then_inc(sp_y.sem, 1)
                used(2)
                arrive(pe, "dft")

            def invert(turn, LT):
                s = iv
                L1 = LEVELS - 1
                for g in range(4):
                    pe.wait_ge(s["xt"].sem, s["xt"].at(turn, g + 1))
                    for t in range(TT):
                        last = pe.transpose(bank[g][:, t * P:(t + 1) * P], XT[g][:, t, :], ident)
                    last.then_inc(s["xps"].sem, 1)
                for m in range(L1):
                    for g in range(4):
                        pe.wait_ge(s["x"].sem, s["x"].at(turn, 4 * m + g + 1))
                        for t in range(TT):
                            last = mm(bank[g][:, t * P:(t + 1) * P], LT[g](t), X[g][:, t, :], start=True, stop=True)
                        last.then_inc(s["yps"].sem, 1)
                    for g in range(4):
                        pe.wait_ge(s["y"].sem, s["y"].at(turn, 4 * m + g + 1))
                        for t in range(TT):
                            last = mm(bank[4 + g][:, t * P:(t + 1) * P], Y[g][:, t, :], XT[g][:, t, :], start=True, stop=True)
                        last.then_inc(s["xtps"].sem, 1)
                    if m < L1 - 1:
                        for g in range(4):
                            pe.wait_ge(s["xt"].sem, s["xt"].at(turn, 4 * (m + 1) + g + 1))
                            for t in range(TT):
                                last = pe.transpose(bank[g][:, t * P:(t + 1) * P], XT[g][:, t, :], ident)
                            last.then_inc(s["xps"].sem, 1)

            def scan(turn, A, R, V, LK, MB, MK, Bt, Kt_, Zs, Ts, Us):
                s = scan_sig
                pe.wait_ge(s["z0"].sem, s["z0"].at(turn, 1))
                for c in range(TT):
                    for d in range(2):
                        t = c if d == 0 else TT - 1 - c
                        if c:
                            pe.wait_ge(s["z"][d].sem, s["z"][d].at(turn, c))
                        for hh in range(2):
                            r = slice(hh * HD, hh * HD + HD)
                            g = 2 * d + hh
                            last = mm(bank[2 * d + hh][:, 0:HD], A[d](t)[r, :], Zs[d][r, :], start=True, stop=LK is None)
                            if LK is not None:
                                last = mm(bank[2 * d + hh][:, 0:HD], LK[g](t), V[:, t, r], start=False, stop=True)
                        last.then_inc(s["tps"][d].sem, 1)
                        for hh in range(2):
                            r = slice(hh * HD, hh * HD + HD)
                            mm(bank[4 + d][r, t * P:(t + 1) * P], Zs[d][r, :], R[d](t)[r, :], start=True, stop=False)
                    for d in range(2):
                        t = c if d == 0 else TT - 1 - c
                        pe.wait_ge(s["t"][d].sem, s["t"][d].at(turn, c + 1))
                        for hh in range(2):
                            r = slice(hh * HD, hh * HD + HD)
                            last = mm(bank[6 + d][:, r], XT[2 * d + hh][:, t, :], Ts[d][:, r], start=True, stop=True)
                        last.then_inc(s["ups"][d].sem, 1)
                    for d in range(2):
                        t = c if d == 0 else TT - 1 - c
                        pe.wait_ge(s["u"][d].sem, s["u"][d].at(turn, c + 1))
                        if c < TT - 1:
                            for hh in range(2):
                                r = slice(hh * HD, hh * HD + HD)
                                last = mm(bank[6 + d][r, P:P + HD], Bt[d](t)[:, r], Us[d][:, r], start=True, stop=Kt_ is None)
                                if Kt_ is not None:
                                    last = mm(bank[6 + d][r, P:P + HD], Kt_[d][:, t, r], V[:, t, r], start=False, stop=True)
                            last.then_inc(s["zps"][d].sem, 1)
                        for hh in range(2):
                            r = slice(hh * HD, hh * HD + HD)
                            g = 2 * d + hh
                            o = bank[4 + d][r, t * P:(t + 1) * P]
                            mm(o, Us[d][:, r], MB[g](t), start=False, stop=MK is None)
                            if MK is not None:
                                mm(o, V[:, t, r], MK[g](t), start=False, stop=True)

            def rwkv(l, j):
                it = l * PAIRS + j
                s0 = U_RWKV % 2
                s1 = 1 - s0
                small = ring[s1][:, KT * P:2 * KT * P]

                def block_of(m):
                    w = ring[(s0, s0, s1)[m]][:, (m % 2) * KT * P:(m % 2 + 1) * KT * P].rearrange("p (k c) -> p k c", k=KT)
                    for k in range(KT):
                        last = mm(bank[m][:, :], w[:, k, :], h[:, k, :], start=k == 0, stop=k == KT - 1)
                    last.then_inc(rw_ps.sem, 1)

                pe.wait_ge(full[(U_RWKV + 1) % 2].sem, landed(l, U_RWKV + 1, j))
                for t in range(TT):
                    for d in range(2):
                        r = slice(d * HD, d * HD + HD)
                        last = mm(bank[6 + d][:, t * P:(t + 1) * P], lwT[r, t * P:(t + 1) * P], small[r, 0:128], start=True, stop=True)
                        if t == TT - 1:
                            last.then_inc(rw_ps.sem, 1)
                for d in range(2):
                    r = slice(d * HD, d * HD + HD)
                    mm(bank[4 + d][:, :], small[r, 128:256], laT[r, :], start=True, stop=True).then_inc(rw_ps.sem, 1)
                mm(bank[3][:, :], small[:, 256:384], lgT[:, :], start=True, stop=True).then_inc(rw_ps.sem, 1)
                pe.wait_ge(full[U_RWKV % 2].sem, landed(l, U_RWKV, j))
                pe.wait_ge(rw_w0.sem, rw_w0.at(it, 2))
                pe.wait_ge(rw_gstd.sem, it + 1)
                block_of(1)
                for d in range(2):
                    pe.wait_ge(rw_sig.sem, rw_sig.at(it, 2))
                    for e in range(2):
                        for t in range(TT):
                            last = mm(bank[4 + 2 * d + e][:, t * P:(t + 1) * P], sg[d][:, t, :], rwtri[d][e], start=True, stop=True)
                        last.then_inc(rw_g.sem, 1)
                block_of(0)
                used()
                pe.wait_ge(rw_kk2.sem, rw_kk2.at(it, 1))
                mm(bank[3][:, :], bones, tmpA[:, :], start=True, stop=True).then_inc(rw_nrm.sem, 1)
                block_of(2)
                used()
                pe.wait_ge(rw_rk.sem, rw_rk.at(it, 1))
                mm(bank[0][:, :], bones, rk[:, :], start=True, stop=True).then_inc(rw_bon.sem, 1)
                for n, (src, b) in enumerate(((BTt[0], 4), (KTt[0], 5), (vT, 1), (BTt[1], 6), (KTt[1], 7))):
                    if n == 2:
                        pe.wait_ge(rw_vt.sem, rw_vt.at(it, 1))
                    else:
                        pe.wait_ge(rw_op.sem, rw_op.at(it, n // 3 + 1))
                    for t in range(TT):
                        last = pe.transpose(bank[b][:, t * P:(t + 1) * P], src[:, t * P:(t + 1) * P], ident)
                    last.then_inc(rw_tp.sem, 1)
                for d in range(2):
                    for n in range(4):
                        src = (BTt, KTt)[n // 2][d]
                        if d:
                            pe.wait_ge(rw_scs.sem, rw_scs.at(it, 2 * n + 2))
                        else:
                            pe.wait_ge(rw_tok.sem, rw_tok.at(it, (3, 3, 4, 5)[n]))
                        for e in range(2):
                            t = 2 * (n % 2) + e
                            for hh in range(2):
                                r = slice(hh * HD, hh * HD + HD)
                                last = mm(bank[4 * hh + n][:, e * 256:(e + 1) * 256], src[r, t * P:(t + 1) * P],
                                          AR[d][r, t, :, :].rearrange("p a b -> p (a b)"), start=True, stop=True)
                                if e:
                                    last.then_inc(rw_scp.sem, 1)
                invert(turn_of(l, 0, j), [lambda t, g=g: SCB[g][:, t, 0, :] for g in range(4)])
                scan(turn_of(l, 0, j), [lambda t, d=d: AR[d][:, t, 0, :] for d in range(2)],
                     [lambda t, d=d: AR[d][:, t, 1, :] for d in range(2)], Vtok,
                     [lambda t, g=g: SCK[g][:, t, 0, :] for g in range(4)],
                     [lambda t, g=g: SCB[g][:, t, 1, :] for g in range(4)],
                     [lambda t, g=g: SCK[g][:, t, 1, :] for g in range(4)],
                     [lambda t, d=d: Btok[d][:, t, :] for d in range(2)], Ktok, Z, Tt, Ut)
                pe.drain().then_inc(rw_fin[0].sem, 1)
                pe.wait_ge(rw_fin[1].sem, rw_fin[1].at(it, 1))
                mm(bank[0][:, :], bones, yo[:, :], start=True, stop=True).then_inc(rw_fin[2].sem, 1)
                pe.wait_ge(rw_fin[3].sem, rw_fin[3].at(it, 1))
                mm(bank[1][:, :], bones, tmpA[:, :], start=True, stop=True).then_inc(rw_fin[4].sem, 1)
                arrive(pe, "rwkv")

            def gdn(l, j):
                it = l * PAIRS + j
                for m in range(4):
                    if m == 1:
                        pe.wait_ge(gd_sel.sem, gd_sel.at(it, 1))
                        settle(pe)
                        for g in range(4):
                            mm(bank[4 + g][:, :], selj[0:2 * HEADS, g, :], gsumT[0:2 * HEADS, :],
                               start=True, stop=True).then_inc(gd_row.sem, 1)
                    if m == 3:
                        for n in range(2):
                            pe.wait_ge(gd_sq.sem, gd_sq.at(it, n + 1))
                            pe.wait_ge(gd_dif.sem, gd_dif.at(it, n + 1))
                            mm(bank[4 + n][:, :], bones, (gs2, gs1)[n][:, :], start=True, stop=True).then_inc(gd_nrm.sem, 1)
                    slot = (U_GDN + m // 2) % 2
                    w = ring[slot][:, (m % 2) * KT * P:(m % 2 + 1) * KT * P].rearrange("p (k c) -> p k c", k=KT)
                    pe.wait_ge(full[(U_GDN + m // 2) % 2].sem, landed(l, U_GDN + m // 2, j))
                    for k in range(KT):
                        last = mm(bank[m][:, :], w[:, k, :], h[:, k, :], start=k == 0, stop=k == KT - 1)
                    last.then_inc(gd_ps.sem, 1)
                    if m % 2:
                        used()
                pe.wait_ge(gd_qk.sem, gd_qk.at(it, 1))
                pe.wait_ge(gd_dif.sem, gd_dif.at(it, 4))
                for n, src in enumerate((gkT, gvT)):
                    if n:
                        pe.wait_ge(gd_silu.sem, gd_silu.at(it, 3))
                    for t in range(TT):
                        last = pe.transpose(bank[7 - n][:, t * P:(t + 1) * P], src[:, t * P:(t + 1) * P], ident)
                    last.then_inc(gd_tp.sem, 1)
                for n in range(2):
                    rhs = (gkT, gqT)[n]
                    if n:
                        pe.wait_ge(gd_qk.sem, gd_qk.at(it, 2))
                    for t in range(TT):
                        for hh in range(2):
                            r = slice(hh * HD, hh * HD + HD)
                            last = mm(bank[4 * n + hh][:, t * P:(t + 1) * P], gkT[r, t * P:(t + 1) * P], rhs[r, t * P:(t + 1) * P],
                                      start=True, stop=True)
                            if t == TT - 1:
                                last.then_inc(gd_kk.sem, 1)
                pe.wait_ge(gd_tok.sem, gd_tok.at(it, 2))
                settle(pe)
                invert(turn_of(l, 1, j), [lambda t, g=g: GL[g][:, t, :] for g in range(4)])
                pe.wait_ge(gd_scan.sem, gd_scan.at(it, 1))
                settle(pe)
                scan(turn_of(l, 1, j), [lambda t, d=d: GA[d][:, t, :] for d in range(2)],
                     [lambda t, d=d: GR[d][:, t, :] for d in range(2)], GV, None,
                     [lambda t, g=g: GAT[g][:, t, :] for g in range(4)], None,
                     [lambda t, d=d: Kend[d][:, t, :, :].rearrange("p a b -> p (a b)") for d in range(2)], None, GZ, GT, GU)
                pe.drain().then_inc(gd_fin[0].sem, 1)
                pe.wait_ge(gd_fin[1].sem, gd_fin[1].at(it, 1))
                mm(bank[3][:, :], bones, gs1[:, :], start=True, stop=True).then_inc(gd_fin[2].sem, 1)
                arrive(pe, "gdn")

            def projections(l, which, n0, source, a_low):
                with pe.Fori(0, 2, 1) as j:
                    it = (l * 3 + which) * 2 + j
                    for s in range(2):
                        pe.wait_ge(ws_lo.sem, ws_lo.at(l, n0 + s + 1) + j * 2)
                        pe.wait_ge(pj_done.sem, it * 4 + (2 * s + 2))
                        two_blocks((n0 + s) % 2, [bank[2 * s + m][:, :] for m in range(2)], a_hi, a_low,
                                   None if s else l * SPLIT_SOURCES + source).then_inc(ws_done.sem, 1)
                if which != 1:
                    for t in range(KT):
                        square_sum(l * 4 + 3 + which // 2, t, 4)
                join(pe, "proj", l * 3 + which, 1)

            def attention(l):
                projections(l, 1, S_XQ, A_XQ, a_lo)
                for m in range(KT):
                    if m >= 4:
                        pe.wait_ge(xk_done.sem, xk_done.at(l, m - 3))
                    project(bank[m % 4][:, 0:N_MEM], (U_XK + m // 2) % 2, m % 2, memn, l, U_XK + m // 2, xk_ps, N_MEM)
                    if m % 2:
                        used()
                for n in range(4):
                    pe.wait_ge(full[(U_XV + n) % 2].sem, landed(l, U_XV + n))
                    w = ring[(U_XV + n) % 2][:, :].rearrange("p (k c) -> p k c", k=KT)
                    for mt in range(2):
                        for k in range(KT):
                            mm(bank[4 + n][:, mt * 256:(mt + 1) * 256], memn[:, k, mt * P:(mt + 1) * P], w[:, k, :],
                                      start=k == 0, stop=k == KT - 1)
                    used()
                pe.sem_inc(xv_ps.sem, 1)
                join(pe, "attn", l * 2, 1)

                def scores(a):
                    for t in range(TT):
                        for b in range(2):
                            last = mm(bank[6 * (a % 2) + t // 2][:, (t % 2) * 256:(t % 2 + 1) * 256],
                                      qT[:, 2 * a + b, t * P:(t + 1) * P], kmT[:, 2 * a + b, :], start=b == 0, stop=b == 1)
                        last.then_inc(at_s.sem, 1)

                scores(0)
                for a in range(XA_HEADS):
                    if a + 1 < XA_HEADS:
                        scores(a + 1)
                    pe.wait_ge(at_n.sem, at_n.at(l, a + 1))
                    for m in range(2):
                        for t in range(TT):
                            last = pe.transpose(bank[2 + m][:, t * P:(t + 1) * P], prob[a % 2][:, t, m * P:(m + 1) * P], ident)
                        last.then_inc(at_tp.sem, 1)
                    if a:
                        pe.wait_ge(at_od.sem, at_od.at(l, 2 * a))
                    for b in range(2):
                        for m in range(2):
                            pe.wait_ge(at_pt.sem, at_pt.at(l, 2 * a + m + 1))
                            last = mm(bank[4 + b][:, :], vm[:, m, (2 * a + b) * P:(2 * a + b + 1) * P], probT[:, m, :],
                                      start=m == 0, stop=m == 1)
                        last.then_inc(at_o.sem, 1)
                join(pe, "attn", l * 2 + 1, 1)
                projections(l, 2, S_XO, A_XO, a_lo)

            pe.sem_inc(free.sem, 2)
            pe.sem_inc(ws_done.sem, 2)
            pe.sem_inc(rw_gstd.sem, 1)
            pe.wait_ge(consts_in.sem, 48)
            join(pe, "start", 0, 1)
            for t in range(KT):
                square_sum(0, t, 0, N_MEM)
            join(pe, "norm", 0, 1)
            for t in range(KT):
                square_sum(1, t, 0)
            with pe.Fori(0, layers, 1) as l:
                join(pe, "layer", l, 1)
                ffn(l, 0, S_FFN1, A_FFN1)
                join(pe, "norm", l + 1, 1)
                lora(l)
                hyena_filter(l)
                hyena(l)
                with pe.Fori(0, PAIRS, 1) as j:
                    rwkv(l, j)
                with pe.Fori(0, PAIRS, 1) as j:
                    gdn(l, j)
                pe.wait_ge(J["gdn"].sem, J["gdn"].at(l * PAIRS + (PAIRS - 1), 4))
                settle(pe)
                projections(l, 0, S_WOUT, A_WOUT, a_lo)
                attention(l)
                ffn(l, 1, S_FFN2, A_FFN2)
            join(pe, "norm", layers + 1, 1)

        @block.scalar
        def _(act):
            A = act.activation

            def squares(it, src, n_tok, updated=None):
                for t in range(KT):
                    if updated is not None:
                        act.wait_ge(updated[0].sem, updated[1] + t + 1)
                        settle(act)
                    A(sq[:, t, 0:n_tok], src[:, t, :], ACT.Square).then_inc(n_sq.sem, 1)

            def norm(it, b, n_tok, joined=None, l=None, source=None, n=None, unit=None):
                act.wait_ge(n_sum.sem, n_sum.at(it, 1))
                A(std[:, 0:n_tok], bank[b][:, 0:n_tok], ACT.Sqrt, bias=eps[:, 0:1], scale=1.0 / D_MODEL).then_inc(n_std.sem, 1)
                if source is not None:
                    unit_hi(l, n, unit)
                    unit_hi(l, n + 1, unit + 1)
                    source_hi(l, source, sq, {A_FFN1: 0, A_XQ: 1, A_FFN2: 2}[source])
                else:
                    join(act, "norm", joined, 1)

            def unit_hi(l, n, unit, later=0, inner=None):
                act.wait_ge(full[unit % 2].sem, landed(l, unit, later))
                act.wait_ge(ws_done.sem, ws_done.at(l, n + 1) + later * 2)
                if inner is not None:
                    A(u_hi[n % 2], inner, ACT.Copy)
                A(w_hi[n % 2], ring[unit % 2][:, :], ACT.Copy).then_inc(ws_hi.sem, 1)

            def source_hi(l, source, src, normed=None):
                for t in range(KT):
                    if normed is not None:
                        act.wait_ge(as_f.sem, as_f.at(l * 3 + normed, t + 1))
                    A(a_hi[:, t, :], src[:, t, :], ACT.Copy).then_inc(as_hi.sem, 1)

            def ffn(l, which, n0, unit, source):
                def silu(it, s, later):
                    act.wait_ge(ws_done.sem, ws_done.at(l, n0 + s + 3) + later * 2)
                    act.wait_ge(f_u.sem, it * 2 + (s + 1))
                    A(sil[s], bank[2 * s][:, :], ACT.Silu).then_inc(f_sil.sem, 1)

                with act.Fori(0, FB // 2 - 1, 1) as j:
                    for s in range(2):
                        silu((l * 2 + which) * (FB // 2) + j, s, j)
                        unit_hi(l, n0 + s + 2, unit + s + 2, j)
                for s in range(2):
                    silu((l * 2 + which) * (FB // 2) + (FB // 2 - 1), s, FB // 2 - 1)
                    unit_hi(l, n0 + FB + s, unit + FB + s, inner=u[:, 2 * s:2 * s + 2, :])
                n0, unit = n0 + FB, unit + FB
                with act.Fori(0, 4, 1) as j:
                    for s in range(2):
                        unit_hi(l, n0 + 2 + s, unit + 2 + s, j, u[:, bass.ds(j * 4 + (2 * s + 4), 2), :])
                act.wait_ge(f_u.sem, ((l * 2 + which) + 1) * FB + 2)
                unit_hi(l, n0 + 10, unit + 10, inner=u[:, 20:22, :])
                squares(l * 4 + 2 + 3 * which, x, SEQ, (x_up, x_up.at(l * 2 + which, 0)))
                join(act, "ffn", l * 2 + which, 1)

            def projections(l, which, n0, unit):
                for n in range((1, 2, 2)[which], KT // 2):
                    unit_hi(l, n0 + n, unit + n)
                if which != 1:
                    squares(l * 4 + 3 + which // 2, x, SEQ, (pj_done, (l * 3 + which) * KT + 4))
                join(act, "proj", l * 3 + which, 1)

            def lora(l):
                for m, dst in enumerate((lwT, laT, lgT)):
                    act.wait_ge(lo_ps.sem, lo_ps.at(l, m + 1))
                    if m == 0:
                        act.wait_ge(ga_a.sem, ga_a.at(l, 1))
                    A(dst[:, :], bank[m][:, :], ACT.Copy, scale=lora_c0[:, m:m + 1]).then_inc(lo_base.sem, 1)
                act.wait_ge(lo_done.sem, lo_done.at(l, 3))
                A(lwT[:, :], lwT[:, :], ACT.Tanh)
                A(lgT[:, :], lgT[:, :], ACT.Sigmoid)
                act.wait_ge(ga_b.sem, ga_b.at(l, 1))
                A(beta[:, :, :], bank[3][:, 0:TT * 24].rearrange("p (t c) -> p t c", t=TT)[:, :, 12:24], ACT.Sigmoid)
                A(ge[:, :, :], ge[:, :, :], ACT.Exp, scale=-1.0)
                A(nega[:, :], cl[:, C_ALOG:C_ALOG + 12], ACT.Exp)
                act.drain()
                A(gl[:, :, :], ge[:, :, :], ACT.Ln, bias=1.0).then_inc(ga_c.sem, 1)
                act.wait_ge(ga_f.sem, ga_f.at(l, 1))
                A(gsum[:, :, :], bank[4][:, 0:TT * 12].rearrange("p (t c) -> p t c", t=TT), ACT.Copy).then_inc(ga_g.sem, 1)
                act.wait_ge(ga_t.sem, ga_t.at(l, 1))
                A(gsumT[0:12, :], bank[5][0:12, :], ACT.Copy)
                join(act, "lora", l, 1)

            def hyena_filter(l):
                for n, dst in enumerate((filt_h1, filt_h2)):
                    act.wait_ge(fl_arg.sem, fl_arg.at(l, n + 1))
                    A(dst[0:HY_FFN, :], filt_arg[0:HY_FFN, :], ACT.Sin).then_inc(fl_h.sem, 1)
                w = ring[U_FILTER % 2]
                act.wait_ge(fl_out.sem, fl_out.at(l, 1))
                for t in range(TT):
                    A(filt_e[:, t, :], w[:, 640:1152], ACT.Exp, scale=kon[:, K_NEGT + t:K_NEGT + t + 1]).then_inc(fl_e.sem, 1)
                for t in range(TT):
                    act.wait_ge(fl_k.sem, fl_k.at(l, t + 1))
                    A(filt_e[:, t, :], filt[:, t, :], ACT.Abs).then_inc(fl_abs.sem, 1)
                act.wait_ge(fl_sum.sem, fl_sum.at(l, 1))
                A(filt_sum[:, :], bank[6][:, :], ACT.Copy).then_inc(fl_s.sem, 1)
                join(act, "filter", l, 1)

            def hyena(l):
                for c in range(HY_C):
                    for m, dst in enumerate((hx0[c], hx1, hv)):
                        act.wait_ge(hy_ps.sem, hy_ps.at(l, 3 * c + m + 1))
                        if c and m:
                            act.wait_ge(hy_cv.sem, hy_cv.at(l, c))
                        col = C_HY + 13 * c
                        A(dst[:, :], bank[4 * c + m][:, :], ACT.Identity, bias=cl[:, col + 9 + m:col + 10 + m],
                          scale=cl[:, col + 3 * m + 1:col + 3 * m + 2]).then_inc(hy_base.sem, 1)
                for c in range(HY_C):
                    act.wait_ge(hy_tp.sem, hy_tp.at(l, c + 1))
                    A(utok[:, :, c * P:(c + 1) * P], bank[4 * c + 3][:, :].rearrange("p (t c) -> p t c", t=TT), ACT.Copy)
                join(act, "hyena", l, 1)
                for n in range(8):
                    act.wait_ge(sp_ps.sem, sp_ps.at(l, n + 1))
                    A(spec[:, n, :], bank[n][:, :], ACT.Copy).then_inc(sp_sb.sem, 1)
                join(act, "dft", l, 1)

            def invert(turn):
                s = iv
                for m in range(LEVELS - 1):
                    for g in range(4):
                        act.wait_ge(s["xps"].sem, s["xps"].at(turn, 4 * m + g + 1))
                        A(X[g].rearrange("p a b -> p (a b)"), bank[g][:, :], ACT.Copy).then_inc(s["x"].sem, 1)

            def scan_u(turn):
                s = scan_sig
                for c in range(TT):
                    for d in range(2):
                        act.wait_ge(s["ups"][d].sem, s["ups"][d].at(turn, c + 1))
                        A(Ut[d][:, :], bank[6 + d][:, 0:P], ACT.Copy).then_inc(s["u"][d].sem, 1)

            def rwkv(l, j):
                it = l * PAIRS + j

                def base(n, m, dst):
                    act.wait_ge(rw_ps.sem, rw_ps.at(it, n))
                    A(dst[:, :], bank[m][:, :], ACT.Copy, scale=rwc[:, m:m + 1]).then_inc(rw_base.sem, 1)

                act.wait_ge(rw_cols.sem, rw_cols.at(it, 1))
                for d in range(2):
                    act.wait_ge(rw_ps.sem, rw_ps.at(it, 3 + d))
                    A(aT[d][:, :], bank[4 + d][:, :], ACT.Sigmoid, bias=clj[:, 6 + d:7 + d])
                act.wait_ge(rw_ps.sem, rw_ps.at(it, 5))
                A(gateT[:, :], bank[3][:, :], ACT.Copy)
                for d in range(2):
                    act.wait_ge(rw_w0.sem, rw_w0.at(it, d + 1))
                    A(sg[d][:, :, :], sg[d][:, :, :], ACT.Sigmoid).then_inc(rw_sig.sem, 1)
                act.drain()
                for d in range(2):
                    A(kd[d][:, :], aT[d][:, :], ACT.Identity, bias=rwc[:, 3:4], scale=clj[:, 9:10])
                base(6, 1, kT)
                for d in range(2):
                    last_t, first_t = (P - 1, 0) if d == 0 else (0, P - 1)
                    act.wait_ge(rw_g.sem, rw_g.at(it, 2 * d + 2))
                    gi = bank[4 + 2 * d][:, :].rearrange("p (t c) -> p t c", t=TT)
                    gx_ = bank[5 + 2 * d][:, :].rearrange("p (t c) -> p t c", t=TT)
                    A(Pinc[d][:, :, :], gi, ACT.Exp, scale=-RW_DECAY_SCALE).then_inc(rw_exp.sem, 1)
                    A(Pinv[d][:, :, :], gi, ACT.Exp, scale=RW_DECAY_SCALE).then_inc(rw_exp.sem, 1)
                    A(Pexc[d][:, :, :], gx_, ACT.Exp, scale=-RW_DECAY_SCALE).then_inc(rw_exp.sem, 1)
                    A(lastP[:, d, :], gi[:, :, last_t], ACT.Exp, scale=-RW_DECAY_SCALE)
                    A(firstP[:, d, :], gx_[:, :, first_t], ACT.Exp, scale=RW_DECAY_SCALE).then_inc(rw_exp.sem, 1)
                base(7, 0, rT)
                act.wait_ge(rw_nrm.sem, rw_nrm.at(it, 1))
                A(tmpB[:, :], bank[3][:, :], ACT.Sqrt, bias=eps[:, 0:1]).then_inc(rw_std.sem, 1)
                base(8, 2, vT)
                for n, (dst, b) in enumerate(((Btok[0], 4), (Ktok[0], 5), (Vtok, 1), (Btok[1], 6), (Ktok[1], 7))):
                    act.wait_ge(rw_tp.sem, rw_tp.at(it, n + 1))
                    A(dst.rearrange("p a b -> p (a b)"), bank[b][:, :], ACT.Copy).then_inc(rw_tok.sem, 1)
                invert(turn_of(l, 0, j))
                scan_u(turn_of(l, 0, j))
                act.wait_ge(rw_fin[0].sem, rw_fin[0].at(it, 1))
                A(tmpB[:, :], bank[5][:, :], ACT.Copy).then_inc(rw_fin[5].sem, 1)
                act.wait_ge(rw_fin[4].sem, rw_fin[4].at(it, 1))
                A(tmpB[:, :], bank[1][:, :], ACT.Sqrt, bias=eps[:, 1:2], scale=1.0 / HD).then_inc(rw_gstd.sem, 1)
                join(act, "rwkv", it, 1)

            def gdn(l, j):
                it = l * PAIRS + j

                def base(m, dst):
                    act.wait_ge(gd_ps.sem, gd_ps.at(it, m + 1))
                    A(dst[:, :], bank[m][:, :], ACT.Copy, scale=clj[:, 3 * m + 1:3 * m + 2]).then_inc(gd_base.sem, 1)

                def silu(m, dst):
                    act.wait_ge(gd_sh.sem, gd_sh.at(it, m + 1))
                    A(dst[:, :], dst[:, :], ACT.Silu).then_inc(gd_silu.sem, 1)

                act.wait_ge(gd_sel.sem, gd_sel.at(it, 1))
                for g in range(4):
                    d, hh = g // 2, g % 2
                    r = slice(hh * HD, hh * HD + HD)
                    act.wait_ge(gd_row.sem, gd_row.at(it, g + 1))
                    A(EG[d][r, :, :].rearrange("p a b -> p (a b)"), bank[4 + g][r, :], ACT.Exp).then_inc(gd_eg.sem, 1)
                for g in range(4):
                    if g == 2:
                        base(0, gqT)
                    act.wait_ge(gd_dif.sem, gd_dif.at(it, g + 1))
                    A(KE[:, g, :], KEp[:, g, :], ACT.Exp)
                    A(GDT[g][:, :, :], GDT[g][:, :, :], ACT.Exp).then_inc(gd_exp.sem, 1)
                base(1, gkT)
                silu(0, gqT)
                silu(1, gkT)
                base(2, gvT)
                for n in range(2):
                    act.wait_ge(gd_nrm.sem, gd_nrm.at(it, n + 1))
                    A((gr2, gr1)[n][:, :], bank[4 + n][:, :], ACT.Sqrt, bias=eps[:, 0:1]).then_inc(gd_std.sem, 1)
                silu(2, gvT)
                act.wait_ge(gd_ps.sem, gd_ps.at(it, 4))
                A(zg[:, :], bank[3][:, :], ACT.Silu)
                for n, dst in enumerate((GKtok, GV)):
                    act.wait_ge(gd_tp.sem, gd_tp.at(it, n + 1))
                    A(dst.rearrange("p a b -> p (a b)"), bank[7 - n][:, :], ACT.Copy).then_inc(gd_tok.sem, 1)
                for hh, dst in enumerate((gvT, go)):
                    act.wait_ge(gd_kk.sem, gd_kk.at(it, hh + 3))
                    A(dst[:, :], bank[4 + hh][:, :], ACT.Copy).then_inc(gd_kq.sem, 1)
                invert(turn_of(l, 1, j))
                act.wait_ge(gd_fin[0].sem, gd_fin[0].at(it, 1))
                A(gs2[:, :], bank[5][:, :], ACT.Copy).then_inc(gd_fin[5].sem, 1)
                act.wait_ge(gd_fin[2].sem, gd_fin[2].at(it, 1))
                A(gr1[:, :], bank[3][:, :], ACT.Sqrt, bias=eps[:, 0:1], scale=1.0 / HD).then_inc(gd_fin[3].sem, 1)
                join(act, "gdn", it, 1)

            def attention(l):
                projections(l, 1, S_XQ, U_XQ)
                for m in range(KT):
                    act.wait_ge(xk_ps.sem, xk_ps.at(l, m + 1))
                    A(kmT[:, m, :], bank[m % 4][:, 0:N_MEM], ACT.Copy).then_inc(xk_done.sem, 1)
                act.wait_ge(xv_ps.sem, xv_ps.at(l, 1))
                for n in range(4):
                    A(vm[:, :, n * 256:(n + 1) * 256], bank[4 + n][:, :].rearrange("p (m c) -> p m c", m=2), ACT.Copy)
                join(act, "attn", l * 2, 1)

                def exponentials(a):
                    act.wait_ge(at_mx.sem, at_mx.at(l, a + 1))
                    for t in range(TT):
                        A(prob[a % 2][:, t, :], bank[6 * (a % 2) + t // 2][:, (t % 2) * 256:(t % 2 + 1) * 256], ACT.Exp,
                          bias=nmx[a % 2][:, t:t + 1], scale=XA_DIM ** -0.5, accum_out=psm[a % 2][:, t:t + 1]).then_inc(at_e.sem, 1)

                exponentials(0)
                for a in range(XA_HEADS):
                    if a + 1 < XA_HEADS:
                        exponentials(a + 1)
                    for m in range(2):
                        act.wait_ge(at_tp.sem, at_tp.at(l, 2 * a + m + 1))
                        A(probT[:, m, :], bank[2 + m][:, :], ACT.Copy).then_inc(at_pt.sem, 1)
                    for b in range(2):
                        act.wait_ge(at_o.sem, at_o.at(l, 2 * a + b + 1))
                        A(oT[:, 2 * a + b, :], bank[4 + b][:, :], ACT.Copy).then_inc(at_od.sem, 1)
                    if a in (1, 2):
                        unit_hi(l, S_XO + a - 1, U_XO + a - 1)
                join(act, "attn", l * 2 + 1, 1)
                source_hi(l, A_XO, oT)
                projections(l, 2, S_XO, U_XO)

            act.wait_ge(consts_in.sem, 48)
            act.wait_ge(x_in.sem, 32)
            join(act, "start", 0, 1)
            mem_in = sc[:, 8192:8192 + KT * N_MEM].rearrange("p (a b) -> p a b", a=KT)
            squares(0, mem_in, N_MEM)
            norm(0, 0, N_MEM, 0)
            squares(1, x, SEQ)
            with act.Fori(0, layers, 1) as l:
                join(act, "layer", l, 1)
                norm(l * 4 + 1, 0, SEQ, None, l, A_FFN1, S_FFN1, U_FFN_UP)
                ffn(l, 0, S_FFN1, U_FFN_UP, A_FFN1)
                norm(l * 4 + 2, 0, SEQ, l + 1)
                lora(l)
                hyena_filter(l)
                hyena(l)
                with act.Fori(0, PAIRS, 1) as j:
                    rwkv(l, j)
                with act.Fori(0, PAIRS, 1) as j:
                    gdn(l, j)
                unit_hi(l, S_WOUT, U_WOUT)
                source_hi(l, A_WOUT, y)
                projections(l, 0, S_WOUT, U_WOUT)
                norm(l * 4 + 3, 4, SEQ, None, l, A_XQ, S_XQ, U_XQ)
                attention(l)
                norm(l * 4 + 4, 4, SEQ, None, l, A_FFN2, S_FFN2, U_FFN2)
                ffn(l, 1, S_FFN2, U_FFN2, A_FFN2)
            norm(4 * layers + 1, 0, SEQ, layers + 1)

        @block.vector
        def _(dve):
            tt_, ts_, stt = dve.tensor_tensor, dve.tensor_scalar, dve.scalar_tensor_tensor

            def norm(it, src, dst, gain, n_tok, joined=None, l=None, source=None, n=None, unit=None):
                dve.wait_ge(n_std.sem, n_std.at(it, 1))
                dve.reciprocal(rstd[:, 0:n_tok], std[:, 0:n_tok])
                dve.drain()
                if source is None:
                    for t in range(KT):
                        stt(dst[:, t, :], src[:, t, :], gain(t), rstd[:, 0:n_tok], ALU.mult, ALU.mult)
                    join(dve, "norm", joined, 1)
                else:
                    unit_lo(l, n, unit)
                    for t in range(KT):
                        stt(sq[:, t, :], src[:, t, :], gain(t), rstd[:, 0:n_tok], ALU.mult, ALU.mult).then_inc(as_f.sem, 1)
                        if t:
                            low(l, source, sq, t - 1)
                    low(l, source, sq, KT - 1)

            def low(l, source, src, t):
                dve.wait_ge(as_hi.sem, as_hi.at(l * SPLIT_SOURCES + source, t + 1))
                tt_(a_lo[:, t, :], src[:, t, :], a_hi[:, t, :].bitcast(F32), ALU.subtract).then_inc(as_lo.sem, 1)

            def unit_lo(l, n, unit, later=0, inner=None):
                dve.wait_ge(ws_hi.sem, ws_hi.at(l, n + 1) + later * 2)
                if inner is not None:
                    tt_(u_lo[n % 2], inner, u_hi[n % 2].bitcast(F32), ALU.subtract)
                tt_(w_lo[n % 2], ring[unit % 2][:, :], w_hi[n % 2].bitcast(F32), ALU.subtract)
                dve.drain().then_inc(free.sem, 1)
                dve.sem_inc(ws_lo.sem, 1)

            def layer_gain(n):
                return lambda t: cl[:, C_NORM + n * KT + t:C_NORM + n * KT + t + 1]

            def ffn(l, which, n0, unit):
                unit_lo(l, n0 + 1, unit + 1)

                def gated(it, s, dst):
                    dve.wait_ge(f_sil.sem, f_sil.at(it, s + 1))
                    tt_(dst, sil[s], bank[2 * s + 1][:, :], ALU.mult).then_inc(f_u.sem, 1)

                with dve.Fori(0, FB // 2 - 1, 1) as j:
                    for s in range(2):
                        gated((l * 2 + which) * (FB // 2) + j, s, u[:, bass.ds(j * 2 + s, 1), :].rearrange("p a n -> p (a n)"))
                        unit_lo(l, n0 + s + 2, unit + s + 2, j)
                for s in range(2):
                    gated((l * 2 + which) * (FB // 2) + (FB // 2 - 1), s, u[:, FB - 2 + s, :])
                    unit_lo(l, n0 + FB + s, unit + FB + s, inner=u[:, 2 * s:2 * s + 2, :])
                n0, unit = n0 + FB, unit + FB
                with dve.Fori(0, 4, 1) as j:
                    for s in range(2):
                        unit_lo(l, n0 + 2 + s, unit + 2 + s, j, u[:, bass.ds(j * 4 + (2 * s + 4), 2), :])
                unit_lo(l, n0 + 10, unit + 10, inner=u[:, 20:22, :])
                for m in range(KT):
                    dve.wait_ge(f_dn.sem, f_dn.at(l * 2 + which, m + 1))
                    stt(x[:, m, :], bank[m][:, :], 0.5, x[:, m, :], ALU.mult, ALU.add).then_inc(x_up.sem, 1)
                join(dve, "ffn", l * 2 + which, 1)

            def taps(dst, ps, prev, nxt):
                stt(dst[:, 1:SEQ], ps[:, 0:SEQ - 1], prev, dst[:, 1:SEQ], ALU.mult, ALU.add)
                dve.drain()
                return stt(dst[:, 0:SEQ - 1], ps[:, 1:SEQ], nxt, dst[:, 0:SEQ - 1], ALU.mult, ALU.add)

            def lora(l):
                ts_(lora_c0[:, :], cl[:, C_LMU:C_LMU + 3], -1.0, 1.0, ALU.mult, ALU.add)
                dve.drain()
                tt_(lora_c0[:, :], lora_c0[:, :], cl[:, C_LMU + 3:C_LMU + 6], ALU.subtract).then_inc(ga_a.sem, 1)
                for m, dst in enumerate((lwT, laT, lgT)):
                    dve.wait_ge(lo_base.sem, lo_base.at(l, m + 1))
                    taps(dst, bank[m], cl[:, C_LMU + m:C_LMU + m + 1], cl[:, C_LMU + 3 + m:C_LMU + 4 + m]).then_inc(lo_done.sem, 1)
                dve.wait_ge(lo_ps.sem, lo_ps.at(l, 4))
                tt_(gx[:, :, :], bank[3][:, 0:TT * 24].rearrange("p (t c) -> p t c", t=TT)[:, :, 0:12],
                    over(cl[:, C_DT:C_DT + 12], TT), ALU.add)
                dve.drain()
                stt(ge[:, :, :], gx[:, :, :], -1.0, gx[:, :, :], ALU.mult, ALU.max).then_inc(ga_b.sem, 1)
                dve.wait_ge(ga_c.sem, ga_c.at(l, 1))
                stt(gtok[:, :, :], gx[:, :, :], 0.0, gl[:, :, :], ALU.max, ALU.add)
                dve.drain()
                stt(gtok[:, :, :], gtok[:, :, :], -1.0, over(nega[:, :], TT), ALU.mult, ALU.mult).then_inc(ga_e.sem, 1)
                join(dve, "lora", l, 1)

            def hyena_filter(l):
                for n in range(2):
                    dve.wait_ge(fl_ps.sem, fl_ps.at(l, n + 1))
                    q = slice(0, HY_FFN)
                    ts_(filt_arg[q, :], bank[n][q, :], cl[q, C_FILT + 1 + n:C_FILT + 2 + n], cl[q, C_FILT:C_FILT + 1], ALU.add, ALU.mult)
                    dve.drain()
                    ts_(filt_k[q, :], filt_arg[q, :], 0.15915494309189535, ROUND_MAGIC, ALU.mult, ALU.add)
                    dve.drain()
                    ts_(filt_k[q, :], filt_k[q, :], ROUND_MAGIC, None, ALU.subtract)
                    dve.drain()
                    stt(filt_arg[q, :], filt_k[q, :], -TWO_PI_HI, filt_arg[q, :], ALU.mult, ALU.add)
                    dve.drain()
                    stt(filt_arg[q, :], filt_k[q, :], -TWO_PI_LO, filt_arg[q, :], ALU.mult, ALU.add)
                    dve.drain()
                    ts_(filt_arg[q, :], filt_arg[q, :], PI_BELOW, -PI_BELOW, ALU.min, ALU.max).then_inc(fl_arg.sem, 1)
                for t in range(TT):
                    dve.wait_ge(fl_e.sem, fl_e.at(l, t + 1))
                    dve.wait_ge(fl_out.sem, fl_out.at(l, t + 1))
                    last = tt_(filt[:, t, :], bank[2 + t][:, :], filt_e[:, t, :], ALU.mult)
                    if t == 0:
                        dve.drain()
                        last = dve.memset(filt[0:1, 0, 256:512], 0.0)
                    last.then_inc(fl_k.sem, 1)
                dve.wait_ge(fl_s.sem, fl_s.at(l, 1))
                tt_(filt_rn[:, :], filt_sum[:, 0:256], filt_sum[:, 256:512], ALU.add)
                tt_(kplus[:, :, :], filt[:, :, 0:256], filt[:, :, 256:512], ALU.add)
                tt_(kminus[:, :, :], filt[:, :, 0:256], filt[:, :, 256:512], ALU.subtract)
                dve.drain()
                dve.reciprocal(filt_rn[:, :], filt_rn[:, :])
                dve.drain()
                for k_ in (kplus, kminus):
                    stt(k_[:, :, :], k_[:, :, :], 1.0 / SEQ, over(filt_rn[:, :], TT), ALU.mult, ALU.mult)
                join(dve, "filter", l, 1)

            def hyena(l):
                for c in range(HY_C):
                    col = C_HY + 13 * c
                    for m, dst in enumerate((hx0[c], hx1, hv)):
                        dve.wait_ge(hy_base.sem, hy_base.at(l, 3 * c + m + 1))
                        taps(dst, bank[4 * c + m], cl[:, col + 3 * m:col + 3 * m + 1], cl[:, col + 3 * m + 2:col + 3 * m + 3])
                    dve.drain()
                    tt_(hu[c][:, :], hx1[:, :], hv[:, :], ALU.mult).then_inc(hy_cv.sem, 1)
                join(dve, "hyena", l, 1)
                dve.wait_ge(sp_sb.sem, sp_sb.at(l, 8))
                u_re, u_im = spec[:, 0:4, 0:256], spec[:, 4:8, 0:256]
                k_re, k_im = spec[:, 0:4, 256:512], spec[:, 4:8, 256:512]
                tt_(prA[:, :, :], u_re, k_re, ALU.mult)
                tt_(prT[:, :, :], u_im, k_im, ALU.mult)
                dve.drain()
                tt_(prA[:, :, :], prA[:, :, :], prT[:, :, :], ALU.subtract).then_inc(sp_pr.sem, 1)
                tt_(prB[:, :, :], u_re, k_im, ALU.mult)
                dve.drain()
                tt_(prT[:, :, :], u_im, k_re, ALU.mult)
                dve.drain()
                tt_(prB[:, :, :], prB[:, :, :], prT[:, :, :], ALU.add).then_inc(sp_pr.sem, 1)
                dve.drain()
                for c in range(HY_C):
                    dve.wait_ge(sp_y.sem, sp_y.at(l, c + 1))
                    stt(hyo[c], hu[c][:, :], cl[:, C_HY + 13 * c + 12:C_HY + 13 * c + 13], bank[c][:, :], ALU.mult, ALU.add)
                    dve.drain()
                    tt_(y[:, c, :], hyo[c], hx0[c][:, :], ALU.mult)
                join(dve, "dft", l, 1)

            def invert(turn):
                s = iv
                for g in range(4):
                    dve.wait_ge(s["half"].sem, s["half"].at(turn, g + 1))
                    tt_(XT[g][:, :, :], Y[g][:, :, :], over(ident, TT), ALU.add).then_inc(s["xt"].sem, 1)
                for m in range(LEVELS - 1):
                    for g in range(4):
                        dve.wait_ge(s["yps"].sem, s["yps"].at(turn, 4 * m + g + 1))
                        tt_(Y[g][:, :, :], bank[g][:, :].rearrange("p (a b) -> p a b", a=TT), over(level_mask(m + 1, g // 2), TT),
                            ALU.mult).then_inc(s["y"].sem, 1)
                    for g in range(4):
                        dve.wait_ge(s["xtps"].sem, s["xtps"].at(turn, 4 * m + g + 1))
                        tt_(XT[g][:, :, :], bank[4 + g][:, :].rearrange("p (a b) -> p a b", a=TT), XT[g][:, :, :],
                            ALU.add).then_inc(s["xt"].sem, 1)

            def rwkv(l, j):
                it = l * PAIRS + j
                dve.wait_ge(rw_cols.sem, rw_cols.at(it, 1))
                small = ring[1 - U_RWKV % 2][:, KT * P:2 * KT * P]
                for d in range(2):
                    dve.wait_ge(rw_ps.sem, rw_ps.at(it, 1 + d))
                    tt_(sg[d][:, :, :], bank[6 + d][:, :].rearrange("p (a b) -> p a b", a=TT),
                        over(small[:, 384 + d * P:384 + (d + 1) * P], TT), ALU.add).then_inc(rw_w0.sem, 1)
                dve.wait_ge(rw_base.sem, rw_base.at(it, 1))
                taps(kT, bank[1], clj[:, 1:2], clj[:, 4:5])
                dve.drain()
                ts_(kkr[:, :], kT[:, :], clj[:, 8:9], None, ALU.mult)
                dve.drain()
                tt_(tmpA[:, :], kkr[:, :], kkr[:, :], ALU.mult).then_inc(rw_kk2.sem, 1)
                dve.wait_ge(rw_base.sem, rw_base.at(it, 2))
                taps(rT, bank[0], clj[:, 0:1], clj[:, 3:4])
                dve.drain()
                stt(rk[:, :], rT[:, :], clj[:, 10:11], kT[:, :], ALU.mult, ALU.mult).then_inc(rw_rk.sem, 1)
                dve.wait_ge(rw_std.sem, rw_std.at(it, 1))
                dve.reciprocal(tmpB[:, :], tmpB[:, :])
                dve.drain()
                tt_(kk[:, :], kkr[:, :], tmpB[:, :], ALU.mult)
                dve.drain()
                ts_(nkk[:, :], kk[:, :], -1.0, None, ALU.mult)
                dve.drain()
                for d in range(2):
                    if d:
                        dve.wait_ge(rw_base.sem, rw_base.at(it, 3))
                        taps(vT, bank[2], clj[:, 2:3], clj[:, 5:6]).then_inc(rw_vt.sem, 1)
                        dve.drain()
                        dve.wait_ge(rw_bon.sem, rw_bon.at(it, 1))
                        tt_(bv[:, :], bank[0][:, :], vT[:, :], ALU.mult)
                    dve.wait_ge(rw_exp.sem, rw_exp.at(it, 4 * d + 4))
                    tt_(AR[d][:, :, 0, :], nkk[:, :].rearrange("p (a b) -> p a b", a=TT), Pexc[d][:, :, :], ALU.mult)
                    tt_(AR[d][:, :, 1, :], rT[:, :].rearrange("p (a b) -> p a b", a=TT), Pinc[d][:, :, :], ALU.mult)
                    dve.wait_ge(rw_kd.sem, rw_kd.at(it, d + 1))
                    tt_(BTt[d][:, :], aP[d][:, :], kk[:, :], ALU.mult)
                    tt_(KTt[d][:, :], kd[d][:, :], Pinv[d].rearrange("p a b -> p (a b)"), ALU.mult).then_inc(rw_op.sem, 1)
                tt_(fac[:, 0, 0:3], lastP[:, 0, 0:3], firstP[:, 0, 1:4], ALU.mult)
                tt_(fac[:, 1, 0:3], lastP[:, 1, 1:4], firstP[:, 1, 0:3], ALU.mult)
                for d in range(2):
                    dve.memset(Z[d][:, :], 0.0)
                for d, n, hh in np.ndindex(2, 4, 2):
                    g = 2 * d + hh
                    dve.wait_ge(rw_scp.sem, rw_scp.at(it, 8 * d + 2 * n + hh + 1))
                    dst = (SCB, SCK)[n // 2][g][:, 2 * (n % 2):2 * (n % 2) + 2, :, :].rearrange("p t a b -> p t (a b)")
                    tt_(dst, bank[4 * hh + n][:, :].rearrange("p (t c) -> p t c", t=2), over(strict_incl[d], 2),
                        ALU.mult).then_inc(rw_scs.sem, 1)
                invert(turn_of(l, 0, j))
                s = scan_sig
                dve.drain().then_inc(s["z0"].sem, 1)
                for c in range(TT):
                    for d in range(2):
                        dve.wait_ge(s["tps"][d].sem, s["tps"][d].at(turn_of(l, 0, j), c + 1))
                        dve.tensor_copy(Tt[d][:, :].rearrange("p (a b) -> p a b", a=2), psum[:, 2 * d:2 * d + 2, 0:HD]).then_inc(s["t"][d].sem, 1)
                    for d in range(2):
                        if c < TT - 1:
                            f = fac[:, d, c:c + 1] if d == 0 else fac[:, d, TT - 2 - c:TT - 1 - c]
                            dve.wait_ge(s["zps"][d].sem, s["zps"][d].at(turn_of(l, 0, j), c + 1))
                            tt_(Z[d][:, :], Z[d][:, :], bank[6 + d][:, P:P + HD], ALU.add)
                            dve.drain()
                            ts_(Z[d][:, :], Z[d][:, :], f, None, ALU.mult).then_inc(s["z"][d].sem, 1)
                dve.wait_ge(rw_fin[5].sem, rw_fin[5].at(it, 1))
                tt_(yo[:, :], bank[4][:, :], tmpB[:, :], ALU.add).then_inc(rw_fin[1].sem, 1)
                dve.wait_ge(rw_fin[2].sem, rw_fin[2].at(it, 1))
                stt(yo[:, :], bank[0][:, :], -1.0 / HD, yo[:, :], ALU.mult, ALU.add)
                dve.drain()
                tt_(tmpA[:, :], yo[:, :], yo[:, :], ALU.mult).then_inc(rw_fin[3].sem, 1)
                dve.wait_ge(rw_gstd.sem, rw_gstd.at(it, 1) + 1)
                dve.reciprocal(tmpB[:, :], tmpB[:, :])
                dve.drain()
                stt(yo[:, :], yo[:, :], clj[:, 11:12], tmpB[:, :], ALU.mult, ALU.mult)
                dve.drain()
                stt(yo[:, :], yo[:, :], clj[:, 12:13], bv[:, :], ALU.add, ALU.add)
                dve.drain()
                tt_(y[:, bass.ds(j + HY_C, 1), :].rearrange("p a n -> p (a n)"), yo[:, :], gateT[:, :], ALU.mult)
                join(dve, "rwkv", it, 1)

            def gdn(l, j):
                it = l * PAIRS + j
                dve.wait_ge(gd_sel.sem, gd_sel.at(it, 1))
                for g in range(4):
                    last_t = P - 1 if g < 2 else 0
                    dve.wait_ge(gd_eg.sem, gd_eg.at(it, g + 1))
                    row = bank[4 + g][:, :].rearrange("p (t c) -> p t c", t=TT)
                    for t in range(TT):
                        ts_(GDT[g][:, t, :], row[:, t, :], gcj[:, t, g:g + 1], 0.0, ALU.subtract, ALU.min)
                    tt_(KEp[:, g, :], row[:, :, last_t], gcj[:, :, g], ALU.subtract).then_inc(gd_dif.sem, 1)
                for m, dst in enumerate((gqT, gkT, gvT)):
                    dve.wait_ge(gd_base.sem, gd_base.at(it, m + 1))
                    taps(dst, bank[m], clj[:, 3 * m:3 * m + 1], clj[:, 3 * m + 2:3 * m + 3]).then_inc(gd_sh.sem, 1)
                for d in range(2):
                    dve.memset(GZ[d][:, :], 0.0)
                for n, (dst, r_, f) in enumerate(((gkT, gr2, 1.0), (gqT, gr1, HD ** -0.5))):
                    dve.wait_ge(gd_std.sem, gd_std.at(it, n + 1))
                    dve.reciprocal(r_[:, :], r_[:, :])
                    dve.drain()
                    stt(dst[:, :], dst[:, :], f, r_[:, :], ALU.mult, ALU.mult).then_inc(gd_qk.sem, 1)
                for g in range(4):
                    dve.wait_ge(gd_kk.sem, gd_kk.at(it, g % 2 + 1))
                    dve.wait_ge(gd_msk.sem, gd_msk.at(it, g + 1))
                    tt_(GL[g][:, :, :], bank[g % 2][:, :].rearrange("p (t c) -> p t c", t=TT), GL[g][:, :, :],
                        ALU.mult).then_inc(gd_L.sem, 1)
                invert(turn_of(l, 1, j))
                s = scan_sig
                dve.drain().then_inc(s["z0"].sem, 1)
                for c in range(TT):
                    for d in range(2):
                        t = c if d == 0 else TT - 1 - c
                        dve.wait_ge(s["tps"][d].sem, s["tps"][d].at(turn_of(l, 1, j), c + 1))
                        tt_(GT[d][:, :].rearrange("p (a b) -> p a b", a=2), GV[:, t, :].rearrange("p (a b) -> p a b", a=2),
                            psum[:, 2 * d:2 * d + 2, 0:HD], ALU.subtract).then_inc(s["t"][d].sem, 1)
                    for d in range(2):
                        t = c if d == 0 else TT - 1 - c
                        dve.wait_ge(s["ups"][d].sem, s["ups"][d].at(turn_of(l, 1, j), c + 1))
                        tt_(GU[d][:, :].rearrange("p (a b) -> p a b", a=2), bank[6 + d][:, 0:P].rearrange("p (a b) -> p a b", a=2),
                            btj[:, t, 2 * d:2 * d + 2].unsqueeze(2).broadcast_to([P, 2, HD]), ALU.mult).then_inc(s["u"][d].sem, 1)
                    for d in range(2):
                        if c < TT - 1:
                            t = c if d == 0 else TT - 1 - c
                            last_t = P - 1 if d == 0 else 0
                            dve.wait_ge(s["zps"][d].sem, s["zps"][d].at(turn_of(l, 1, j), c + 1))
                            stt(GZ[d][:, :], GZ[d][:, :], EG[d][:, t, last_t:last_t + 1], bank[6 + d][:, P:P + HD],
                                ALU.mult, ALU.add).then_inc(s["z"][d].sem, 1)
                dve.wait_ge(gd_fin[5].sem, gd_fin[5].at(it, 1))
                tt_(go[:, :], bank[4][:, :], gs2[:, :], ALU.add)
                dve.drain()
                tt_(gs1[:, :], go[:, :], go[:, :], ALU.mult).then_inc(gd_fin[1].sem, 1)
                dve.wait_ge(gd_fin[3].sem, gd_fin[3].at(it, 1))
                dve.reciprocal(gr1[:, :], gr1[:, :])
                dve.drain()
                stt(go[:, :], go[:, :], cl[:, C_GNW:C_GNW + 1], gr1[:, :], ALU.mult, ALU.mult)
                dve.drain()
                tt_(y[:, bass.ds(j + HY_C + PAIRS, 1), :].rearrange("p a n -> p (a n)"), go[:, :], zg[:, :], ALU.mult)
                join(dve, "gdn", it, 1)

            def projections(l, which, n0, unit):
                def blocks(n):
                    for m in range(2 * n, 2 * n + 2):
                        if m % 2 == 0:
                            dve.wait_ge(ws_done.sem, ws_done.at(l, n0 + n + 3))
                        if which == 1:
                            ts_(qT[:, m, :], bank[m % 4][:, :], 1.0, None, ALU.mult).then_inc(pj_done.sem, 1)
                        else:
                            tt_(x[:, m, :], bank[m % 4][:, :], x[:, m, :], ALU.add).then_inc(pj_done.sem, 1)

                for n in range(KT // 2):
                    if n >= 2:
                        blocks(n - 2)
                    if n >= (1, 1, 2)[which]:
                        unit_lo(l, n0 + n, unit + n)
                blocks(KT // 2 - 2)
                blocks(KT // 2 - 1)
                join(dve, "proj", l * 3 + which, 1)

            def attention(l):
                projections(l, 1, S_XQ, U_XQ)
                join(dve, "attn", l * 2, 1)

                def maxima(a):
                    dve.wait_ge(at_s.sem, at_s.at(l, TT * (a + 1)))
                    for b in range(2):
                        dve.tensor_reduce(nmx[a % 2][:, 2 * b:2 * b + 2],
                                          bank[6 * (a % 2) + b][:, :].rearrange("p (t c) -> p t c", t=2),
                                          mybir.AxisListType.X, ALU.max)
                    dve.drain()
                    ts_(nmx[a % 2][:, :], nmx[a % 2][:, :], -(XA_DIM ** -0.5), None, ALU.mult).then_inc(at_mx.sem, 1)

                maxima(0)
                for a in range(XA_HEADS):
                    if a + 1 < XA_HEADS:
                        maxima(a + 1)
                    dve.wait_ge(at_e.sem, at_e.at(l, TT * (a + 1)))
                    dve.reciprocal(rsm[a % 2][:, :], psm[a % 2][:, :])
                    dve.drain()
                    for t in range(TT):
                        last = ts_(prob[a % 2][:, t, :], prob[a % 2][:, t, :], rsm[a % 2][:, t:t + 1], None, ALU.mult)
                    last.then_inc(at_n.sem, 1)
                    if a in (1, 2):
                        unit_lo(l, S_XO + a - 1, U_XO + a - 1)
                join(dve, "attn", l * 2 + 1, 1)
                for t in range(KT):
                    low(l, A_XO, oT, t)
                projections(l, 2, S_XO, U_XO)

            dve.sem_inc(f_u.sem, 2)
            dve.sem_inc(pj_done.sem, 4)
            dve.wait_ge(consts_in.sem, 48)
            join(dve, "start", 0, 1)
            mem_in = sc[:, 8192:8192 + KT * N_MEM].rearrange("p (a b) -> p a b", a=KT)
            norm(0, mem_in, memn, lambda t: gc[:, C_MEM + t:C_MEM + t + 1], N_MEM, 0)
            with dve.Fori(0, layers, 1) as l:
                join(dve, "layer", l, 1)
                norm(l * 4 + 1, x, h, layer_gain(0), SEQ, None, l, A_FFN1, S_FFN1, U_FFN_UP)
                ffn(l, 0, S_FFN1, U_FFN_UP)
                norm(l * 4 + 2, x, h, layer_gain(1), SEQ, l + 1)
                lora(l)
                hyena_filter(l)
                hyena(l)
                with dve.Fori(0, PAIRS, 1) as j:
                    rwkv(l, j)
                with dve.Fori(0, PAIRS, 1) as j:
                    gdn(l, j)
                unit_lo(l, S_WOUT, U_WOUT)
                for t in range(KT):
                    low(l, A_WOUT, y, t)
                projections(l, 0, S_WOUT, U_WOUT)
                norm(l * 4 + 3, x, h, layer_gain(2), SEQ, None, l, A_XQ, S_XQ, U_XQ)
                attention(l)
                norm(l * 4 + 4, x, h, layer_gain(3), SEQ, None, l, A_FFN2, S_FFN2, U_FFN2)
                ffn(l, 1, S_FFN2, U_FFN2)
                if UNITS > U_PAD:
                    dve.wait_ge(full[U_PAD % 2].sem, landed(l, U_PAD))
                    dve.sem_inc(free.sem, 1)
            norm(4 * layers + 1, x, h, lambda t: gc[:, C_FINAL + t:C_FINAL + t + 1], SEQ, layers + 1)

        @block.gpsimd
        def _(pool):
            tt_, ts_ = pool.tensor_tensor, pool.tensor_scalar

            def rwkv(l, j):
                it = l * PAIRS + j
                pool.tensor_copy(clj[:, 0:RWC], cl[:, bass.ds(j * RWC + C_RW, RWC)])
                pool.drain()
                tt_(rwc[:, 0:3], clj[:, 0:3], clj[:, 3:6], ALU.add)
                ts_(rwc[:, 3:4], clj[:, 9:10], -1.0, 1.0, ALU.mult, ALU.add)
                pool.drain()
                ts_(rwc[:, 0:3], rwc[:, 0:3], -1.0, 1.0, ALU.mult, ALU.add).then_inc(rw_cols.sem, 1)
                pool.wait_ge(rw_kk2.sem, rw_kk2.at(it, 1))
                for d in range(2):
                    pool.wait_ge(rw_exp.sem, rw_exp.at(it, 4 * d + 2))
                    tt_(kd[d][:, :], kd[d][:, :], kT[:, :], ALU.mult)
                    tt_(aP[d][:, :], aT[d][:, :], Pinv[d].rearrange("p a b -> p (a b)"), ALU.mult).then_inc(rw_kd.sem, 1)
                for g in range(4):
                    pool.wait_ge(rw_scs.sem, rw_scs.at(it, 8 * (g // 2) + 3 + g % 2))
                    tt_(Y[g][:, :, :], SCB[g][:, :, 0, :], over(level_mask(0, 1 - g // 2), TT), ALU.mult).then_inc(iv["half"].sem, 1)
                join(pool, "rwkv", it, 1)

            def gdn(l, j):
                it = l * PAIRS + j
                pool.tensor_copy(clj[:, 0:GDC], cl[:, bass.ds(j * GDC + C_GD, GDC)])
                pool.tensor_copy(selj[0:12, :, :].rearrange("p a b -> p (a b)"), kon[0:12, bass.ds(j * (4 * P) + K_SEL, 4 * P)])
                for dst, src in ((gcj, gsum), (btj, beta)):
                    for d in range(2):
                        pool.tensor_copy(dst[:, :, 2 * d:2 * d + 2], src[:, :, bass.ds(j * 2 + d * HEADS, 2)])
                pool.drain()
                ts_(nbj[:, :, :], btj[:, :, :], -1.0, 0.0, ALU.mult, ALU.add)
                pool.drain().then_inc(gd_sel.sem, 1)
                for g in range(4):
                    pool.wait_ge(gd_exp.sem, gd_exp.at(it, g + 1))
                    tt_(GDT[g][:, :, :], GDT[g][:, :, :], over(incl[g // 2], TT), ALU.mult)
                    pool.drain()
                    tt_(GL[g][:, :, :], GDT[g][:, :, :], nbj[:, :, g].unsqueeze(2).broadcast_to([P, TT, P]),
                        ALU.mult).then_inc(gd_msk.sem, 1)
                for n, (dst, src) in enumerate(((gs2, gkT), (gs1, gqT))):
                    pool.wait_ge(gd_silu.sem, gd_silu.at(it, 2))
                    tt_(dst[:, :], src[:, :], src[:, :], ALU.mult).then_inc(gd_sq.sem, 1)
                pool.wait_ge(gd_qk.sem, gd_qk.at(it, 2))
                for d in range(2):
                    pool.wait_ge(gd_eg.sem, gd_eg.at(it, 2 * d + 2))
                    tt_(GA[d].rearrange("p a b -> p (a b)"), gkT[:, :], EG[d].rearrange("p a b -> p (a b)"), ALU.mult)
                    tt_(GR[d].rearrange("p a b -> p (a b)"), gqT[:, :], EG[d].rearrange("p a b -> p (a b)"), ALU.mult)
                for g in range(4):
                    pool.wait_ge(gd_L.sem, gd_L.at(it, g + 1))
                    tt_(Y[g][:, :, :], GL[g][:, :, :], over(level_mask(0, 1 - g // 2), TT), ALU.mult).then_inc(iv["half"].sem, 1)
                pool.wait_ge(gd_tok.sem, gd_tok.at(it, 1))
                for d in range(2):
                    for hh in range(2):
                        tt_(Kend[d][:, :, hh, :], GKtok[:, :, hh * HD:hh * HD + HD],
                            KE[:, 2 * d + hh, :].unsqueeze(2).broadcast_to([P, TT, HD]), ALU.mult)
                for g in range(4):
                    pool.wait_ge(gd_kq.sem, gd_kq.at(it, g % 2 + 1))
                    tt_(GAT[g].rearrange("p a b -> p (a b)"), (gvT, go)[g % 2][:, :], GDT[g].rearrange("p a b -> p (a b)"), ALU.mult)
                pool.drain().then_inc(gd_scan.sem, 1)
                join(pool, "gdn", it, 1)

            pool.memset(eps[:, 0:1], NORM_EPS)
            pool.memset(eps[:, 1:2], RW_GN_EPS)
            pool.wait_ge(consts_in.sem, 48)
            join(pool, "start", 0, 1)
            join(pool, "norm", 0, 1, idle=True)
            with pool.Fori(0, layers, 1) as l:
                pool.tensor_copy(cl[:, :], cols_all[:, bass.ds(l, 1), :].rearrange("p a n -> p (a n)"))
                join(pool, "layer", l, 1)
                for which in range(2):
                    if which:
                        join(pool, "norm", l + 1, 1)
                        join(pool, "lora", l, 1, idle=True)
                        join(pool, "filter", l, 1, idle=True)
                        join(pool, "hyena", l, 1, idle=True)
                        join(pool, "dft", l, 1, idle=True)
                        with pool.Fori(0, PAIRS, 1) as j:
                            rwkv(l, j)
                        with pool.Fori(0, PAIRS, 1) as j:
                            gdn(l, j)
                        join(pool, "proj", l * 3, 1)
                        join(pool, "proj", l * 3 + 1, 1, idle=True)
                        join(pool, "attn", l * 2, 1, idle=True)
                        join(pool, "attn", l * 2 + 1, 1, idle=True)
                        join(pool, "proj", l * 3 + 2, 1, idle=True)
                    join(pool, "ffn", l * 2 + which, 1, idle=True)
            join(pool, "norm", layers + 1, 1, idle=True)


def tiles_of(w):
    n = w.shape[1] // P
    return w.reshape(KT, P, n, P).transpose(2, 1, 0, 3).reshape(n, P, KT * P)


def weight_units(a, l):
    out = np.zeros((UNITS, P, UNIT), np.float32)
    half = KT * P
    for which, base in ((1, U_FFN_UP), (2, U_FFN2)):
        out[base:base + FB, :, :half] = tiles_of(a[f"ffn{which}_w1"][l])
        out[base:base + FB, :, half:] = tiles_of(a[f"ffn{which}_w3"][l])
        w2 = a[f"ffn{which}_w2"][l].reshape(FB // 2, 2, P, D_MODEL)
        out[base + FB:base + N_FFN] = w2.transpose(0, 2, 1, 3).reshape(FB // 2, P, UNIT)
    w = a["w_in"][l]
    hy, rw, gd = 0, 768, 768 + 1536
    b = [tiles_of(w[:, s:s + n * P]) for s, n in ((hy, 6), (rw, 12), (gd, 12))]
    for m in range(2):
        out[U_LORA, :, m * half:(m + 1) * half] = b[1][9 + m]
    out[U_LORA + 1, :, :half] = b[1][11]
    out[U_LORA + 1, :, half:half + KT * 24] = w[:, -24:].reshape(KT, P, 24).transpose(1, 0, 2).reshape(P, KT * 24)
    f = out[U_FILTER]
    f[:HY_FFN, :512] = a["hy_w3"][l]
    f[:HY_EMB, 512:576] = a["hy_w1"][l]
    f[:HY_FFN, 576:640] = a["hy_w2"][l]
    f[:, 640:1152] = a["hy_decay"][l][None, :]
    f[:HY_EMB, 1152:1152 + SEQ] = positional_features().T
    for c in range(HY_C):
        for m in range(3):
            out[U_HYENA + 2 * c + m // 2, :, (m % 2) * half:(m % 2 + 1) * half] = b[0][2 * m + c]
    out[U_DFT:U_DFT + 4] = dft_units()
    for j in range(PAIRS):
        for m in range(3):
            out[U_RWKV + 2 * j + m // 2, :, (m % 2) * half:(m % 2 + 1) * half] = b[1][3 * m + j]
        s, q = out[U_RWKV + 2 * j + 1, :, half:], slice(j * P, (j + 1) * P)
        s[:, 0:128] = a["rw_w_lora"][l].reshape(P, -1)[:, q]
        s[:, 128:256] = a["rw_a_lora"][l].reshape(P, -1)[:, q]
        s[:, 256:384] = a["rw_g_lora"][l][:, q]
        s[:, 384:512] = a["rw_w0"][l, 0, q][None, :]
        s[:, 512:640] = a["rw_w0"][l, 1, q][None, :]
        for m in range(4):
            out[U_GDN + 2 * j + m // 2, :, (m % 2) * half:(m % 2 + 1) * half] = b[2][3 * m + j]
    for name, base in (("w_out", U_WOUT), ("xa_wq", U_XQ), ("xa_wk", U_XK), ("xa_wo", U_XO)):
        t = tiles_of(a[name][l]).reshape(KT // 2, 2, P, half)
        out[base:base + KT // 2] = t.transpose(0, 2, 1, 3).reshape(KT // 2, P, UNIT)
    out[U_XV:U_XV + 4] = a["xa_wv"][l].reshape(KT, P, 4, 256).transpose(2, 1, 0, 3).reshape(4, P, UNIT)
    return out


def column_params(a, l):
    c = np.zeros((P, N_COLS), np.float32)

    def put(at, v):
        v = np.asarray(v).reshape(-1, P)
        c[:, at:at + v.shape[0]] = v.T

    for n, name in enumerate(("norm_ffn1", "norm_mix", "norm_xattn", "norm_ffn2")):
        put(C_NORM + n * KT, a[name][l])
    for t in range(HY_C):
        for m in range(3):
            q = slice(m * 256 + t * P, m * 256 + (t + 1) * P)
            for tap in range(3):
                put(C_HY + 13 * t + 3 * m + tap, a["hy_conv_w"][l, tap, q])
            put(C_HY + 13 * t + 9 + m, a["hy_conv_b"][l, q])
        put(C_HY + 13 * t + 12, a["hy_bias"][l, t * P:(t + 1) * P])
    for n, name in enumerate(("hy_freq", "hy_b1", "hy_b2")):
        c[:HY_FFN, C_FILT + n] = a[name][l]
    for e, name in enumerate(("rw_mu_prev", "rw_mu_next")):
        put(C_LMU + 3 * e, a[name][l, 9 * P:])
        for j in range(PAIRS):
            for m in range(3):
                put(C_RW + RWC * j + 3 * e + m, a[name][l, (3 * m + j) * P:(3 * m + j + 1) * P])
    c[:, C_GNW] = np.concatenate([a["gdn_norm_w"][l]] * 2)
    c[:, C_DT:C_DT + 12] = a["gdn_dt_bias"][l].reshape(1, 12)
    c[:, C_ALOG:C_ALOG + 12] = a["gdn_a_log"][l].reshape(1, 12)
    for j in range(PAIRS):
        q = slice(j * P, (j + 1) * P)
        at = C_RW + RWC * j
        for d in range(2):
            put(at + 6 + d, a["rw_a0"][l, d, q])
        for n, name in enumerate(("rw_k_k", "rw_k_a", "rw_r_k", "rw_gn_w", "rw_gn_b")):
            put(at + 8 + n, a[name][l, q])
        for m in range(3):
            for tap in range(3):
                put(C_GD + GDC * j + 3 * m + tap, a["gdn_conv_w"][l, tap, m * 384 + j * P:m * 384 + (j + 1) * P])
    return c


def feature_tiles(v):
    return np.ascontiguousarray(v.T.reshape(KT, P, -1).transpose(1, 0, 2))


def host_arrays(a):
    units = np.concatenate([weight_units(a, l) for l in range(DEPTH)])
    cols = np.stack([column_params(a, l) for l in range(DEPTH)], axis=1)
    gcols = np.concatenate([a["mem_norm"].reshape(KT, P).T, a["norm_final"].reshape(KT, P).T], axis=1)
    return {"xT": feature_tiles(a["x"][0]), "memT": feature_tiles(a["mem"][0]), "units": units, "cols": cols,
            "gcols": np.ascontiguousarray(gcols), "consts": shape_constants()}


def kernel(**inputs):
    import concourse.bacc as _bacc
    from concourse.bass_utils import run_bass_kernel_spmd as _run

    arrays = host_arrays({k: np.asarray(v) for k, v in inputs.items()})
    nc = _bacc.Bacc("TRN2", target_bir_lowering=False, num_devices=1)
    args = [nc.dram_tensor(n, v.shape, F32, kind="ExternalInput").ap() for n, v in arrays.items()]
    out = nc.dram_tensor("out", (P, KT, SEQ), F32, kind="ExternalOutput").ap()
    trunk_program(nc, *args, out)
    r = _run(nc, [arrays], core_ids=[0])
    o = r.results[0]["out"]
    return o.transpose(1, 0, 2).reshape(1, D_MODEL, SEQ).transpose(0, 2, 1)
```
